# Optimizing a Trainium2 kernel written in Bass

```python
import jax, jax.numpy as jnp
from jax import lax
import numpy as np

D_MODEL = 1024
BATCH = 1
SEQ = 512
DEPTH = 1

N_META = 16
BLOCK = 128
N_PAD = BLOCK - N_META
EPS = 1e-6
N_BRANCH = 4
SB_DIM = 64
SB_HEADS = D_MODEL // 128
SB_W = SB_HEADS * SB_DIM
RET_QK = 64
RET_V = 128
RET_HEADS = D_MODEL // 256
RET_QK_W = RET_HEADS * RET_QK
RET_V_W = RET_HEADS * RET_V
RW_DIM = 64
RW_HEADS = D_MODEL // 128
RW_W = RW_HEADS * RW_DIM
RW_W_LORA = 64
RW_A_LORA = 64
RW_V_LORA = 32
RW_G_LORA = 128
RW_IN = 3 * RW_W + RW_W_LORA + RW_A_LORA + RW_G_LORA
RW_LN_EPS = 64e-5
SW_DIM = 64
SW_QH = D_MODEL // 128
SW_KVH = SW_QH // 4
SW_G = SW_QH // SW_KVH
SW_Q_W = SW_QH * SW_DIM
SW_KV_W = SW_KVH * SW_DIM
WINDOW = 128
D_FF = 4 * D_MODEL
IN_SIZES = (SB_W, SB_W, SB_W,
            RET_QK_W, RET_QK_W, RET_V_W, RET_V_W,
            RW_IN,
            SW_Q_W, SW_KV_W, SW_KV_W,
            N_BRANCH * D_MODEL)
N_IN = 3 * SB_W + 2 * RET_QK_W + 2 * RET_V_W + RW_IN + SW_Q_W + 2 * SW_KV_W + N_BRANCH * D_MODEL

kernel_name = 'hybrid_gated_four_mixer_block'

def _split(z, sizes):
    return jnp.split(z, np.cumsum(np.array(sizes))[:-1].tolist(), axis=-1)

def _rms(x, g=None, eps=EPS):
    xf = x.astype(jnp.float32)
    y = xf * lax.rsqrt(jnp.mean(xf * xf, axis=-1, keepdims=True) + eps)
    if g is not None:
        y = y * g.astype(jnp.float32)
    return y

def stick_breaking_attention(q, k, v, valid):
    B, L, H, Dh = q.shape
    nb = L // BLOCK
    scale = Dh ** -0.5
    qb = q.reshape(B, nb, BLOCK, H, Dh).transpose(1, 0, 3, 2, 4)
    kpos = jnp.arange(L)

    def one_block(args):
        qblk, b = args
        z = jnp.einsum('bhqd,bkhd->bhqk', qblk, k).astype(jnp.float32) * scale
        qpos = b * BLOCK + jnp.arange(BLOCK)
        allowed = (kpos[None, :] < qpos[:, None]) & valid[None, :]
        log_1mb = jnp.where(allowed, jax.nn.log_sigmoid(-z), 0.0)
        after = lax.cumsum(log_1mb, axis=3, reverse=True) - log_1mb
        log_a = jax.nn.log_sigmoid(z) + after
        a = jnp.where(allowed, jnp.exp(log_a), 0.0)
        return jnp.einsum('bhqk,bkhd->bqhd', a.astype(v.dtype), v)

    out = lax.map(one_block, (qb, jnp.arange(nb)))
    return out.transpose(1, 0, 2, 3, 4).reshape(B, L, H * Dh)

def retention(q, k, v):
    B, L, H, dk = q.shape
    dv = v.shape[-1]
    nc = L // BLOCK
    f32 = jnp.float32
    log_g = jnp.log(1.0 - 2.0 ** (-5.0 - jnp.arange(H, dtype=f32)))
    qc = q.astype(f32).reshape(B, nc, BLOCK, H, dk)
    kc = (k.astype(f32) * dk ** -0.5).reshape(B, nc, BLOCK, H, dk)
    vc = v.astype(f32).reshape(B, nc, BLOCK, H, dv)
    idx = jnp.arange(BLOCK, dtype=f32)
    diff = idx[:, None] - idx[None, :]
    dmask = jnp.where(diff >= 0, jnp.exp(log_g[:, None, None] * jnp.maximum(diff, 0.0)), 0.0)
    scores = jnp.einsum('bcihd,bcjhd->bchij', qc, kc) * dmask
    o_intra = jnp.einsum('bchij,bcjhe->bcihe', scores, vc)
    k_dec = kc * jnp.exp((BLOCK - 1 - idx)[:, None] * log_g[None, :])[:, :, None]
    kv = jnp.einsum('bcjhd,bcjhe->cbhde', k_dec, vc)
    chunk_decay = jnp.exp(log_g * BLOCK)[None, :, None, None]

    def step(S, kv_c):
        return S * chunk_decay + kv_c, S

    _, s_prev = lax.scan(step, jnp.zeros((B, H, dk, dv), f32), kv)
    q_dec = qc * jnp.exp((idx + 1.0)[:, None] * log_g[None, :])[:, :, None]
    o = o_intra + jnp.einsum('bcihd,cbhde->bcihe', q_dec, s_prev)
    o = _rms(o)
    return o.reshape(B, L, H * dv)

def rwkv7_project(c_in, mu, w0, w2, a0, a2, g2, k_k, k_a):
    B, L, _ = c_in.shape
    prev = jnp.pad(c_in, ((0, 0), (1, 0), (0, 0)))[:, :-1]
    c = c_in + (prev - c_in) * mu
    r, k, v, w_d, a_d, g_d = _split(c, (RW_W, RW_W, RW_W, RW_W_LORA, RW_A_LORA, RW_G_LORA))
    w = -jax.nn.softplus(-(w0 + jnp.tanh(w_d) @ w2)) - 0.5
    decay = jnp.exp(-jnp.exp(w.astype(jnp.float32)))
    a = jax.nn.sigmoid(a0 + a_d @ a2)
    g = jax.nn.sigmoid(g_d) @ g2
    kk = (k * k_k).reshape(B, L, RW_HEADS, RW_DIM).astype(jnp.float32)
    kk = kk / jnp.maximum(jnp.linalg.norm(kk, axis=-1, keepdims=True), 1e-12)
    kk = kk.reshape(B, L, RW_W)
    k = k * (1.0 + (a - 1.0) * k_a)
    return r, decay, k, v, kk, a, g

def rwkv7_mix(r, decay, k, v, kk, a, g, r_k, ln_g, ln_b):
    B, L, C = r.shape
    f32 = jnp.float32

    def hd(t):
        return t.reshape(B, L, RW_HEADS, RW_DIM).astype(f32)

    r_, w_, k_, v_, kk_, a_ = hd(r), hd(decay), hd(k), hd(v), hd(kk), hd(a)
    b_ = kk_ * a_

    def step(S, inp):
        r_t, w_t, k_t, v_t, kk_t, b_t = inp
        S = (S * w_t[:, :, None, :]
             - jnp.einsum('bhij,bhj->bhi', S, kk_t)[..., None] * b_t[:, :, None, :]
             + v_t[..., None] * k_t[:, :, None, :])
        return S, jnp.einsum('bhij,bhj->bhi', S, r_t)

    xs = tuple(t.transpose(1, 0, 2, 3) for t in (r_, w_, k_, v_, kk_, b_))
    _, y = lax.scan(step, jnp.zeros((B, RW_HEADS, RW_DIM, RW_DIM), f32), xs)
    y = y.transpose(1, 0, 2, 3)
    mean = jnp.mean(y, axis=-1, keepdims=True)
    var = jnp.mean(jnp.square(y - mean), axis=-1, keepdims=True)
    y = ((y - mean) * lax.rsqrt(var + RW_LN_EPS)).reshape(B, L, C) * ln_g + ln_b
    bonus = jnp.sum(r_ * k_ * r_k, axis=-1, keepdims=True) * v_
    y = y + bonus.reshape(B, L, C)
    return y * g

def sliding_window_attention(q, k, v, qn_g, kn_g, sink):
    B, L, _ = q.shape
    nb = L // BLOCK
    f32 = jnp.float32
    q = _rms(q.reshape(B, L, SW_KVH, SW_G, SW_DIM), qn_g)
    k = _rms(k.reshape(B, L, SW_KVH, SW_DIM), kn_g)
    v = v.reshape(B, L, SW_KVH, SW_DIM).astype(f32)
    scale = SW_DIM ** -0.5
    qb = q.reshape(B, nb, BLOCK, SW_KVH, SW_G, SW_DIM)

    def band(t):
        tb = t.reshape(B, nb, BLOCK, SW_KVH, SW_DIM)
        prev = jnp.pad(tb, ((0, 0), (1, 0), (0, 0), (0, 0), (0, 0)))[:, :-1]
        return jnp.concatenate([prev, tb], axis=2)

    kband, vband = band(k), band(v)
    k_meta, v_meta = k[:, N_PAD:BLOCK], v[:, N_PAD:BLOCK]
    qpos = jnp.arange(nb)[:, None] * BLOCK + jnp.arange(BLOCK)[None, :]
    kpos = jnp.arange(nb)[:, None] * BLOCK - BLOCK + jnp.arange(2 * BLOCK)[None, :]
    dist = qpos[:, :, None] - kpos[:, None, :]
    band_ok = (dist >= 0) & (dist < WINDOW) & (kpos[:, None, :] >= BLOCK)
    meta_ok = (N_PAD + jnp.arange(N_META))[None, None, :] <= qpos[:, :, None]
    slopes = (2.0 ** (-8.0 * jnp.arange(1, SW_QH + 1, dtype=f32) / SW_QH)).reshape(SW_KVH, SW_G)
    s_band = (jnp.einsum('bnqhgd,bnkhd->bnhgqk', qb, kband) * scale
              - slopes[:, :, None, None] * dist[:, None, None].astype(f32))
    s_band = jnp.where(band_ok[:, None, None], s_band, -jnp.inf)
    s_meta = jnp.einsum('bnqhgd,bmhd->bnhgqm', qb, k_meta) * scale
    s_meta = jnp.where(meta_ok[:, None, None], s_meta, -jnp.inf)
    sink_logit = jnp.broadcast_to(sink.reshape(SW_KVH, SW_G).astype(f32)[None, None, :, :, None, None],
                                  (B, nb, SW_KVH, SW_G, BLOCK, 1))
    p = jax.nn.softmax(jnp.concatenate([s_meta, s_band, sink_logit], axis=-1), axis=-1)
    o = (jnp.einsum('bnhgqm,bmhd->bnqhgd', p[..., :N_META], v_meta)
         + jnp.einsum('bnhgqk,bnkhd->bnqhgd', p[..., N_META:N_META + 2 * BLOCK], vband))
    return o.reshape(B, L, SW_Q_W)

def squared_relu_mlp(h, w_up, w_down):
    u = jax.nn.relu(h @ w_up)
    return (u * u) @ w_down

def setup_inputs(seed: int = 0) -> dict:
    key = jax.random.key(seed)
    keys = list(jax.random.split(key, 40))
    f32 = jnp.float32
    D = D_MODEL

    def nrm(shape, scale):
        return jax.random.normal(keys.pop(), shape, f32) * scale

    def gain(shape):
        return 1.0 + nrm(shape, 0.05)

    return {
        'x': nrm((BATCH, SEQ, D), 1.0),
        'meta': nrm((N_META, D), 1.0),
        'norm1_g': gain((DEPTH, D)),
        'w_in': nrm((DEPTH, D, N_IN), D ** -0.5),
        'rw_mu': jax.random.uniform(keys.pop(), (DEPTH, RW_IN), f32),
        'rw_w0': jax.random.uniform(keys.pop(), (DEPTH, RW_W), f32, -6.0, -1.0),
        'rw_w2': nrm((DEPTH, RW_W_LORA, RW_W), 0.5 * RW_W_LORA ** -0.5),
        'rw_a0': nrm((DEPTH, RW_W), 0.5),
        'rw_a2': nrm((DEPTH, RW_A_LORA, RW_W), 0.5 * RW_A_LORA ** -0.5),
        'rw_g2': nrm((DEPTH, RW_G_LORA, RW_W), RW_G_LORA ** -0.5),
        'rw_kk': 1.0 + nrm((DEPTH, RW_W), 0.1),
        'rw_ka': 1.0 + nrm((DEPTH, RW_W), 0.1),
        'rw_rk': nrm((DEPTH, RW_HEADS, RW_DIM), 0.1),
        'rw_ln_g': gain((DEPTH, RW_W)),
        'rw_ln_b': nrm((DEPTH, RW_W), 0.02),
        'rw_v0': nrm((DEPTH - 1, RW_W), 0.5),
        'rw_v1': nrm((DEPTH - 1, D, RW_V_LORA), D ** -0.5),
        'rw_v2': nrm((DEPTH - 1, RW_V_LORA, RW_W), 0.5 * RW_V_LORA ** -0.5),
        'sw_qn_g': gain((DEPTH, SW_DIM)),
        'sw_kn_g': gain((DEPTH, SW_DIM)),
        'sw_sink': nrm((DEPTH, SW_QH), 0.5),
        'p_sb': nrm((DEPTH, SB_W, D), SB_W ** -0.5),
        'p_ret': nrm((DEPTH, RET_V_W, D), RET_V_W ** -0.5),
        'p_rw': nrm((DEPTH, RW_W, D), RW_W ** -0.5),
        'p_sw': nrm((DEPTH, SW_Q_W, D), SW_Q_W ** -0.5),
        'w_o': nrm((DEPTH, D, D), D ** -0.5),
        'norm2_g': gain((DEPTH, D)),
        'w_up': nrm((DEPTH, D, D_FF), D ** -0.5),
        'w_down': nrm((DEPTH, D_FF, D), 0.5 * D_FF ** -0.5),
    }

def reference(x, meta, norm1_g, w_in, rw_mu, rw_w0, rw_w2, rw_a0, rw_a2, rw_g2,
              rw_kk, rw_ka, rw_rk, rw_ln_g, rw_ln_b, rw_v0, rw_v1, rw_v2,
              sw_qn_g, sw_kn_g, sw_sink, p_sb, p_ret, p_rw, p_sw, w_o,
              norm2_g, w_up, w_down):
    B = x.shape[0]
    dt = x.dtype
    pad = jnp.zeros((B, N_PAD, D_MODEL), dt)
    metas = jnp.broadcast_to(meta.astype(dt)[None], (B, N_META, D_MODEL))
    x = jnp.concatenate([pad, metas, x], axis=1)
    L = x.shape[1]
    valid_b = jnp.arange(L) >= N_PAD
    valid = valid_b[None, :, None].astype(dt)
    v_first = None
    for l in range(DEPTH):
        h = (_rms(x, norm1_g[l]) * valid).astype(dt)
        z = h @ w_in[l]
        aq, ak, av, bq, bk, bv, bg, c_in, dq, dk, dv, gz = _split(z, IN_SIZES)
        y_sb = stick_breaking_attention(aq.reshape(B, L, SB_HEADS, SB_DIM),
                                        ak.reshape(B, L, SB_HEADS, SB_DIM),
                                        av.reshape(B, L, SB_HEADS, SB_DIM), valid_b)
        y_ret = jax.nn.silu(bg.astype(jnp.float32)) * retention(
            bq.reshape(B, L, RET_HEADS, RET_QK), bk.reshape(B, L, RET_HEADS, RET_QK),
            bv.reshape(B, L, RET_HEADS, RET_V))
        r, decay, k, v, kk, a, g = rwkv7_project(c_in, rw_mu[l], rw_w0[l], rw_w2[l], rw_a0[l],
                                                 rw_a2[l], rw_g2[l], rw_kk[l], rw_ka[l])
        if l == 0:
            v_first = v
        else:
            v = v + (v_first - v) * jax.nn.sigmoid(rw_v0[l - 1] + (h @ rw_v1[l - 1]) @ rw_v2[l - 1])
        y_rw = rwkv7_mix(r, decay, k, v, kk, a, g, rw_rk[l], rw_ln_g[l], rw_ln_b[l])
        y_sw = sliding_window_attention(dq, dk, dv, sw_qn_g[l], sw_kn_g[l], sw_sink[l])
        gates = jax.nn.sigmoid(gz.astype(jnp.float32)).reshape(B, L, N_BRANCH, D_MODEL)
        merged = (gates[:, :, 0] * (y_sb.astype(dt) @ p_sb[l])
                  + gates[:, :, 1] * (y_ret.astype(dt) @ p_ret[l])
                  + gates[:, :, 2] * (y_rw.astype(dt) @ p_rw[l])
                  + gates[:, :, 3] * (y_sw.astype(dt) @ p_sw[l]))
        x = x + (merged.astype(dt) @ w_o[l]).astype(dt)
        h2 = _rms(x, norm2_g[l]).astype(dt)
        x = x + squared_relu_mlp(h2, w_up[l], w_down[l]).astype(dt)
    return x[:, BLOCK:]


_drawn_inputs = setup_inputs


def setup_inputs(seed=0):
    import zlib

    import numpy as np

    out = dict(_drawn_inputs(seed))
    spreads = {}
    factors = {'rw_w2': 8.0,
     'rw_kk': 2.827,
     'rw_ln_g': 4.39,
     'rw_ln_b': 8.0,
     'sw_qn_g': 8.0,
     'sw_kn_g': 8.0,
     'sw_sink': 8.0,
     'norm2_g': 2.855}
    for name, (base, spread) in spreads.items():
        noise = np.random.default_rng([zlib.crc32(name.encode()), seed]).standard_normal(out[name].shape)
        drawn = base * np.exp(spread * noise) if base else spread * noise
        out[name] = __import__('jax').numpy.asarray(drawn.astype(out[name].dtype))
    for name, factor in factors.items():
        out[name] = (out[name] * factor).astype(out[name].dtype)
    return out
```

```python
from contextlib import ExitStack

import numpy as np
import concourse.bass as bass
from concourse import mybir

ALU = mybir.AluOpType
ACT = mybir.ActivationFunctionType
AX = mybir.AxisListType
F32 = mybir.dt.float32
F32R = mybir.dt.float32r

P = 128
D = 1024
KD = D // P
T = 512
NB = T // P
N_META = 16
MB = 32
L = MB + T
HL = L // 2
DFF = 4 * D
EPS = 1e-6
RW_LN_EPS = 64e-5
HD = 64
SBH = 8
RWH = 8
RETH = 4
SWH = 8
CH = 64
NCHUNK = 1 + T // CH
LEVELS = 6
NEG = -1.0e30

AQ, AK, AV, BQ, BK, BV, BG, CIN, DQ, DK, DV, GZ = 0, 4, 8, 12, 14, 16, 20, 24, 38, 42, 43, 44
CR, CK, CV, CWA, CG = 0, 4, 8, 12, 13
BRANCH_SB, BRANCH_RET, BRANCH_RW, BRANCH_SW = 0, 1, 2, 3

RAW_SLOTS = 3
W_SLOTS = 4
UW = KD * P


def merge_jobs(br):
    out = []
    for half in range(2):
        out += [("gate", br, 4 * half + i) for i in range(4)]
        out += [("proj", br, 4 * half + i) for i in range(4)]
    return out


def av_jobs(name):
    return [(name, pair, blk) for pair in range(2) for blk in range(NB + 1)]


PHASE_C = [("c", i, 0) for i in (CWA, CG)] + [("c", i, 0) for i in (CK, CR, CV)] + \
          [("c", i + t, 0) for t in range(1, 4) for i in (CK, CR, CV)]
PHASE_A = [("aq", t, 0) for t in range(4)] + [("ak", t, 0) for t in range(4)] + av_jobs("av")
PHASE_B = [("bq", t, 0) for t in range(2)] + [("bk", t, 0) for t in range(2)] + av_jobs("bv") + \
          [("bg", t, 0) for t in range(4)]
PHASE_D = [("dq", t, 0) for t in range(4)] + [("dk", 0, 0)] + [("dv", 0, b) for b in range(NB + 1)]
PHASE_O = [("wo", c, b) for c in range(4) for b in range(NB)]
FH = DFF // P // 2


def up_jobs(half):
    return [("up", half, f) for f in range(FH)]


def down_jobs(half):
    return [("down", half, (c, kk)) for c in range(2) for kk in range(FH // 2)]


JOBS = (PHASE_C + merge_jobs(BRANCH_RW) + PHASE_A + merge_jobs(BRANCH_SB) + PHASE_B + merge_jobs(BRANCH_RET) +
        PHASE_D + merge_jobs(BRANCH_SW) + PHASE_O + up_jobs(0) + down_jobs(0) + up_jobs(1) + down_jobs(1))
JOB_NO = {j: n for n, j in enumerate(JOBS)}


def units_of(job):
    kind, a, b = job
    if kind == "c":
        return [("w_in", CIN + a)]
    if kind in ("aq", "ak", "bq", "bk", "bg", "dq", "dk", "dv"):
        base = {"aq": AQ, "ak": AK, "bq": BQ, "bk": BK, "bg": BG, "dq": DQ, "dk": DK, "dv": DV}[kind]
        return [("w_in", base + a)]
    if kind in ("av", "bv"):
        base = {"av": AV, "bv": BV}[kind]
        return [("w_in", base + 2 * a), ("w_in", base + 2 * a + 1)]
    if kind == "gate":
        return [("w_in", GZ + KD * a + b)]
    if kind == "proj":
        return [("p", a, b // 2)]
    if kind == "wo":
        return [("w_o", 2 * a), ("w_o", 2 * a + 1)]
    if kind == "up":
        return [("w_up", a * FH + b)]
    c, kk = b
    return [("w_down", a * FH // 2 + kk, c)]


UNITS, UNIT_NO, LAST_JOB = [], {}, {}
for _n, _j in enumerate(JOBS):
    for _u in units_of(_j):
        if _u not in UNIT_NO:
            UNIT_NO[_u] = len(UNITS)
            UNITS.append(_u)
        LAST_JOB[UNIT_NO[_u]] = _n
NU = len(UNITS)
KIND_NO, _c = [], {}
for _j in JOBS:
    KIND_NO.append(_c.get(_j[0], 0))
    _c[_j[0]] = KIND_NO[-1] + 1
assert all(UNIT_NO[units_of(j)[0]] % 2 == 0 for j in JOBS if j[0] in ("av", "bv", "wo"))


def pack_weights(w_in, p_sb, p_ret, p_rw, p_sw, w_o, w_up, w_down):
    ps = (p_sb, p_ret, p_rw, p_sw)
    out = np.empty((NU, P, UW), np.float32)
    for n, u in enumerate(UNITS):
        if u[0] == "p":
            m = ps[u[1]][0][:, 256 * u[2]:256 * u[2] + 256]
        elif u[0] == "w_down":
            m = w_down[0][256 * u[1]:256 * u[1] + 256, 512 * u[2]:512 * u[2] + 512]
        else:
            m = {"w_in": w_in, "w_o": w_o, "w_up": w_up}[u[0]][0][:, P * u[1]:P * u[1] + P]
        out[n] = m.reshape(-1, P, m.shape[1]).transpose(1, 0, 2).reshape(P, UW)
    return out


def constants():
    i = np.arange(P)
    c = {"ident": np.eye(P), "headsum": (i[:, None] // HD == i[None, :] // HD) * 1.0}
    s, t = i[:, None], i[None, :]
    same = s // CH == t // CH
    c["rw_mask"] = np.concatenate([same & (s < t), same & (s <= t)], 1)
    c["levels"] = np.concatenate(
        [(s // (2 << l) == t // (2 << l)) & ((s >> l) % 2 == 0) & ((t >> l) % 2 == 1) for l in range(LEVELS)], 1)
    start = np.ones(L)
    start[[0] + [MB + CH * k for k in range(T // CH)]] = 0
    c["scan_keep"] = np.broadcast_to(start, (P, L))
    c["suffix"] = -1.0 * (s >= t)
    c["suffix_meta"] = -1.0 * ((s >= t) & (s // MB == t // MB))
    strip = np.zeros((P, 3 * MB + MB + 3 * MB))
    strip[:, 3 * MB:4 * MB] = -1.0
    c["carry_meta"] = strip
    c["neg_ones"] = -np.ones((P, P))
    g = 1.0 - 2.0 ** (-5.0 - np.arange(RETH))
    diff = t - s
    c["ret_mask"] = np.concatenate([np.where(diff >= 0, gh ** np.maximum(diff, 0), 0) * HD ** -0.5 for gh in g], 1)
    c["ret_kdec"] = np.stack([gh ** (P - 1 - i) for gh in g], 1) * HD ** -0.5
    c["ret_kdec_meta"] = np.stack([gh ** np.maximum(MB - 1 - i, 0) for gh in g], 1) * HD ** -0.5
    c["ret_qdec"] = np.concatenate(
        [np.where(i[:, None] < HD, g[2 * p] ** (t + 1.0), g[2 * p + 1] ** (t + 1.0)) for p in range(2)], 1)
    key = np.arange(2 * P)[None, :]
    dist = (i[:, None] + P) - key
    band = np.where((dist >= 0) & (dist < P), -dist, NEG)
    meta = np.where(np.arange(MB)[None, :] < MB - N_META, NEG, 0.0) + 0.0 * i[:, None]
    c["sw_bias"] = np.concatenate([meta, band], 1)
    return {k: np.ascontiguousarray(v, np.float32) for k, v in c.items()}


RET_CHUNK_DECAY = [float((1.0 - 2.0 ** (-5.0 - h)) ** P) for h in range(RETH)]
CONSTS = constants()
CONST_AT, _o = {}, 0
for _k, _v in CONSTS.items():
    CONST_AT[_k] = (_o, _v.shape[1])
    _o += _v.shape[1]
NCONST = _o

PARAMS = [("norm1_g", 8), ("norm2_g", 8), ("rw_mu", 14), ("rw_w0", 4), ("rw_a0", 4), ("rw_kk", 4), ("rw_ka", 4),
          ("rw_rk", 4), ("rw_ln_g", 4), ("rw_ln_b", 4), ("qn", 1), ("kn", 1), ("sink", 8)]
PARAM_AT, _o = {}, 0
for _k, _n in PARAMS:
    PARAM_AT[_k] = (_o, _n)
    _o += _n
NPARAM = _o

SBUF_BASE, SBUF_END = 16512, 229344


def build(nc, x, meta, weights, lora, consts, params, out, debug=None, upto="all"):
    with ExitStack() as ctx:
        cursor = [SBUF_BASE]

        def place(name, shape, dt=F32, at=None):
            size = 4 * int(np.prod(shape[1:]))
            size = (size + 31) // 32 * 32
            if at is None:
                at = cursor
            t = nc.alloc_sbuf_tensor_at(name, shape, dt, offset=at[0])
            at[0] += size
            assert at[0] <= SBUF_END, (name, at[0])
            return t

        slab = SBUF_BASE
        cst = place("cst", [P, NCONST])
        par = place("par", [P, NPARAM])
        half_wa = place("half_wa", [P, 8])
        one_minus_ka = place("one_minus_ka", [P, 4])
        gain_q = place("gain_q", [P, 1])
        lor = place("lor", [P, 2 * T])
        h_hi = place("h_hi", [P, KD, L], F32R)
        h_lo = place("h_lo", [P, KD, L], F32R)
        raw = place("raw", [P, RAW_SLOTS, UW])
        w_hi = place("w_hi", [P, W_SLOTS, UW], F32R)
        w_lo = place("w_lo", [P, W_SLOTS, UW], F32R)
        region = cursor[0]

        at = [region]
        xt = place("xt", [P, NB, D], at=at)
        xm = place("xm", [MB, D], at=at)
        sq0 = place("sq0", [P, D], at=at)
        ss0 = place("ss0", [P, NB + 1], at=at)
        rs0 = place("rs0", [P, NB + 1], at=at)

        at = [region]
        KR = place("rw_kappa_r", [P, 4, 2, L], at=at)
        KH = place("rw_k", [P, 4, L], at=at)
        BH = place("rw_b", [P, 4, L], at=at)
        RV = place("rw_v", [P, 4, L], at=at)
        BON = place("rw_bonus", [P, 4, L], at=at)
        SG = place("rw_sig_g", [P, L], at=at)
        GC = place("rw_chunk_decay", [P, 4, NCHUNK], at=at)
        mix_at = at[0]
        cbuf = place("cbuf", [P, 3, L + 1], at=at)
        cdif = place("cdif", [P, L], at=at)
        WA = place("rw_wa", [P, L], at=at)
        tmp_names = ["LAM", "AA", "LG", "LGX", "KKR", "T1", "SQ", "RN", "BB", "E1", "E2", "E3"]
        tt = {k: place("rw_" + k, [P, L], at=at) for k in tmp_names}
        at = [mix_at]
        KT = place("rw_k_tok", [P, T], at=at)
        BT = place("rw_b_tok", [P, T], at=at)
        VT = place("rw_v_tok", [P, T], at=at)
        FK = place("rw_wz", [P, RWH, 2, HD], at=at)
        AM = place("rw_scores", [P, RWH, 4, P], at=at)
        XX = place("rw_x", [P, RWH, P], at=at)
        TT = place("rw_t", [P, RWH, P], at=at)
        C1 = place("rw_c1", [P, RWH, P], at=at)
        MM = place("rw_m", [P, 2, RWH, P], at=at)
        MD = place("rw_md", [P, 2, 4, P], at=at)
        QD = place("rw_qd", [P, 2, 4, P], at=at)
        QQ = place("rw_q", [P, 4, HD], at=at)
        NG = place("rw_ng", [P, 2, 4, HD], at=at)
        at = [mix_at]
        post = {k: place("rwp_" + k, [P, 2, T], at=at) for k in ("sq", "rs", "bon")}
        at = [SBUF_END - 4 * (2 * 4 * T + 4 * T + 2 * T + KD * T)]
        y_hi = place("y_hi", [P, 4, T], F32R, at=at)
        y_lo = place("y_lo", [P, 4, T], F32R, at=at)
        gate_t = place("gate_t", [P, 4, T], at=at)
        gtmp = place("gtmp", [P, 2, T], at=at)
        merged = place("merged", [P, KD, T], at=at)

        at = [region]
        sb_q = place("sb_q", [P, 4, T], at=at)
        sb_k = place("sb_k", [P, 4, L], at=at)
        sb_v = place("sb_v", [P, NB, T], at=at)
        sb_vm = place("sb_vm", [MB, T], at=at)
        sb_kmd = place("sb_kmd", [P, 4, P], at=at)
        sb_vmd = place("sb_vmd", [P, SBH, HD], at=at)
        sb_e = place("sb_e", [P, 3, T], at=at)
        sb_s = place("sb_s", [P, 3, T], at=at)
        sb_cs = place("sb_cs", [P, 3, T], at=at)
        sb_em = place("sb_em", [P, T], at=at)
        sb_sm = place("sb_sm", [P, T], at=at)
        assert at[0] <= SBUF_END - 45056
        at = [region]
        rq = place("ret_q", [P, 2, T], at=at)
        rk = place("ret_k", [P, 2, L], at=at)
        rv = place("ret_v", [P, NB, T], at=at)
        rvm = place("ret_vm", [MB, T], at=at)
        rg = place("ret_g", [P, 4, T], at=at)
        rth = place("ret_th", [P, 4, T], at=at)
        rqd = place("ret_qd", [P, 2, T], at=at)
        rkd = place("ret_kd", [P, RETH, HD], at=at)
        rsc = place("ret_sc", [P, RETH, P], at=at)
        rsz = place("ret_state", [P, RETH, P], at=at)
        ro = place("ret_o", [P, RETH, T], at=at)
        rsq = place("ret_sq", [P, 2, T], at=at)
        assert at[0] <= SBUF_END - 45056
        at = [region]
        dq = place("sw_q", [P, 4, T], at=at)
        dk = place("sw_k", [P, L], at=at)
        dk2 = place("sw_k2", [P, 2, L], at=at)
        dv = place("sw_v", [P, NB, P], at=at)
        dvm = place("sw_vm", [MB, P], at=at)
        dsq = place("sw_sq", [P, 2, L], at=at)
        dsc = place("sw_scores", [P, 2, 4, MB + 2 * P], at=at)
        dpt = place("sw_probs_t", [P, 2, 3, T], at=at)
        dst_ = place("sw_stats", [P, 2, 5, 4], at=at)
        assert at[0] <= SBUF_END - 45056
        at = [region]
        x2 = place("x2", [P, NB, D], at=at)
        u_hi = place("u_hi", [P, FH, T], F32R, at=at)
        u_lo = place("u_lo", [P, FH, T], F32R, at=at)
        ub = place("ub", [P, 2, T], at=at)
        usq = place("usq", [P, 2, T], at=at)
        ss2 = place("ss2", [P, 2, NB], at=at)
        assert at[0] <= SBUF_END - 16384
        h2n = place("h2n", [P, NB, D], at=[SBUF_END - 16384])

        pst = ctx.enter_context(nc.psum_tensor("pst", [P, 8, 512], F32))

        def sem(name):
            return ctx.enter_context(nc.semaphore(name))

        const_in = sem("const_in")
        x_in = sem("x_in")
        raw_in = [sem(f"raw_in{i}") for i in range(RAW_SLOTS)]
        hi_ready = sem("hi_ready")
        lo_ready = sem("lo_ready")
        dense_done = sem("dense_done")
        dve_step, act_step, pool_step = sem("dve_step"), sem("act_step"), sem("pool_step")
        ss_ready = sem("ss_ready")
        rs_ready = sem("rs_ready")
        hn_ready = sem("hn_ready")
        ht_done = sem("ht_done")
        hhi_ready = sem("hhi_ready")
        hlo_ready = sem("hlo_ready")
        par_ready = sem("par_ready")
        zeros_ready, cbuf_zeroed, diag_zeroed = sem("zeros_ready"), sem("cbuf_zeroed"), sem("diag_zeroed")
        c_copied, c_mixed = sem("c_copied"), sem("c_mixed")
        wa_tanh, sg_tanh, sg_ready = sem("wa_tanh"), sem("sg_tanh"), sem("sg_ready")
        lora_done, lora_act = sem("lora_done"), sem("lora_act")
        kkr_ready, kksq_ready, kksum_done, kkclamped, rn_ready = (
            sem("kkr_ready"), sem("kksq_ready"), sem("kksum_done"), sem("kkclamped"), sem("rn_ready"))
        lg_ready, e_ready, rw_elem = sem("lg_ready"), sem("e_ready"), sem("rw_elem")
        tok_done, tok_act, tok_dve = sem("tok_done"), sem("tok_act"), sem("tok_dve")
        am_done, am_ready = sem("am_done"), sem("am_ready")
        m_ready = [sem("m_ready0"), sem("m_ready1")]
        c1_done = [sem("c1_done0"), sem("c1_done1")]
        c1_copied = [sem("c1_copied0"), sem("c1_copied1")]
        tu_done = [sem("tu_done0"), sem("tu_done1")]
        x_ready = [sem("x_ready0"), sem("x_ready1")]
        f_done, f_copied, wz_done, wz_ready = sem("f_done"), sem("f_copied"), sem("wz_done"), sem("wz_ready")
        rt_done, rt_ready = sem("rt_done"), sem("rt_ready")
        mn_done, mn_ready = sem("mn_done"), sem("mn_ready")
        qn_done, q_ready, qd_ready = sem("qn_done"), sem("q_ready"), sem("qd_ready")
        yy_done, yy_copied = sem("yy_done"), sem("yy_copied")
        post_done, postc_ready, postq_ready, postv_done, postr_ready, post_free = (
            sem("post_done"), sem("postc_ready"), sem("postq_ready"), sem("postv_done"), sem("postr_ready"),
            sem("post_free"))
        yf_ready, yh_ready, yl_ready = sem("yf_ready"), sem("yh_ready"), sem("yl_ready")
        gate_ready, merged_ready = sem("gate_ready"), sem("merged_ready")
        out_done = sem("out_done")
        job_out = {k: sem(k + "_out") for k in
                   ("aq", "ak", "av", "bq", "bk", "bv", "bg", "dq", "dk", "dv", "gate", "proj", "wo", "up", "down")}
        gate_tanh = sem("gate_tanh")
        sb_diag_zeroed, sb_kmd_ready, sb_vmd_ready = sem("sb_diag_zeroed"), sem("sb_kmd_ready"), sem("sb_vmd_ready")
        zm_done, zm_ln, zm_sp, zm_arg, zm_a = (
            sem("zm_done"), sem("zm_ln"), sem("zm_sp"), sem("zm_arg"), sem("zm_a"))
        z_done, z_ln, z_sp, z_spm, z_cs, z_arg, z_a, z_am, o_done = (
            sem("z_done"), sem("z_ln"), sem("z_sp"), sem("z_spm"), sem("z_cs"), sem("z_arg"),
            sem("z_a"), sem("z_am"), sem("o_done"))
        sb_used = sem("sb_used")
        rg_tanh, rg_ready, rqd_ready, rsz_zeroed = sem("rg_tanh"), sem("rg_ready"), sem("rqd_ready"), sem("rsz_zeroed")
        rkt_done, rkd_ready, rs_done, rsc_ready, rkv_done, rstate, ro_done, ro_ready = (
            sem("rkt_done"), sem("rkd_ready"), sem("rs_done"), sem("rsc_ready"), sem("rkv_done"), sem("rstate"),
            sem("ro_done"), sem("ro_ready"))
        rsq_ready, rss_done, rrs_ready, ry_ready = sem("rsq_ready"), sem("rss_done"), sem("rrs_ready"), sem("ry_ready")
        dsq_ready, dss_done, drs_ready, dn_ready, dk2_own, dk2_in = (
            sem("dsq_ready"), sem("dss_done"), sem("drs_ready"), sem("dn_ready"), sem("dk2_own"), sem("dk2_in"))
        ds_done, ds_read, dmx_ready, dexp_ready, dp_ready, dpt_done, dpt_act, dpt_dve, do_done = (
            sem("ds_done"), sem("ds_read"), sem("dmx_ready"), sem("dexp_ready"), sem("dp_ready"), sem("dpt_done"),
            sem("dpt_act"), sem("dpt_dve"), sem("do_done"))
        x2_in, m_hi, m_lo = sem("x2_in"), sem("m_hi"), sem("m_lo")
        ss2_ready, rs2_ready, h2n_ready, h2t_done, h2hi_ready, h2lo_ready = (
            sem("ss2_ready"), sem("rs2_ready"), sem("h2n_ready"), sem("h2t_done"), sem("h2hi_ready"), sem("h2lo_ready"))
        u_hi_ready, u_lo_ready = sem("u_hi_ready"), sem("u_lo_ready")

        def C(name, lo=0, hi=None, rows=P):
            a, n = CONST_AT[name]
            return cst[0:rows, a + lo:a + (n if hi is None else hi)]

        def PAR(name, t):
            a, _ = PARAM_AT[name]
            return par[:, a + t:a + t + 1]

        ident = C("ident")
        headsum = C("headsum")
        w2, a2, g2 = lor[0:HD, 0:T], lor[HD:P, 0:T], lor[:, T:2 * T]

        def pair(slot):
            return pst[:, 2 * slot:2 * slot + 2, 0:HL]

        def halves(row):
            return row.rearrange("p (a b) -> p a b", a=2)

        def job_slot(n):
            return n % 2

        def kind_no(n):
            return KIND_NO[n]

        def emptied(n):
            kind, a, b = JOBS[n]
            if kind == "c":
                return c_copied, kind_no(n) + 1
            if kind == "down":
                half, (c, kk) = a, b
                return job_out["down"], 4 * (2 * half + c) + 4
            return job_out[kind], kind_no(n) + 1

        def down_bank(c, blk):
            return (4 if c == 0 else 0) + blk

        def all_out(kind, job):
            return emptied(JOB_NO[job])

        br_order = [BRANCH_RW, BRANCH_SB, BRANCH_RET, BRANCH_SW]

        def y_count(br):
            return 4 * br_order.index(br)

        def y_free(br):
            n = br_order.index(br)
            return JOB_NO[("proj", br_order[n - 1], KD - 1)] + 1

        JOBN = JOB_NO
        NRUN = len(JOBS)
        NUNITS = NU
        ends = {"rw": PHASE_C[-1], "ysb": PHASE_A[-1], "yret": PHASE_B[-1], "ysw": PHASE_D[-1]}
        if upto in ends:
            NRUN = JOB_NO[ends[upto]] + 1
            NUNITS = UNIT_NO[units_of(JOBS[NRUN - 1])[-1]] + 1
        rw_blocks = [(MB, 0)] + [(P, MB + P * b) for b in range(NB)]
        levels_of = [LEVELS - 1] + [LEVELS] * NB
        level0 = [sum(levels_of[:b]) for b in range(NB + 1)]
        tblocks = rw_blocks

        block = ctx.enter_context(nc.Block())

        def debug_srcs():
            cnt = {"rw": 4, "ysb": 8, "yret": 12, "ysw": 20}[upto]
            return {
                "hh": (h_hi[:].bitcast(F32), yl_ready, cnt),
                "yh": (y_hi[:].bitcast(F32), yl_ready, cnt), "yl": (y_lo[:].bitcast(F32), yl_ready, cnt),
            }

        def run_after_rw(engine, jobs, f):
            g = lambda name, *a: f[name](*a) if name in f else None
            if upto == "rw":
                return
            jobs(16)
            g("sb_prep")
            jobs(8)
            jobs(len(PHASE_A) - 8)
            g("sb_values")
            for grp in range(2):
                g("sb_meta", grp)
                for h in range(4 * grp, 4 * grp + 4):
                    g("sb_z", h)
                    g("sb_mask", h)
                    g("sb_sums", h)
                    g("sb_arg", h)
                    g("sb_amask", h)
                    g("sb_o", h)
                g("sb_end", grp)
            if upto == "ysb":
                return
            jobs(16)
            g("ret_prep")
            jobs(len(PHASE_B))
            g("ret_gate")
            for b in range(NB + 1):
                g("ret_block", b)
            g("ret_post")
            if upto == "yret":
                return
            jobs(16)
            jobs(len(PHASE_D))
            g("sw_norm")
            for b in range(NB):
                for kv in range(2):
                    g("sw_scores", b, kv)
                    g("sw_probs", b, kv)
                    g("sw_out", b, kv)
            if upto == "ysw":
                return
            jobs(16)
            g("merge_split")
            jobs(len(PHASE_O))
            g("norm2")
            for half in range(2):
                jobs(FH)
                jobs(FH)

        @block.sync
        def _(sp):
            sp.dma_start(xt[:], x[0].rearrange("(b p) d -> p b d", p=P)).then_inc(x_in, 16)
            sp.wait_ge(zeros_ready, 1)
            sp.dma_start(xm[MB - N_META:MB, :], meta).then_inc(x_in, 16)
            sp.dma_start(cst[:], consts).then_inc(const_in, 16)
            sp.dma_start(par[:], params).then_inc(const_in, 16)
            sp.dma_start(lor[:], lora).then_inc(const_in, 16)
            for u in range(NUNITS):
                if u >= RAW_SLOTS:
                    sp.wait_ge(lo_ready, u - RAW_SLOTS + 1)
                sp.dma_start(raw[:, u % RAW_SLOTS, :], weights[u]).then_inc(raw_in[u % RAW_SLOTS], 16)
            if debug is not None:
                n = 0
                for name, (src_, wait_sem, val) in debug_srcs().items():
                    sp.wait_ge(wait_sem, val)
                    sp.dma_start(debug[name], src_).then_inc(out_done, 16)
                    n += 16
                sp.wait_ge(out_done, n)
                return
            for c in range(2):
                for b in range(NB):
                    sp.wait_ge(job_out["down"], 8 + 4 * c + b + 1)
                    sp.dma_start(out[0, P * b:P * b + P, T * c:T * c + T], x2[:, b, T * c:T * c + T])\
                        .then_inc(out_done, 16)
            sp.wait_ge(out_done, 16 * 2 * NB)

        @block.gpsimd
        def _(pool):
            nc.gpsimd.memset(xm[:], 0.0).then_inc(zeros_ready, 1)
            done = [0]

            def low(upto_unit):
                while done[0] < min(upto_unit, NUNITS):
                    u = done[0]
                    pool.wait_ge(hi_ready, u + 1)
                    nc.gpsimd.tensor_tensor(w_lo[:, u % W_SLOTS, :], raw[:, u % RAW_SLOTS, :],
                                            w_hi[:, u % W_SLOTS, :].bitcast(F32), ALU.subtract).then_inc(lo_ready, 1)
                    done[0] += 1

            def sb_prep():
                pool.wait_ge(yl_ready, 4)
                nc.gpsimd.memset(sb_kmd[:], 0.0).then_inc(sb_diag_zeroed, 1)
                nc.gpsimd.memset(sb_vmd[:], 0.0).then_inc(pool_step, 1)

            def sb_values():
                pool.wait_ge(pool_step, 1)
                pool.wait_ge(*emptied(JOB_NO[("av", 1, 0)]))
                for h in range(SBH):
                    q = MB * (h % 4)
                    pool.dma_start(sb_vmd[q:q + MB, h, :], sb_vm[:, HD * h:HD * h + HD]).then_inc(sb_vmd_ready, 16)

            def sb_diag(tile):
                v = tile[:, :, 0:P]
                nc.gpsimd.affine_select(out=v, in_=v, compare_op=ALU.is_gt, fill=0.0, base=0,
                                        pattern=[[0, 3], [1, P]], channel_multiplier=-1)
                v = tile[:, 2, 2 * P:3 * P]
                return nc.gpsimd.affine_select(out=v, in_=v, compare_op=ALU.is_gt, fill=0.0, base=0,
                                               pattern=[[1, P]], channel_multiplier=-1)

            def sb_mask(h):
                pool.wait_ge(z_sp, h + 1)
                sb_diag(sb_s).then_inc(z_spm, 1)

            def sb_amask(h):
                pool.wait_ge(z_a, h + 1)
                sb_diag(sb_e).then_inc(z_am, 1)

            def ret_prep():
                pool.wait_ge(yl_ready, 8)
                nc.gpsimd.memset(rsz[:], 0.0).then_inc(rsz_zeroed, 1)

            low(UNIT_NO[units_of(PHASE_C[-1])[0]] + 1)
            pool.wait_ge(rw_elem, 4)
            nc.gpsimd.memset(MD[:], 0.0).then_inc(diag_zeroed, 1)
            nc.gpsimd.memset(QD[:], 0.0).then_inc(diag_zeroed, 1)
            for b, (n, c0) in enumerate(rw_blocks):
                for l in range(levels_of[b]):
                    for g in range(2):
                        if l == 0:
                            pool.wait_ge(am_ready, 8 * b + 4 * g + 4)
                        step = level0[b] + l
                        if step >= 2:
                            pool.wait_ge(x_ready[g], step - 1)
                        nc.gpsimd.tensor_tensor(
                            MM[0:n, step % 2, 4 * g:4 * g + 4, 0:n], AM[0:n, 4 * g:4 * g + 4, 2, 0:n],
                            C("levels", P * l, P * l + n, n).unsqueeze(1).broadcast_to([n, 4, n]),
                            ALU.mult).then_inc(m_ready[g], 1)
            jobno = [len(PHASE_C)]

            def jobs(k):
                for _ in range(k):
                    low(UNIT_NO[units_of(JOBS[jobno[0]])[0]] + W_SLOTS)
                    jobno[0] += 1

            run_after_rw("pool", jobs, {
                "sb_prep": sb_prep, "sb_mask": sb_mask, "sb_amask": sb_amask,
                "ret_prep": ret_prep, "sb_values": sb_values})
            low(NUNITS)

        @block.scalar
        def _(act):
            steps = [0]

            def link(ins):
                ins.then_inc(act_step, 1)
                steps[0] += 1
                act.wait_ge(act_step, steps[0])

            units = [0]

            def high(upto_unit):
                while units[0] < min(upto_unit, NUNITS):
                    u = units[0]
                    act.wait_ge(raw_in[u % RAW_SLOTS], 16 * (u // RAW_SLOTS + 1))
                    if u >= W_SLOTS:
                        act.wait_ge(dense_done, LAST_JOB[u - W_SLOTS] + 1)
                    nc.scalar.activation(w_hi[:, u % W_SLOTS, :], raw[:, u % RAW_SLOTS, :], ACT.Copy)\
                        .then_inc(hi_ready, 1)
                    units[0] += 1

            def after_job(n):
                high(UNIT_NO[units_of(JOBS[n])[0]] + W_SLOTS)

            A = nc.scalar.activation
            nc.scalar.preload_act_table_set("natural_log_exp_and_others")
            act.wait_ge(x_in, 32)
            for b in range(NB):
                A(sq0[:], xt[:, b, :], ACT.Square, accum_out=ss0[:, b:b + 1]).then_inc(ss_ready, 1)
                act.wait_ge(ss_ready, b + 1)
            A(sq0[0:MB, :], xm[:], ACT.Square, accum_out=ss0[0:MB, NB:NB + 1]).then_inc(ss_ready, 1)
            act.wait_ge(ss_ready, NB + 1)
            for r, cc in ((P, slice(0, NB)), (MB, slice(NB, NB + 1))):
                link(A(rs0[0:r, cc], ss0[0:r, cc], ACT.Ln, scale=1.0 / D, bias=EPS))
                A(rs0[0:r, cc], rs0[0:r, cc], ACT.Exp, scale=-0.5).then_inc(rs_ready, 1)
            high(RAW_SLOTS)
            act.wait_ge(const_in, 48)
            for k in range(KD):
                act.wait_ge(ht_done, k + 1)
                A(h_hi[:, k, MB:L], pst[:, k % 4, :], ACT.Copy, scale=PAR("norm1_g", k)).then_inc(hhi_ready, 1)
                A(h_hi[:, k, 0:MB], pst[:, 4 + k % 4, 0:MB], ACT.Copy, scale=PAR("norm1_g", k)).then_inc(hhi_ready, 1)

            nc.scalar.preload_act_table_set("exp_and_others")
            act.wait_ge(cbuf_zeroed, 1)

            def c_copy(i):
                n = JOBN[PHASE_C[i]]
                act.wait_ge(dense_done, n + 1)
                if i >= 3:
                    act.wait_ge(c_mixed, i - 2)
                A(halves(cbuf[:, i % 3, 1:L + 1]), pair(job_slot(n)), ACT.Copy).then_inc(c_copied, 1)
                after_job(n)

            c_copy(0)
            c_copy(1)
            act.wait_ge(c_mixed, 1)
            A(WA[0:HD, :], WA[0:HD, :], ACT.Tanh).then_inc(wa_tanh, 1)
            act.wait_ge(c_mixed, 2)
            A(SG[:], SG[:], ACT.Tanh, scale=0.5).then_inc(sg_tanh, 1)
            act.wait_ge(par_ready, 3)
            for t in range(4):
                for i in range(3):
                    c_copy(2 + 3 * t + i)
                act.wait_ge(lora_done, 2 * t + 1)
                if t >= 1:
                    act.wait_ge(rw_elem, t)
                A(halves(tt["LAM"][:]), pst[:, 4:6, 0:HL], ACT.Tanh, scale=0.5, bias=half_wa[:, t:t + 1])\
                    .then_inc(lora_act, 1)
                act.wait_ge(lora_done, 2 * t + 2)
                A(halves(tt["AA"][:]), pst[:, 6:8, 0:HL], ACT.Tanh, scale=0.5, bias=half_wa[:, 4 + t:5 + t])\
                    .then_inc(lora_act, 1)
                nc.scalar.preload_act_table_set("natural_log_exp_and_others")
                act.wait_ge(kkr_ready, t + 1)
                A(tt["SQ"][:], tt["KKR"][:], ACT.Square).then_inc(kksq_ready, 1)
                act.wait_ge(lg_ready, t + 1)
                A(tt["E1"][:], tt["LG"][:], ACT.Exp).then_inc(e_ready, 1)
                A(tt["E2"][:], tt["LGX"][:], ACT.Exp).then_inc(e_ready, 1)
                A(tt["E3"][:], tt["LG"][:], ACT.Exp, scale=-1.0).then_inc(e_ready, 1)
                act.wait_ge(kkclamped, t + 1)
                link(A(tt["RN"][:], tt["RN"][:], ACT.Ln, scale=2.0 ** 20))
                A(tt["RN"][:], tt["RN"][:], ACT.Exp, scale=-0.5, bias=float(10 * np.log(2.0))).then_inc(rn_ready, 1)
                if t < 3:
                    nc.scalar.preload_act_table_set("exp_and_others")

            for b, (n, c0) in enumerate(rw_blocks):
                act.wait_ge(tok_done, 4 * b + 1)
                if b == 0:
                    act.wait_ge(rw_elem, 4)
                A(FK[0:n, :, 0, :], pst[0:n, 0, :].rearrange("p (h d) -> p h d", h=RWH), ACT.Copy).then_inc(tok_act, 1)
                act.wait_ge(tok_done, 4 * b + 2)
                A(VT[0:n, :], pst[0:n, 1, :], ACT.Copy).then_inc(tok_act, 1)
                for l in range(1, levels_of[b]):
                    for g in range(2):
                        s = level0[b] + l - b
                        act.wait_ge(c1_done[g], level0[b] + l + 1)
                        A(C1[0:n, 4 * g:4 * g + 4, 0:n], pst[0:n, 4 * g + 1, 0:4 * n].rearrange("p (h d) -> p h d", h=4),
                          ACT.Copy).then_inc(c1_copied[g], 1)
                for g in range(2):
                    act.wait_ge(f_done, 2 * b + g + 1)
                    A(FK[0:n, 4 * g:4 * g + 4, 1, :], pst[0:n, 4 * g, 0:256].rearrange("p (h d) -> p h d", h=4),
                      ACT.Copy).then_inc(f_copied, 1)
                if b == 0:
                    continue
                for ci in range(2):
                    c = 2 * b - 1 + ci
                    act.wait_ge(q_ready, c)
                    if b == 1 and ci == 0:
                        act.wait_ge(diag_zeroed, 2)
                    if b >= 2:
                        act.wait_ge(yy_done, 2 * (b - 1))
                    for hf in range(2):
                        r = slice(HD * hf, HD * hf + HD)
                        A(QD[r, ci, :, HD * hf:HD * hf + HD], QQ[r, :, :], ACT.Copy).then_inc(qd_ready, 1)
                for g in range(2):
                    act.wait_ge(yy_done, 2 * (b - 1) + g + 1)
                    A(KR[:, 2 * g:2 * g + 2, 0, c0:c0 + n],
                      pst[:, 4 * g + 2, 0:2 * n].rearrange("p (h d) -> p h d", h=2), ACT.Copy).then_inc(yy_copied, 1)
            for t in range(4):
                s = t % 2
                act.wait_ge(postc_ready, t + 1)
                A(post["sq"][:, s, :], KR[:, t, 0, MB:L], ACT.Square).then_inc(postq_ready, 1)
                act.wait_ge(postv_done, t + 1)
                if t >= 2:
                    act.wait_ge(yf_ready, t - 1)
                link(A(post["rs"][:, s, :], pst[:, 4 * s + 1, :], ACT.Ln, scale=1.0 / HD, bias=RW_LN_EPS))
                A(post["rs"][:, s, :], post["rs"][:, s, :], ACT.Exp, scale=-0.5).then_inc(postr_ready, 1)
                act.wait_ge(yf_ready, t + 1)
                A(y_hi[:, t, :], KR[:, t, 0, MB:L], ACT.Copy).then_inc(yh_ready, 1)

            jobno = [len(PHASE_C)]

            def jobs(k):
                for _ in range(k):
                    job(jobno[0])
                    jobno[0] += 1

            def job(n):
                kind, a, b = JOBS[n]
                s = job_slot(n)
                one, two = pst[:, 2 * s, :], pair(s)
                if kind in ("aq", "ak", "bq", "bk", "bg", "dq", "dk", "gate", "up"):
                    act.wait_ge(dense_done, n + 1)
                if kind in ("aq", "ak") and (a, kind) == (0, "aq"):
                    act.wait_ge(yl_ready, 4)
                if (a, kind) == (0, "bq"):
                    act.wait_ge(yl_ready, 8)
                if (a, kind) == (0, "dq"):
                    act.wait_ge(yl_ready, 12)
                if kind == "aq":
                    A(sb_q[:, a, :], one, ACT.Copy, scale=float(HD) ** -0.5).then_inc(job_out[kind], 1)
                elif kind == "ak":
                    A(halves(sb_k[:, a, :]), two, ACT.Copy).then_inc(job_out[kind], 1)
                elif kind == "bq":
                    A(rq[:, a, :], one, ACT.Copy).then_inc(job_out[kind], 1)
                elif kind == "bk":
                    A(halves(rk[:, a, :]), two, ACT.Copy).then_inc(job_out[kind], 1)
                elif kind == "bg":
                    A(rg[:, a, :], one, ACT.Copy).then_inc(job_out[kind], 1)
                elif kind == "dq":
                    A(dq[:, a, :], one, ACT.Copy).then_inc(job_out[kind], 1)
                elif kind == "dk":
                    A(halves(dk[:]), two, ACT.Copy).then_inc(job_out[kind], 1)
                elif kind == "gate":
                    i = kind_no(n)
                    if i >= 4:
                        act.wait_ge(job_out["proj"], i - 3)
                    A(gate_t[:, b % 4, :], one, ACT.Copy).then_inc(job_out[kind], 1)
                    if b % 4 == 3:
                        nc.scalar.preload_act_table_set("exp_and_others")
                        act.wait_ge(job_out[kind], i + 1)
                        A(gate_t[:], gate_t[:], ACT.Tanh, scale=0.5).then_inc(gate_tanh, 1)
                        nc.scalar.preload_act_table_set("natural_log_exp_and_others")
                elif kind == "up":
                    i = kind_no(n)
                    if i >= 2:
                        act.wait_ge(u_lo_ready, i - 1)
                    A(ub[:, i % 2, :], one, ACT.Relu).then_inc(job_out[kind], 1)
                    act.wait_ge(job_out[kind], i + 1)
                    if a == 1 and b == 0:
                        act.wait_ge(dense_done, n)
                    A(u_hi[:, b, :], ub[:, i % 2, :], ACT.Square).then_inc(u_hi_ready, 1)
                after_job(n)

            def sb_meta(grp):
                act.wait_ge(zm_done, grp + 1)
                link(A(sb_em[:], pst[:, 7, :], ACT.Abs))
                link(A(sb_em[:], sb_em[:], ACT.Exp, scale=-1.0))
                A(sb_em[:], sb_em[:], ACT.Ln, bias=1.0).then_inc(zm_ln, 1)

            def sb_pieces(tile):
                return tile[:, 0, :], tile[:, 1:3, 0:3 * P]

            def sb_z(h):
                act.wait_ge(z_done, h + 1)
                if h:
                    act.wait_ge(sb_used, h)
                e0, e1 = sb_pieces(sb_e)
                A(e0, pst[:, 4, :], ACT.Abs)
                link(A(e1, pst[:, 5:7, 0:3 * P], ACT.Abs))
                A(e0, e0, ACT.Exp, scale=-1.0)
                link(A(e1, e1, ACT.Exp, scale=-1.0))
                A(e0, e0, ACT.Ln, bias=1.0)
                A(e1, e1, ACT.Ln, bias=1.0).then_inc(z_ln, 1)

            def sb_arg(h):
                act.wait_ge(z_arg, h + 1)
                e0, e1 = sb_pieces(sb_e)
                A(e0, pst[:, 4, :], ACT.Exp)
                A(e1, pst[:, 5:7, 0:3 * P], ACT.Exp).then_inc(z_a, 1)

            def sb_end(grp):
                act.wait_ge(zm_arg, grp + 1)
                A(sb_em[:], pst[:, 7, :], ACT.Exp).then_inc(zm_a, 1)
                for t in (2 * grp, 2 * grp + 1):
                    act.wait_ge(o_done, t + 1)
                    if t == 0:
                        act.wait_ge(dense_done, y_free(BRANCH_SB))
                    A(y_hi[:, t, :], pst[:, 1 + 2 * (t % 2), :], ACT.Copy).then_inc(yh_ready, 1)

            def ret_gate():
                nc.scalar.preload_act_table_set("exp_and_others")
                act.wait_ge(job_out["bg"], 4)
                A(rth[:], rg[:], ACT.Tanh, scale=0.5).then_inc(rg_tanh, 1)
                nc.scalar.preload_act_table_set("natural_log_exp_and_others")

            def ret_block(b):
                if b:
                    act.wait_ge(ro_done, b)
                    A(ro[:, :, P * (b - 1):P * b], pst[:, 3 + 4 * (b % 2), :].rearrange("p (h i) -> p h i", h=RETH),
                      ACT.Copy).then_inc(ro_ready, 1)

            def ret_post():
                act.wait_ge(ro_ready, NB)
                for h in range(RETH):
                    if h >= 2:
                        act.wait_ge(ry_ready, h - 1)
                    A(rsq[:, h % 2, :], ro[:, h, :], ACT.Square).then_inc(rsq_ready, 1)
                    act.wait_ge(rss_done, h + 1)
                    link(A(rsq[:, h % 2, :], pst[:, 4 + h % 2, :], ACT.Ln, scale=-1.0 / P, bias=EPS))
                    A(rsq[:, h % 2, :], rsq[:, h % 2, :], ACT.Exp, scale=-0.5).then_inc(rrs_ready, 1)
                    act.wait_ge(ry_ready, h + 1)
                    if h == 0:
                        act.wait_ge(dense_done, y_free(BRANCH_RET))
                    A(y_hi[:, h, :], ro[:, h, :], ACT.Copy).then_inc(yh_ready, 1)

            def sw_norm():
                for t in range(5):
                    n = T if t < 4 else L
                    src = dq[:, t, :] if t < 4 else dk[:]
                    act.wait_ge(*(all_out("dq", ("dq", t, 0)) if t < 4 else all_out("dk", ("dk", 0, 0))))
                    sq = dsq[:, t % 2, 0:n]
                    if t >= 2:
                        act.wait_ge(dn_ready, t - 1)
                    A(sq, src, ACT.Square).then_inc(dsq_ready, 1)
                    act.wait_ge(dss_done, t + 1)
                    ps = pst[:, 4 + t % 2, :] if t < 4 else pst[:, 6:8, 0:HL]
                    sq_ = sq if t < 4 else halves(sq)
                    link(A(sq_, ps, ACT.Ln, scale=1.0 / HD, bias=EPS))
                    A(sq, sq, ACT.Exp, scale=-0.5).then_inc(drs_ready, 1)
                act.wait_ge(dn_ready, 5)
                for kv in range(2):
                    own, other = slice(HD * kv, HD * kv + HD), slice(HD - HD * kv, P - HD * kv)
                    act.dma_start(dk2[other, kv, :], dk[own, :]).then_inc(dk2_in, 16)

            def sw_probs(b, kv):
                i = 2 * b + kv
                st = dst_[:, i % 2]
                act.wait_ge(dmx_ready, i + 1)
                A(st[:, 2, :], st[:, 2, :], ACT.Exp).then_inc(dexp_ready, 1)
                w = MB + (2 * P if b else P)
                for j in range(4):
                    A(dsc[:, i % 2, j, 0:w], dsc[:, i % 2, j, 0:w], ACT.Exp, bias=st[:, 0, j:j + 1],
                      accum_out=st[:, 1, j:j + 1]).then_inc(dexp_ready, 1)

            def sw_out(b, kv):
                i = 2 * b + kv
                act.wait_ge(dpt_done, i + 1)
                A(dpt[:, i % 2, 0, :], pst[:, 1, :], ACT.Copy).then_inc(dpt_act, 1)
                act.wait_ge(do_done, i + 1)
                if i == 0:
                    act.wait_ge(dense_done, y_free(BRANCH_SW))
                A(y_hi[:, 2 * kv:2 * kv + 2, P * b:P * b + P], pst[:, 6, 0:2 * P].rearrange("p (t q) -> p t q", t=2),
                  ACT.Copy).then_inc(yh_ready, 1)

            def merge_split():
                act.wait_ge(dense_done, JOB_NO[("gate", BRANCH_SW, KD - 1)] + 1)
                for k in range(KD):
                    act.wait_ge(merged_ready, 2 * KD + k + 1)
                    A(h_hi[:, k, 0:T], merged[:, k, :], ACT.Copy, scale=0.5).then_inc(m_hi, 1)
                act.wait_ge(yl_ready, y_count(BRANCH_SW) + 8)
                act.dma_start(x2[:], x[0].rearrange("(b p) d -> p b d", p=P)).then_inc(x2_in, 16)

            def norm2():
                act.wait_ge(m_lo, KD)
                for b in range(NB):
                    act.wait_ge(*all_out("wo", ("wo", 3, b)))
                    A(h2n[:, b, :], x2[:, b, :], ACT.Square, accum_out=ss2[:, 0, b:b + 1]).then_inc(ss2_ready, 1)
                act.wait_ge(ss2_ready, NB)
                link(A(ss2[:, 1, :], ss2[:, 0, :], ACT.Ln, scale=1.0 / D, bias=EPS))
                A(ss2[:, 1, :], ss2[:, 1, :], ACT.Exp, scale=-0.5).then_inc(rs2_ready, 1)
                for k in range(KD):
                    act.wait_ge(h2t_done, k + 1)
                    A(h_hi[:, k, 0:T], pst[:, 4 + k % 4, :], ACT.Copy, scale=PAR("norm2_g", k)).then_inc(h2hi_ready, 1)

            run_after_rw("act", jobs, dict(
                sb_meta=sb_meta, sb_z=sb_z, sb_arg=sb_arg, sb_end=sb_end, ret_gate=ret_gate, ret_block=ret_block,
                ret_post=ret_post, sw_norm=sw_norm, sw_probs=sw_probs, sw_out=sw_out, merge_split=merge_split,
                norm2=norm2))

        @block.vector
        def _(dve):
            steps = [0]

            def link(ins):
                ins.then_inc(dve_step, 1)
                steps[0] += 1
                dve.wait_ge(dve_step, steps[0])

            V = nc.vector
            for b in range(NB + 1):
                r = P if b < NB else MB
                src = xt[:, b, :] if b < NB else xm[:]
                dve.wait_ge(rs_ready, 1 if b < NB else 2)
                V.tensor_scalar(src, src, rs0[0:r, b:b + 1], None, ALU.mult).then_inc(hn_ready, 1)
            dve.wait_ge(const_in, 48)
            a, _ = PARAM_AT["rw_w0"]
            V.tensor_scalar(half_wa[:], par[:, a:a + 8], 0.5, None, ALU.mult).then_inc(par_ready, 1)
            a, _ = PARAM_AT["rw_ka"]
            V.tensor_scalar(one_minus_ka[:], par[:, a:a + 4], -1.0, 1.0, ALU.mult, ALU.add).then_inc(par_ready, 1)
            V.tensor_scalar(gain_q[:], PAR("qn", 0), float(HD) ** -0.5, None, ALU.mult).then_inc(par_ready, 1)
            for k in range(KD):
                dve.wait_ge(hhi_ready, 2 * k + 2)
                V.scalar_tensor_tensor(out=h_lo[:, k, MB:L], in0=pst[:, k % 4, :], scalar=PAR("norm1_g", k),
                                       in1=h_hi[:, k, MB:L].bitcast(F32), op0=ALU.mult, op1=ALU.subtract)\
                    .then_inc(hlo_ready, 1)
                V.scalar_tensor_tensor(out=h_lo[:, k, 0:MB], in0=pst[:, 4 + k % 4, 0:MB], scalar=PAR("norm1_g", k),
                                       in1=h_hi[:, k, 0:MB].bitcast(F32), op0=ALU.mult, op1=ALU.subtract)\
                    .then_inc(hlo_ready, 1)
            dve.wait_ge(ht_done, KD)
            V.memset(cbuf[:, :, 0:1], 0.0).then_inc(cbuf_zeroed, 1)

            def c_mix(i, dst):
                dve.wait_ge(c_copied, i + 1)
                cur = cbuf[:, i % 3, 1:L + 1]
                link(V.tensor_tensor(cdif[:], cbuf[:, i % 3, 0:L], cur, ALU.subtract))
                V.scalar_tensor_tensor(out=dst, in0=cdif[:], scalar=PAR("rw_mu", PHASE_C[i][1]), in1=cur,
                                       op0=ALU.mult, op1=ALU.add).then_inc(c_mixed, 1)
                dve.wait_ge(c_mixed, i + 1)

            c_mix(0, WA[:])
            c_mix(1, SG[:])
            dve.wait_ge(sg_tanh, 1)
            V.tensor_scalar(SG[:], SG[:], 1.0, 0.5, ALU.add, ALU.mult).then_inc(sg_ready, 1)
            for t in range(4):
                LAM, AA, LG, LGX, KKR, T1, SQ, RN, BB, E1, E2, E3 = (tt[k][:] for k in tmp_names)
                kt, rt = KH[:, t, :], KR[:, t, 1, :]
                c_mix(2 + 3 * t, kt)
                V.tensor_scalar(KKR, kt, PAR("rw_kk", t), None, ALU.mult).then_inc(kkr_ready, 1)
                c_mix(3 + 3 * t, rt)
                c_mix(4 + 3 * t, RV[:, t, :])
                dve.wait_ge(lora_act, 2 * t + 1)
                link(V.tensor_scalar(LAM, LAM, 1.0, -0.5 * float(np.exp(-0.5)), ALU.add, ALU.mult))
                link(V.tensor_tensor_scan(LG, C("scan_keep"), LAM, 0.0, ALU.mult, ALU.add))
                V.tensor_tensor(LGX, LG, LAM, ALU.subtract).then_inc(lg_ready, 1)
                dve.wait_ge(lora_act, 2 * t + 2)
                link(V.tensor_scalar(AA, AA, 1.0, 0.5, ALU.add, ALU.mult))
                link(V.tensor_scalar(T1, AA, PAR("rw_ka", t), one_minus_ka[:, t:t + 1], ALU.mult, ALU.add))
                link(V.tensor_tensor(kt, kt, T1, ALU.mult))
                V.scalar_tensor_tensor(out=BON[:, t, :], in0=rt, scalar=PAR("rw_rk", t), in1=kt,
                                       op0=ALU.mult, op1=ALU.mult)
                dve.wait_ge(kksum_done, t + 1)
                V.tensor_scalar(halves(RN), pst[:, 4:6, 0:HL], 1e-24, None, ALU.max).then_inc(kkclamped, 1)
                dve.wait_ge(e_ready, 3 * t + 3)
                V.tensor_copy(GC[:, t, 0:1], E1[:, MB - 1:MB])
                V.tensor_copy(GC[:, t, 1:NCHUNK], E1[:, MB:L].rearrange("p (c s) -> p c s", s=CH)[:, :, CH - 1])
                V.tensor_tensor(kt, kt, E3, ALU.mult)
                link(V.tensor_tensor(rt, rt, E1, ALU.mult))
                dve.wait_ge(rn_ready, t + 1)
                link(V.tensor_tensor(KKR, KKR, RN, ALU.mult))
                link(V.scalar_tensor_tensor(out=BB, in0=KKR, scalar=-1.0, in1=AA, op0=ALU.mult, op1=ALU.mult))
                V.tensor_tensor(KR[:, t, 0, :], KKR, E2, ALU.mult)
                V.tensor_tensor(BH[:, t, :], BB, E3, ALU.mult).then_inc(rw_elem, 1)

            for b, (n, c0) in enumerate(rw_blocks):
                if b == 0:
                    dve.wait_ge(rw_elem, 4)
                dve.wait_ge(tok_done, 4 * b + 3)
                V.tensor_copy(KT[0:n, :], pst[0:n, 2, :]).then_inc(tok_dve, 1)
                dve.wait_ge(tok_done, 4 * b + 4)
                V.tensor_copy(BT[0:n, :], pst[0:n, 3, :]).then_inc(tok_dve, 1)
                for h in range(RWH):
                    dve.wait_ge(am_done, 8 * b + h + 1)
                    V.tensor_tensor(
                        AM[0:n, h, :, 0:n].rearrange("p (a b) c -> p a b c", a=2),
                        pst[0:n, h, 0:4 * n].rearrange("p (a b c) -> p a b c", a=2, b=2),
                        C("rw_mask", rows=n).rearrange("p (b c) -> p b c", b=2)[:, :, 0:n].unsqueeze(1)
                        .broadcast_to([n, 2, 2, n]), ALU.mult).then_inc(am_ready, 1)
                idb = cst[0:n, 0:n].unsqueeze(1).broadcast_to([n, 4, n])
                for l in range(levels_of[b]):
                    for g in range(2):
                        hs = slice(4 * g, 4 * g + 4)
                        step = level0[b] + l
                        if l == 0:
                            dve.wait_ge(m_ready[g], step + 1)
                            V.tensor_tensor(XX[0:n, hs, 0:n], MM[0:n, step % 2, hs, 0:n], idb, ALU.add)
                            dve.wait_ge(c1_done[g], step + 1)
                            V.tensor_tensor(TT[0:n, hs, 0:n],
                                            pst[0:n, 4 * g + 1, 0:4 * n].rearrange("p (h d) -> p h d", h=4),
                                            idb, ALU.add).then_inc(x_ready[g], 1)
                            dve.wait_ge(x_ready[g], step + 1)
                            continue
                        dve.wait_ge(tu_done[g], step - b)
                        if l < levels_of[b] - 1:
                            V.tensor_tensor(TT[0:n, hs, 0:n], TT[0:n, hs, 0:n],
                                            pst[0:n, 4 * g + 2, 0:4 * n].rearrange("p (h d) -> p h d", h=4), ALU.add)
                        V.tensor_tensor(XX[0:n, hs, 0:n], XX[0:n, hs, 0:n],
                                        pst[0:n, 4 * g + 3, 0:4 * n].rearrange("p (h d) -> p h d", h=4),
                                        ALU.add).then_inc(x_ready[g], 1)
                        dve.wait_ge(x_ready[g], step + 1)
                for g in range(2):
                    dve.wait_ge(wz_done, 2 * b + g + 1)
                    V.tensor_copy(FK[0:n, 4 * g:4 * g + 4, :, :],
                                  pst[0:n, 4 * g + 1, :].rearrange("p (h a d) -> p h a d", h=4, a=2)).then_inc(wz_ready, 1)
                if b >= 1:
                    for g in range(2):
                        dve.wait_ge(rt_done, 2 * (b - 1) + g + 1)
                        rr = KR[:, 2 * g:2 * g + 2, 1, c0:c0 + n]
                        V.tensor_tensor(rr, rr, pst[:, 4 * g + 2, 0:2 * n].rearrange("p (h d) -> p h d", h=2),
                                        ALU.add).then_inc(rt_ready, 1)
                for g in range(2):
                    ts = slice(2 * g, 2 * g + 2)
                    for ci in range(2 if b else 1):
                        c = 2 * b - 1 + ci if b else 0
                        bank = 4 * g + 3 * ci
                        dve.wait_ge(mn_done, (1 + 2 * g + ci + 4 * (b - 1) + 2) if b else g + 1)
                        gcb = GC[:, ts, c:c + 1].broadcast_to([P, 2, HD])
                        nps = pst[:, bank, 128:256].rearrange("p (h d) -> p h d", h=2)
                        if b == 0:
                            V.tensor_tensor(QQ[:, ts, :], nps, gcb, ALU.mult).then_inc(q_ready if g else mn_ready, 1)
                            continue
                        for hf in range(2):
                            r = slice(HD * hf, HD * hf + HD)
                            V.tensor_tensor(MD[r, ci, ts, HD * hf:HD * hf + HD],
                                            pst[r, bank, 0:128].rearrange("p (h d) -> p h d", h=2),
                                            cst[r, HD * hf:HD * hf + HD].unsqueeze(1).broadcast_to([HD, 2, HD]), ALU.add)
                        V.tensor_tensor(NG[:, ci, ts, :], nps, gcb, ALU.mult).then_inc(mn_ready, 1)
                if b == 0:
                    dve.wait_ge(q_ready, 1)
                    dve.wait_ge(diag_zeroed, 2)
                    continue
                for ci in range(2):
                    c = 2 * b - 1 + ci
                    if c == NCHUNK - 1:
                        continue
                    dve.wait_ge(qn_done, c)
                    dve.wait_ge(qd_ready, 2 * c)
                    dve.wait_ge(mn_ready, 1 + 4 * b)
                    link(V.tensor_tensor(QQ[:], pst[:, 1 + 4 * ci, 0:256].rearrange("p (h d) -> p h d", h=4),
                                         GC[:, :, c:c + 1].broadcast_to([P, 4, HD]), ALU.mult))
                    V.tensor_tensor(QQ[:], QQ[:], NG[:, ci], ALU.add).then_inc(q_ready, 1)
                    dve.wait_ge(q_ready, c + 1)
            for t in range(4):
                s = t % 2
                y = KR[:, t, 0, MB:L]
                dve.wait_ge(post_done, 3 * t + 1)
                V.scalar_tensor_tensor(out=y, in0=pst[:, 4 * s, :], scalar=-1.0 / HD, in1=y, op0=ALU.mult,
                                       op1=ALU.add).then_inc(postc_ready, 1)
                dve.wait_ge(post_done, 3 * t + 2)
                V.tensor_tensor(post["bon"][:, s, :], pst[:, 4 * s + 2, :], RV[:, t, MB:L], ALU.mult)
                dve.wait_ge(postr_ready, t + 1)
                link(V.tensor_tensor(y, y, post["rs"][:, s, :], ALU.mult))
                link(V.tensor_scalar(y, y, PAR("rw_ln_g", t), PAR("rw_ln_b", t), ALU.mult, ALU.add))
                link(V.tensor_tensor(y, y, post["bon"][:, s, :], ALU.add))
                dve.wait_ge(post_done, 3 * t + 3)
                V.tensor_tensor(y, y, pst[:, 4 * s + 3, :], ALU.mult).then_inc(yf_ready, 1)
                dve.wait_ge(yh_ready, t + 1)
                V.tensor_tensor(y_lo[:, t, :], y, y_hi[:, t, :].bitcast(F32), ALU.subtract).then_inc(yl_ready, 1)

            jobno = [len(PHASE_C)]

            def jobs(k):
                for _ in range(k):
                    job(jobno[0])
                    jobno[0] += 1

            def job(n):
                kind, a, b = JOBS[n]
                s = job_slot(n)
                one = pst[:, 2 * s, :]
                if kind in ("av", "bv", "dv", "proj", "wo"):
                    dve.wait_ge(dense_done, n + 1)
                if kind in ("av", "bv"):
                    if b == 0:
                        if kind == "bv":
                            dve.wait_ge(yl_ready, 8)
                        dst = (sb_vm if kind == "av" else rvm)[:, 2 * P * a:2 * P * a + 2 * P]
                        V.tensor_copy(dst, pst[0:MB, 2 * s, 0:2 * P]).then_inc(job_out[kind], 1)
                    else:
                        dst = (sb_v if kind == "av" else rv)[:, b - 1, 2 * P * a:2 * P * a + 2 * P]
                        V.tensor_copy(dst, pst[:, 2 * s, 0:2 * P]).then_inc(job_out[kind], 1)
                elif kind == "dv":
                    if b == 0:
                        V.tensor_copy(dvm[:], pst[0:MB, 2 * s, 0:P]).then_inc(job_out[kind], 1)
                    else:
                        V.tensor_copy(dv[:, b - 1, :], pst[:, 2 * s, 0:P]).then_inc(job_out[kind], 1)
                elif kind == "proj":
                    dve.wait_ge(gate_tanh, kind_no(n) // 4 + 1)
                    if a == br_order[0]:
                        V.scalar_tensor_tensor(out=merged[:, b, :], in0=gate_t[:, b % 4, :], scalar=1.0, in1=one,
                                               op0=ALU.add, op1=ALU.mult).then_inc(job_out[kind], 1)
                    else:
                        V.scalar_tensor_tensor(out=gtmp[:, b % 2, :], in0=gate_t[:, b % 4, :], scalar=1.0, in1=one,
                                               op0=ALU.add, op1=ALU.mult).then_inc(job_out[kind], 1)
                        dve.wait_ge(job_out[kind], kind_no(n) + 1)
                        V.tensor_tensor(merged[:, b, :], merged[:, b, :], gtmp[:, b % 2, :], ALU.add)\
                            .then_inc(merged_ready, 1)
                elif kind == "wo":
                    dve.wait_ge(x2_in, 16)
                    dst = x2[:, b, 2 * P * a:2 * P * a + 2 * P]
                    V.tensor_tensor(dst, pst[:, 2 * s, 0:2 * P], dst, ALU.add).then_inc(job_out[kind], 1)
                elif kind == "up":
                    i = kind_no(n)
                    r, q = ub[:, i % 2, :], usq[:, i % 2, :]
                    dve.wait_ge(job_out[kind], i + 1)
                    link(V.tensor_tensor(q, r, r, ALU.mult))
                    dve.wait_ge(u_hi_ready, i + 1)
                    V.tensor_tensor(u_lo[:, b, :], q, u_hi[:, b, :].bitcast(F32), ALU.subtract).then_inc(u_lo_ready, 1)
                elif kind == "down":
                    c, kk = b
                    if kk == FH // 2 - 1:
                        dve.wait_ge(dense_done, n + 1)
                        for blk in range(NB):
                            dst = x2[:, blk, T * c:T * c + T]
                            V.tensor_tensor(dst, pst[:, down_bank(c, blk), :], dst, ALU.add)\
                                .then_inc(job_out["down"], 1)

            def sb_values():
                dve.wait_ge(sb_diag_zeroed, 1)
                dve.wait_ge(*all_out("ak", ("ak", 3, 0)))
                for h in range(SBH):
                    r = slice(HD * (h % 2), HD * (h % 2) + HD)
                    V.tensor_copy(sb_kmd[r, h // 2, MB * (h % 4):MB * (h % 4) + MB], sb_k[r, h // 2, 0:MB])\
                        .then_inc(sb_kmd_ready, 1)

            def sb_meta(grp):
                dve.wait_ge(zm_ln, grp + 1)
                V.scalar_tensor_tensor(out=sb_sm[:], in0=pst[:, 7, :], scalar=0.0, in1=sb_em[:], op0=ALU.max,
                                       op1=ALU.add).then_inc(zm_sp, 1)

            def sb_z(h):
                dve.wait_ge(z_ln, h + 1)
                V.scalar_tensor_tensor(out=sb_s[:, 0, :], in0=pst[:, 4, :], scalar=0.0, in1=sb_e[:, 0, :],
                                       op0=ALU.max, op1=ALU.add)
                V.scalar_tensor_tensor(out=sb_s[:, 1:3, 0:3 * P], in0=pst[:, 5:7, 0:3 * P], scalar=0.0,
                                       in1=sb_e[:, 1:3, 0:3 * P], op0=ALU.max, op1=ALU.add).then_inc(z_sp, 1)

            def sb_sums(h):
                dve.wait_ge(z_spm, h + 1)
                V.tensor_copy(sb_cs[:, :, 0:P], sb_s[:, :, 0:P])
                link(V.tensor_tensor(sb_cs[:, 2, P:2 * P], sb_s[:, 2, P:2 * P], sb_s[:, 2, 2 * P:3 * P], ALU.add))
                link(V.tensor_tensor(sb_cs[:, 1, P:3 * P], sb_s[:, 1, P:3 * P], sb_cs[:, 2, 0:2 * P], ALU.add))
                V.tensor_tensor(sb_cs[:, 0, P:T], sb_s[:, 0, P:T], sb_cs[:, 1, 0:3 * P], ALU.add).then_inc(z_cs, 1)

            def sb_end(grp):
                for t in (2 * grp, 2 * grp + 1):
                    dve.wait_ge(yh_ready, y_count(BRANCH_SB) + t + 1)
                    V.tensor_tensor(y_lo[:, t, :], pst[:, 1 + 2 * (t % 2), :], y_hi[:, t, :].bitcast(F32),
                                    ALU.subtract).then_inc(yl_ready, 1)

            def ret_gate():
                dve.wait_ge(job_out["bq"], 2)
                for t in range(2):
                    V.tensor_tensor(rqd[:, t, :].rearrange("p (b i) -> p b i", b=NB),
                                    rq[:, t, :].rearrange("p (b i) -> p b i", b=NB),
                                    C("ret_qdec", P * t, P * t + P).unsqueeze(1).broadcast_to([P, NB, P]),
                                    ALU.mult).then_inc(rqd_ready, 1)
                dve.wait_ge(rg_tanh, 1)
                V.scalar_tensor_tensor(out=rg[:], in0=rth[:], scalar=1.0, in1=rg[:], op0=ALU.add, op1=ALU.mult)\
                    .then_inc(rg_ready, 1)

            def ret_block(b):
                n = P if b else MB
                dve.wait_ge(rkt_done, b + 1)
                V.tensor_tensor(rkd[0:n], pst[0:n, 4, 0:2 * P].rearrange("p (h d) -> p h d", h=RETH),
                                C("ret_kdec" if b else "ret_kdec_meta", rows=n).unsqueeze(2).broadcast_to([n, RETH, HD]),
                                ALU.mult).then_inc(rkd_ready, 1)
                if b:
                    dve.wait_ge(rs_done, b)
                    m = C("ret_mask").rearrange("p (h i) -> p h i", h=RETH)
                    for par_ in range(2):
                        V.tensor_tensor(rsc[:, par_:RETH:2, :], pst[:, 5 + par_, 0:2 * P].rearrange("p (h i) -> p h i", h=2),
                                        m[:, par_:RETH:2, :], ALU.mult).then_inc(rsc_ready, 1)
                if b < NB:
                    dve.wait_ge(rkv_done, b + 1)
                    if b == 0:
                        dve.wait_ge(rsz_zeroed, 1)
                    else:
                        dve.wait_ge(ro_done, b)
                    for h in range(RETH):
                        r = slice(HD * (h % 2), HD * (h % 2) + HD)
                        V.scalar_tensor_tensor(out=rsz[r, h, :], in0=rsz[r, h, :], scalar=RET_CHUNK_DECAY[h],
                                               in1=pst[r, 4, 2 * P + P * (h // 2):3 * P + P * (h // 2)],
                                               op0=ALU.mult, op1=ALU.add).then_inc(rstate, 1)
                    dve.wait_ge(rstate, 4 * b + 4)

            def ret_post():
                for h in range(RETH):
                    y = ro[:, h, :]
                    dve.wait_ge(rrs_ready, h + 1)
                    link(V.tensor_tensor(y, y, rsq[:, h % 2, :], ALU.mult))
                    V.scalar_tensor_tensor(out=y, in0=y, scalar=0.5, in1=rg[:, h, :], op0=ALU.mult, op1=ALU.mult)\
                        .then_inc(ry_ready, 1)
                    dve.wait_ge(yh_ready, y_count(BRANCH_RET) + h + 1)
                    V.tensor_tensor(y_lo[:, h, :], y, y_hi[:, h, :].bitcast(F32), ALU.subtract).then_inc(yl_ready, 1)

            def sw_norm():
                dve.wait_ge(par_ready, 3)
                for t in range(5):
                    dve.wait_ge(drs_ready, t + 1)
                    y = dq[:, t, :] if t < 4 else dk[:]
                    V.scalar_tensor_tensor(out=y, in0=y, scalar=gain_q[:] if t < 4 else PAR("kn", 0),
                                           in1=dsq[:, t % 2, 0:T if t < 4 else L], op0=ALU.mult, op1=ALU.mult)\
                        .then_inc(dn_ready, 1)
                dve.wait_ge(dn_ready, 5)
                for kv in range(2):
                    own = slice(HD * kv, HD * kv + HD)
                    V.tensor_copy(dk2[own, kv, :], dk[own, :]).then_inc(dk2_own, 1)

            def sw_scores(b, kv):
                i = 2 * b + kv
                w = MB + (2 * P if b else P)
                st = dst_[:, i % 2]
                if i >= 2:
                    dve.wait_ge(dpt_done, i - 1)
                for j in range(4):
                    h = 4 * kv + j
                    dve.wait_ge(ds_done, 4 * i + j + 1)
                    slope = 2.0 ** (-8.0 * (h + 1) / SWH)
                    if b:
                        V.scalar_tensor_tensor(out=dsc[:, i % 2, j, 0:w], in0=C("sw_bias"), scalar=slope,
                                               in1=pst[:, 4 + j, 0:w], op0=ALU.mult, op1=ALU.add).then_inc(ds_read, 1)
                    else:
                        V.scalar_tensor_tensor(out=dsc[:, i % 2, j, 0:MB], in0=C("sw_bias", 0, MB), scalar=slope,
                                               in1=pst[:, 4 + j, 0:MB], op0=ALU.mult, op1=ALU.add)
                        V.scalar_tensor_tensor(out=dsc[:, i % 2, j, MB:w], in0=C("sw_bias", MB + P, MB + 2 * P),
                                               scalar=slope, in1=pst[:, 4 + j, MB:w], op0=ALU.mult, op1=ALU.add)\
                            .then_inc(ds_read, 1)
                dve.wait_ge(ds_read, 4 * i + 4)
                sink = par[:, PARAM_AT["sink"][0] + 4 * kv:PARAM_AT["sink"][0] + 4 * kv + 4]
                link(V.tensor_reduce(st[:, 0, :], dsc[:, i % 2, :, 0:w], AX.X, ALU.max))
                link(V.tensor_tensor(st[:, 0, :], st[:, 0, :], sink, ALU.max))
                link(V.tensor_scalar(st[:, 0, :], st[:, 0, :], -1.0, None, ALU.mult))
                V.tensor_tensor(st[:, 2, :], st[:, 0, :], sink, ALU.add).then_inc(dmx_ready, 1)

            def sw_probs(b, kv):
                i = 2 * b + kv
                w = MB + (2 * P if b else P)
                st = dst_[:, i % 2]
                dve.wait_ge(dexp_ready, 5 * i + 5)
                link(V.tensor_tensor(st[:, 3, :], st[:, 1, :], st[:, 2, :], ALU.add))
                link(V.reciprocal(st[:, 4, :], st[:, 3, :]))
                V.tensor_tensor(dsc[:, i % 2, :, 0:w], dsc[:, i % 2, :, 0:w],
                                st[:, 4, :].unsqueeze(2).broadcast_to([P, 4, w]), ALU.mult).then_inc(dp_ready, 1)

            def sw_out(b, kv):
                i = 2 * b + kv
                dve.wait_ge(dpt_done, i + 1)
                if b:
                    V.tensor_copy(dpt[:, i % 2, 1, :], pst[:, 3, :])
                V.tensor_copy(dpt[0:MB, i % 2, 2, :], pst[0:MB, 7, :]).then_inc(dpt_dve, 1)
                dve.wait_ge(yh_ready, y_count(BRANCH_SW) + i + 1)
                dst = (slice(None), slice(2 * kv, 2 * kv + 2), slice(P * b, P * b + P))
                V.tensor_tensor(y_lo[dst], pst[:, 6, 0:2 * P].rearrange("p (t q) -> p t q", t=2),
                                y_hi[dst].bitcast(F32), ALU.subtract).then_inc(yl_ready, 1)

            def merge_split():
                for k in range(KD):
                    dve.wait_ge(m_hi, k + 1)
                    dve.wait_ge(merged_ready, 3 * KD)
                    V.scalar_tensor_tensor(out=h_lo[:, k, 0:T], in0=merged[:, k, :], scalar=0.5,
                                           in1=h_hi[:, k, 0:T].bitcast(F32), op0=ALU.mult, op1=ALU.subtract)\
                        .then_inc(m_lo, 1)

            def norm2():
                dve.wait_ge(rs2_ready, 1)
                for b in range(NB):
                    V.tensor_scalar(h2n[:, b, :], x2[:, b, :], ss2[:, 1, b:b + 1], None, ALU.mult).then_inc(h2n_ready, 1)
                for k in range(KD):
                    dve.wait_ge(h2hi_ready, k + 1)
                    V.scalar_tensor_tensor(out=h_lo[:, k, 0:T], in0=pst[:, 4 + k % 4, :], scalar=PAR("norm2_g", k),
                                           in1=h_hi[:, k, 0:T].bitcast(F32), op0=ALU.mult, op1=ALU.subtract)\
                        .then_inc(h2lo_ready, 1)

            run_after_rw("dve", jobs, dict(
                sb_values=sb_values, sb_meta=sb_meta, sb_z=sb_z, sb_sums=sb_sums, sb_end=sb_end,
                ret_gate=ret_gate, ret_block=ret_block, ret_post=ret_post, sw_norm=sw_norm, sw_scores=sw_scores,
                sw_probs=sw_probs, sw_out=sw_out, merge_split=merge_split, norm2=norm2))

        @block.tensor
        def _(pe):
            M = nc.tensor.matmul

            def wslice(tile, u, k):
                return tile[:, u % W_SLOTS, P * k:P * k + P]

            def product3(out, terms):
                for i, ((lh, ll), (rh, rl)) in enumerate(terms):
                    M(out, lh, rh, start=(i == 0), stop=False)
                    M(out, lh, rl, start=False, stop=False)
                    last = M(out, ll, rh, start=False, stop=(i == len(terms) - 1))
                return last

            def job_begin(n):
                s = job_slot(n)
                if n >= 2:
                    pe.wait_ge(*emptied(n - 2))
                pe.wait_ge(lo_ready, UNIT_NO[units_of(JOBS[n])[-1]] + 1)
                return s

            def feature_job(job, cols):
                n = JOBN[job]
                s = job_begin(n)
                u = UNIT_NO[units_of(job)[0]]
                for i, (c0, c1) in enumerate(cols):
                    last = product3(pst[:, 2 * s + i, 0:c1 - c0],
                                    [((wslice(w_hi, u, k), wslice(w_lo, u, k)),
                                      (h_hi[:, k, c0:c1], h_lo[:, k, c0:c1])) for k in range(KD)])
                last.then_inc(dense_done, 1)

            ALL = [(0, HL), (HL, L)]
            pe.wait_ge(const_in, 48)
            pe.wait_ge(hn_ready, NB + 1)
            for k in range(KD):
                if k >= 4:
                    pe.wait_ge(hlo_ready, 2 * (k - 4) + 2)
                nc.tensor.transpose(pst[:, 4 + k % 4, 0:MB], xm[:, P * k:P * k + P], cst[0:MB, 0:MB])
                for b in range(NB):
                    last = nc.tensor.transpose(pst[:, k % 4, P * b:P * b + P], xt[:, b, P * k:P * k + P], ident)
                last.then_inc(ht_done, 1)
            pe.wait_ge(hlo_ready, 2 * KD)

            def lora(t):
                if t == 0:
                    pe.wait_ge(wa_tanh, 1)
                else:
                    pe.wait_ge(kkclamped, t)
                    pe.wait_ge(lora_act, 2 * t)
                for i in range(2):
                    last = M(pst[:, 4 + i, 0:HL], w2[:, P * t:P * t + P], WA[0:HD, HL * i:HL * i + HL],
                             start=True, stop=True)
                last.then_inc(lora_done, 1)
                for i in range(2):
                    last = M(pst[:, 6 + i, 0:HL], a2[:, P * t:P * t + P], WA[HD:P, HL * i:HL * i + HL],
                             start=True, stop=True)
                last.then_inc(lora_done, 1)

            def kksum(t):
                pe.wait_ge(kksq_ready, t + 1)
                pe.wait_ge(lora_act, 2 * t + 1)
                for i in range(2):
                    last = M(pst[:, 4 + i, 0:HL], headsum, tt["SQ"][:, HL * i:HL * i + HL], start=True, stop=True)
                last.then_inc(kksum_done, 1)

            feature_job(PHASE_C[0], ALL)
            feature_job(PHASE_C[1], ALL)
            for t in range(4):
                for i in range(3):
                    feature_job(PHASE_C[2 + 3 * t + i], ALL)
                    if t >= 1 and i == 0:
                        kksum(t - 1)
                lora(t)
            kksum(3)

            pe.wait_ge(rw_elem, 4)
            pe.wait_ge(c_copied, len(PHASE_C))
            for b, (n, c0) in enumerate(rw_blocks):
                toks = slice(c0, c0 + n)
                for q, tile in enumerate((lambda t: KR[:, t, 0, toks], lambda t: RV[:, t, toks],
                                          lambda t: KH[:, t, toks], lambda t: BH[:, t, toks])):
                    if b >= 1:
                        pe.wait_ge(mn_ready, 1 + 4 * (b - 1))
                        pe.wait_ge(q_ready, min(2 * b - 1, NCHUNK - 1))
                        if q == 2 and b >= 2:
                            pe.wait_ge(yy_copied, 2 * (b - 1) - 1)
                    for t in range(4):
                        last = nc.tensor.transpose(pst[0:n, q, P * t:P * t + P], tile(t), ident)
                    last.then_inc(tok_done, 1)
                for h in range(RWH):
                    r = slice(HD * (h % 2), HD * (h % 2) + HD)
                    if h == 0:
                        pe.wait_ge(tok_act, 2 * b + 2)
                    if h == 2:
                        pe.wait_ge(tok_dve, 2 * b + 2)
                    if h == 4 and b >= 2:
                        pe.wait_ge(yy_copied, 2 * (b - 1))
                    rhs = KR[r, h // 2, :, toks]
                    M(pst[0:n, h, 0:2 * n].rearrange("p (a c) -> p a c", a=2), KH[r, h // 2, toks], rhs,
                      start=True, stop=True)
                    M(pst[0:n, h, 2 * n:4 * n].rearrange("p (a c) -> p a c", a=2), BH[r, h // 2, toks], rhs,
                      start=True, stop=True).then_inc(am_done, 1)
                for l in range(levels_of[b]):
                    step = level0[b] + l
                    for g in range(2):
                        pe.wait_ge(m_ready[g], step + 1)
                        if l:
                            pe.wait_ge(x_ready[g], step)
                        for h in range(4):
                            last = M(pst[0:n, 4 * g + 1, n * h:n * h + n], MM[0:n, step % 2, 4 * g + h, 0:n],
                                     TT[0:n, 4 * g + h, 0:n] if l else cst[0:n, 0:n], start=True, stop=True)
                        last.then_inc(c1_done[g], 1)
                    if l == 0:
                        continue
                    for g in range(2):
                        pe.wait_ge(c1_copied[g], step - b)
                        for h in range(4):
                            hh = 4 * g + h
                            if l < levels_of[b] - 1:
                                M(pst[0:n, 4 * g + 2, n * h:n * h + n], XX[0:n, hh, 0:n], C1[0:n, hh, 0:n],
                                  start=True, stop=True)
                        for h in range(4):
                            hh = 4 * g + h
                            last = M(pst[0:n, 4 * g + 3, n * h:n * h + n], C1[0:n, hh, 0:n], XX[0:n, hh, 0:n],
                                     start=True, stop=True)
                        last.then_inc(tu_done[g], 1)
                for g in range(2):
                    for h in range(4 * g, 4 * g + 4):
                        last = M(pst[0:n, 4 * g, HD * (h % 4):HD * (h % 4) + HD], AM[0:n, h, 0, 0:n],
                                 VT[0:n, HD * h:HD * h + HD], start=True, stop=True)
                    last.then_inc(f_done, 1)
                for g in range(2):
                    pe.wait_ge(f_copied, 2 * b + g + 1)
                    pe.wait_ge(x_ready[g], level0[b] + levels_of[b])
                    for h in range(4 * g, 4 * g + 4):
                        last = M(pst[0:n, 4 * g + 1, P * (h % 4):P * (h % 4) + P].rearrange("p (a d) -> p a d", a=2),
                                 XX[0:n, h, 0:n], FK[0:n, h, :, :], start=True, stop=True)
                    last.then_inc(wz_done, 1)
                for g in range(2):
                    pe.wait_ge(wz_ready, 2 * b + g + 1)
                    if b == 0:
                        continue
                    for h in range(4 * g, 4 * g + 4):
                        o = HD * (h % 2)
                        cc = n * (h // 2 % 2)
                        last = M(pst[o:o + HD, 4 * g + 2, cc:cc + n], FK[0:n, h, 0, :], AM[0:n, h, 3, 0:n],
                                 start=True, stop=True)
                    last.then_inc(rt_done, 1)
                for g in range(2):
                    for ci in range(2 if b else 1):
                        rows = slice(CH * ci, CH * ci + CH) if b else slice(0, n)
                        bank = 4 * g + 3 * ci
                        for h in range(4 * g, 4 * g + 4):
                            o = HD * (h % 2)
                            cc = HD * (h // 2 % 2)
                            hc = slice(HD * h, HD * h + HD)
                            if b:
                                M(pst[o:o + HD, bank, cc:cc + HD], FK[rows, h, 0, :], BT[rows, hc], start=True, stop=True)
                            M(pst[o:o + HD, bank, 128 + cc:128 + cc + HD], KT[rows, hc], VT[rows, hc],
                              start=True, stop=False)
                            last = M(pst[o:o + HD, bank, 128 + cc:128 + cc + HD], BT[rows, hc], FK[rows, h, 1, :],
                                     start=False, stop=True)
                        last.then_inc(mn_done, 1)
                if b == 0:
                    continue
                for ci in range(2):
                    c = 2 * b - 1 + ci
                    if c == NCHUNK - 1:
                        continue
                    pe.wait_ge(q_ready, c)
                    pe.wait_ge(mn_ready, 1 + 4 * b)
                    for t in range(4):
                        last = M(pst[:, 1 + 4 * ci, HD * t:HD * t + HD], MD[:, ci, t, :], QQ[:, t, :], start=True, stop=True)
                    last.then_inc(qn_done, 1)
                for g in range(2):
                    pe.wait_ge(rt_ready, 2 * b)
                    pe.wait_ge(qd_ready, 4 * b)
                    for t in range(2 * g, 2 * g + 2):
                        cc = n * (t % 2)
                        for h in (2 * t, 2 * t + 1):
                            o = HD * (h % 2)
                            dst = pst[o:o + HD, 4 * g + 2, cc:cc + n]
                            M(dst, VT[0:n, HD * h:HD * h + HD], AM[0:n, h, 1, 0:n], start=True, stop=False)
                            M(dst, FK[0:n, h, 1, :], AM[0:n, h, 3, 0:n], start=False, stop=True)
                        for ci in range(2):
                            last = M(pst[:, 4 * g + 2, cc + CH * ci:cc + CH * ci + CH], QD[:, ci, t, :],
                                     KR[:, t, 1, c0 + CH * ci:c0 + CH * ci + CH], start=False, stop=True,
                                     skip_group_check=True)
                    last.then_inc(yy_done, 1)
            pe.wait_ge(yy_copied, 2 * NB)
            pe.wait_ge(sg_ready, 1)

            def post_first(t):
                s = t % 2
                if t >= 2:
                    pe.wait_ge(yf_ready, t - 1)
                M(pst[:, 4 * s, :], headsum, KR[:, t, 0, MB:L], start=True, stop=True).then_inc(post_done, 1)
                M(pst[:, 4 * s + 2, :], headsum, BON[:, t, MB:L], start=True, stop=True).then_inc(post_done, 1)
                M(pst[:, 4 * s + 3, :], g2[:, P * t:P * t + P], SG[:, MB:L], start=True, stop=True).then_inc(post_done, 1)

            def post_var(t):
                pe.wait_ge(postq_ready, t + 1)
                M(pst[:, 4 * (t % 2) + 1, :], headsum, post["sq"][:, t % 2, :], start=True, stop=True)\
                    .then_inc(postv_done, 1)

            post_first(0)
            for t in range(4):
                post_var(t)
                if t < 3:
                    post_first(t + 1)
            pe.wait_ge(yf_ready, 4)

            jobno = [len(PHASE_C)]

            def jobs(k):
                for _ in range(k):
                    job(jobno[0])
                    jobno[0] += 1

            def job(n):
                kind, a, b = JOBS[n]
                u = UNIT_NO[units_of(JOBS[n])[0]]
                if kind in ("aq", "bq", "bg", "dq", "gate"):
                    feature_job(JOBS[n], [(MB, L)])
                elif kind in ("ak", "bk", "dk"):
                    feature_job(JOBS[n], ALL)
                elif kind in ("av", "bv", "dv"):
                    s = job_begin(n)
                    r, toks = (P, slice(MB + P * (b - 1), MB + P * b)) if b else (MB, slice(0, MB))
                    us = u % W_SLOTS
                    if kind == "dv":
                        o = pst[0:r, 2 * s, 0:P]
                        wsl = lambda w, k: wslice(w, u, k)
                    else:
                        o = pst[0:r, 2 * s, 0:2 * P].rearrange("p (a f) -> p a f", a=2)
                        wsl = lambda w, k: w[:, us:us + 2, P * k:P * k + P]
                    product3(o, [((h_hi[:, k, toks], h_lo[:, k, toks]), (wsl(w_hi, k), wsl(w_lo, k)))
                                 for k in range(KD)]).then_inc(dense_done, 1)
                elif kind == "proj":
                    s = job_begin(n)
                    pe.wait_ge(yl_ready, y_count(a) + (8 if a == BRANCH_SW else 4))
                    us = u % W_SLOTS
                    ws = [slice(2 * P * k + P * (b % 2), 2 * P * k + P * (b % 2) + P) for k in range(4)]
                    product3(pst[:, 2 * s, :], [((w_hi[:, us, ws[k]], w_lo[:, us, ws[k]]), (y_hi[:, k, :], y_lo[:, k, :]))
                                                for k in range(4)]).then_inc(dense_done, 1)
                elif kind == "wo":
                    s = job_begin(n)
                    pe.wait_ge(m_lo, KD)
                    us = u % W_SLOTS
                    toks = slice(P * b, P * b + P)
                    product3(pst[:, 2 * s, 0:2 * P].rearrange("p (a f) -> p a f", a=2),
                             [((h_hi[:, k, toks], h_lo[:, k, toks]),
                               (w_hi[:, us:us + 2, P * k:P * k + P], w_lo[:, us:us + 2, P * k:P * k + P]))
                              for k in range(KD)]).then_inc(dense_done, 1)
                elif kind == "up":
                    if a == 1 and b < 2:
                        pe.wait_ge(job_out["down"], 8)
                    s = job_begin(n)
                    product3(pst[:, 2 * s, :], [((wslice(w_hi, u, k), wslice(w_lo, u, k)),
                                                 (h_hi[:, k, 0:T], h_lo[:, k, 0:T])) for k in range(KD)])\
                        .then_inc(dense_done, 1)
                elif kind == "down":
                    c, kk = b
                    if kk == 0:
                        pe.wait_ge(u_lo_ready, FH * (a + 1))
                        if a == 1:
                            pe.wait_ge(job_out["down"], 8)
                    pe.wait_ge(lo_ready, u + 1)
                    us = u % W_SLOTS
                    for j in range(2):
                        f = 2 * kk + j
                        ws = slice(T * j, T * j + T)
                        for blk in range(NB):
                            o = pst[:, down_bank(c, blk), :]
                            toks = slice(P * blk, P * blk + P)
                            M(o, u_hi[:, f, toks], w_hi[:, us, ws], start=(f == 0), stop=False)
                            M(o, u_hi[:, f, toks], w_lo[:, us, ws], start=False, stop=False)
                            last = M(o, u_lo[:, f, toks], w_hi[:, us, ws], start=False, stop=(f == FH - 1))
                    last.then_inc(dense_done, 1)

            def sb_rows(h):
                return slice(HD * (h % 2), HD * (h % 2) + HD)

            def sb_meta(grp):
                if grp == 0:
                    pe.wait_ge(sb_kmd_ready, SBH)
                else:
                    pe.wait_ge(zm_a, grp)
                for t in (2 * grp, 2 * grp + 1):
                    last = M(pst[:, 7, :], sb_kmd[:, t, :], sb_q[:, t, :], start=(t == 2 * grp), stop=(t == 2 * grp + 1))
                last.then_inc(zm_done, 1)

            SB_AT = [(4, 0), (5, 0), (6, 0), (6, 2 * P)]

            def sb_z(h):
                if h:
                    pe.wait_ge(z_a, h)
                r = sb_rows(h)
                for kb in range(NB):
                    bank, c = SB_AT[kb]
                    last = M(pst[:, bank, c:c + T - P * kb], sb_k[r, h // 2, MB + P * kb:MB + P * kb + P],
                             sb_q[r, h // 2, P * kb:T], start=(kb < 3), stop=True, skip_group_check=(kb == 3))
                last.then_inc(z_done, 1)

            def sb_arg(h):
                pe.wait_ge(z_cs, h + 1)
                for kb in range(NB):
                    bank, c = SB_AT[kb]
                    i, ci = bank - 4, c
                    w = T - P * kb
                    last = M(pst[:, bank, c:c + w], C("suffix"), sb_s[:, i, ci:ci + w], start=False, stop=True,
                             skip_group_check=True)
                    if kb < 3:
                        rhs = sb_s[:, 2, 2 * P:3 * P] if kb == 2 else sb_cs[:, kb + 1, 0:w - P]
                        last = M(pst[:, bank, c + P:c + w], C("neg_ones"), rhs, start=False, stop=True,
                                 skip_group_check=True)
                last.then_inc(z_arg, 1)
                grp, j = h // 4, h % 4
                if j == 0:
                    pe.wait_ge(zm_sp, grp + 1)
                    M(pst[:, 7, :], C("suffix_meta"), sb_sm[:], start=False, stop=True, skip_group_check=True)
                o = 3 * MB - MB * j
                last = M(pst[:, 7, :], C("carry_meta", o, o + P), sb_cs[:, 0, :], start=False, stop=True,
                         skip_group_check=True)
                if j == 3:
                    last.then_inc(zm_arg, 1)

            def sb_o(h):
                pe.wait_ge(z_am, h + 1)
                grp, t = h // 4, h // 2
                if h % 4 == 0 and grp:
                    pe.wait_ge(yl_ready, y_count(BRANCH_SB) + 2 * grp)
                if h == 0:
                    pe.wait_ge(*all_out("av", ("av", 1, NB)))
                r = sb_rows(h)
                bank = 1 + 2 * (t % 2)
                for kb in range(NB):
                    i, c = SB_AT[kb][0] - 4, SB_AT[kb][1]
                    last = M(pst[r, bank, P * kb:T], sb_v[:, kb, HD * h:HD * h + HD], sb_e[:, i, c:c + T - P * kb],
                             start=(kb == 0), stop=False)
                last.then_inc(sb_used, 1)

            def sb_end(grp):
                pe.wait_ge(sb_vmd_ready, 16 * SBH)
                pe.wait_ge(zm_a, grp + 1)
                for h in range(4 * grp, 4 * grp + 4):
                    last = M(pst[sb_rows(h), 1 + 2 * (h // 2 % 2), :], sb_vmd[:, h, :], sb_em[:], start=False, stop=True)
                    if h % 2:
                        last.then_inc(o_done, 1)

            def ret_block(b):
                n, c0 = rw_blocks[b]
                toks = slice(c0, c0 + n)
                if b == 0:
                    pe.wait_ge(*all_out("bk", ("bk", 1, 0)))
                    pe.wait_ge(yl_ready, y_count(BRANCH_RET))
                else:
                    pe.wait_ge(rstate, 4 * b)
                for t in range(2):
                    last = nc.tensor.transpose(pst[0:n, 4, P * t:P * t + P], rk[:, t, toks], ident)
                last.then_inc(rkt_done, 1)
                if b:
                    if b == 1:
                        pe.wait_ge(*all_out("bq", ("bq", 1, 0)))
                    else:
                        pe.wait_ge(rsc_ready, 2 * (b - 1))
                    for h in range(RETH):
                        r = slice(HD * (h % 2), HD * (h % 2) + HD)
                        last = M(pst[:, 5 + h % 2, P * (h // 2):P * (h // 2) + P], rk[r, h // 2, toks],
                                 rq[r, h // 2, P * (b - 1):P * b], start=True, stop=True)
                    last.then_inc(rs_done, 1)
                if b < NB:
                    pe.wait_ge(rkd_ready, b + 1)
                    if b == 0:
                        pe.wait_ge(*all_out("bv", ("bv", 1, NB)))
                    vv = rv[:, b - 1, :] if b else rvm[:]
                    for h in range(RETH):
                        last = M(pst[HD * (h % 2):HD * (h % 2) + HD, 4, 2 * P + P * (h // 2):3 * P + P * (h // 2)],
                                 rkd[0:n, h, :], vv[:, P * h:P * h + P], start=True, stop=True)
                    last.then_inc(rkv_done, 1)
                if b:
                    pe.wait_ge(rsc_ready, 2 * b)
                    if b == 1:
                        pe.wait_ge(rqd_ready, 2)
                    if b >= 3:
                        pe.wait_ge(ro_ready, b - 2)
                    for h in range(RETH):
                        o = pst[:, 3 + 4 * (b % 2), P * h:P * h + P]
                        M(o, rv[:, b - 1, P * h:P * h + P], rsc[:, h, :], start=True, stop=False)
                        last = M(o, rsz[:, h, :], rqd[:, h // 2, P * (b - 1):P * b], start=False, stop=True)
                    last.then_inc(ro_done, 1)

            def ret_post():
                for h in range(RETH):
                    pe.wait_ge(rsq_ready, h + 1)
                    M(pst[:, 4 + h % 2, :], C("neg_ones"), rsq[:, h % 2, :], start=True, stop=True).then_inc(rss_done, 1)

            def sw_norm():
                for t in range(5):
                    pe.wait_ge(dsq_ready, t + 1)
                    if t < 4:
                        last = M(pst[:, 4 + t % 2, :], headsum, dsq[:, t % 2, 0:T], start=True, stop=True)
                    else:
                        for i in range(2):
                            last = M(pst[:, 6 + i, 0:HL], headsum, dsq[:, t % 2, HL * i:HL * i + HL], start=True, stop=True)
                    last.then_inc(dss_done, 1)

            def sw_scores(b, kv):
                i = 2 * b + kv
                if i == 0:
                    pe.wait_ge(dn_ready, 5)
                    pe.wait_ge(dk2_own, 2)
                    pe.wait_ge(dk2_in, 32)
                else:
                    pe.wait_ge(dpt_dve, i)
                    pe.wait_ge(yl_ready, y_count(BRANCH_SW) + i)
                for j in range(4):
                    h = 4 * kv + j
                    r = slice(HD * (h % 2), HD * (h % 2) + HD)
                    q = dq[r, h // 2, P * b:P * b + P]
                    if b:
                        M(pst[:, 4 + j, 0:MB], q, dk2[r, kv, 0:MB], start=True, stop=True)
                        last = M(pst[:, 4 + j, MB:MB + 2 * P], q, dk2[r, kv, MB + P * (b - 1):MB + P * (b + 1)],
                                 start=True, stop=True)
                    else:
                        last = M(pst[:, 4 + j, 0:MB + P], q, dk2[r, kv, 0:MB + P], start=True, stop=True)
                    last.then_inc(ds_done, 1)

            def sw_out(b, kv):
                i = 2 * b + kv
                pe.wait_ge(dp_ready, i + 1)
                own = MB + (P if b else 0)
                if i:
                    pe.wait_ge(dpt_act, i)
                for j in range(4):
                    p_ = dsc[:, i % 2, j, :]
                    c = slice(P * j, P * j + P)
                    nc.tensor.transpose(pst[:, 1, c], p_[:, own:own + P], ident)
                    if b:
                        nc.tensor.transpose(pst[:, 3, c], p_[:, MB:MB + P], ident)
                    last = nc.tensor.transpose(pst[0:MB, 7, c], p_[:, 0:MB], ident)
                last.then_inc(dpt_done, 1)
                pe.wait_ge(dpt_act, i + 1)
                pe.wait_ge(dpt_dve, i + 1)
                if i == 0:
                    pe.wait_ge(*all_out("dv", ("dv", 0, NB)))
                vc = slice(HD * kv, HD * kv + HD)
                for par_ in range(2):
                    o = pst[HD * par_:HD * par_ + HD, 6, 0:2 * P].rearrange("p (t q) -> p t q", t=2)

                    def pick(which, rows=P):
                        return dpt[0:rows, i % 2, which, :].rearrange("p (t s q) -> p s t q", t=2, s=2)[:, par_]
                    M(o, dv[:, b, vc], pick(0), start=True, stop=False)
                    if b:
                        M(o, dv[:, b - 1, vc], pick(1), start=False, stop=False)
                    last = M(o, dvm[:, vc], pick(2, MB), start=False, stop=True)
                last.then_inc(do_done, 1)

            def norm2():
                pe.wait_ge(h2n_ready, NB)
                for k in range(KD):
                    if k >= 4:
                        pe.wait_ge(h2lo_ready, k - 3)
                    for b in range(NB):
                        last = nc.tensor.transpose(pst[:, 4 + k % 4, P * b:P * b + P], h2n[:, b, P * k:P * k + P], ident)
                    last.then_inc(h2t_done, 1)
                pe.wait_ge(h2lo_ready, KD)

            run_after_rw("pe", jobs, dict(
                sb_meta=sb_meta, sb_z=sb_z, sb_arg=sb_arg, sb_o=sb_o, sb_end=sb_end, ret_block=ret_block,
                ret_post=ret_post, sw_norm=sw_norm, sw_scores=sw_scores, sw_out=sw_out, norm2=norm2))


def host_layout(inp):
    f = lambda a: np.asarray(a)
    weights = pack_weights(*(f(inp[k]) for k in ("w_in", "p_sb", "p_ret", "p_rw", "p_sw", "w_o", "w_up", "w_down")))
    lora = np.concatenate([np.concatenate([f(inp["rw_w2"])[0], f(inp["rw_a2"])[0]], 0), f(inp["rw_g2"])[0]], 1)
    cols = []
    for name, n in PARAMS:
        if name in ("qn", "kn"):
            v = f(inp[{"qn": "sw_qn_g", "kn": "sw_kn_g"}[name]])[0]
            cols.append(np.concatenate([v, v])[:, None])
        elif name == "sink":
            cols.append(np.broadcast_to(f(inp["sw_sink"])[0][None, :], (P, SWH)))
        else:
            cols.append(f(inp[name]).reshape(n, P).T)
    params = np.ascontiguousarray(np.concatenate(cols, 1))
    return {"weights": weights, "lora": np.ascontiguousarray(lora), "params": params,
            "consts": np.concatenate(list(CONSTS.values()), 1)}


def kernel(**inputs):
    import concourse.bacc as bacc
    from concourse.bass_utils import run_bass_kernel_spmd

    nc = bacc.Bacc("TRN2", target_bir_lowering=False, num_devices=1)
    arrays = {"x": np.asarray(inputs["x"]), "meta": np.asarray(inputs["meta"]), **host_layout(inputs)}
    aps = {k: nc.dram_tensor("in_" + k, a.shape, mybir.dt.from_np(a.dtype), kind="ExternalInput").ap()
           for k, a in arrays.items()}
    out = nc.dram_tensor("out_0", (1, T, D), F32, kind="ExternalOutput").ap()
    build(nc, out=out, **aps)
    r = run_bass_kernel_spmd(nc, [{"in_" + k: a for k, a in arrays.items()}], core_ids=[0])
    return r.results[0]["out_0"]
```

```python
from contextlib import ExitStack

import numpy as np
import concourse.bass as bass
from concourse import mybir

ALU = mybir.AluOpType
ACT = mybir.ActivationFunctionType
AX = mybir.AxisListType
F32 = mybir.dt.float32
F32R = mybir.dt.float32r

P = 128
D = 1024
KD = D // P
T = 512
NB = T // P
N_META = 16
MB = 32
L = MB + T
HL = L // 2
DFF = 4 * D
EPS = 1e-6
RW_LN_EPS = 64e-5
HD = 64
SBH = 8
RWH = 8
RETH = 4
SWH = 8
CH = 64
NCHUNK = 1 + T // CH
LEVELS = 6
NEG = -1.0e30

AQ, AK, AV, BQ, BK, BV, BG, CIN, DQ, DK, DV, GZ = 0, 4, 8, 12, 14, 16, 20, 24, 38, 42, 43, 44
CR, CK, CV, CWA, CG = 0, 4, 8, 12, 13
BRANCH_SB, BRANCH_RET, BRANCH_RW, BRANCH_SW = 0, 1, 2, 3

RW_FILL = [dict(score=1, c1=[1, 1, 1, 1, 1], tu=[0, 1, 1, 1, 1], f=1, wz=0, mn=0, end=0)] + \
          [dict(score=1, c1=[1] * 6, tu=[0, 1, 1, 1, 1, 1], f=1, wz=w, mn=1, end=1) for w in (0, 0, 1, 1)]
SB_FILL = [(2, 1)] * 8
RET_FILL = [(2, 1)] * 5
RET_POST_FILL = [(1, 1), (1, 1), (1, 1), (1, 0)]
SW_FILL = [(2, 1), (2, 1)] + [(1, 1)] * 6

RAW_SLOTS = 3
W_SLOTS = 4
UW = KD * P


def proj_jobs(br):
    return [("proj", br, i) for i in range(KD)]


def gate_jobs(br):
    return [("gate", br, i) for i in range(KD)]


def av_jobs(name):
    return [(name, pair, blk) for pair in range(2) for blk in range(NB + 1)]


PHASE_C = [("c", i, 0) for i in (CWA, CG)] + [("c", i, 0) for i in (CK, CR, CV)] + \
          [("c", i + t, 0) for t in range(1, 4) for i in (CK, CR, CV)]
SPILLED = ("rgate", "bq", "bk", "bv", "bg", "dq", "dk", "dv")
PHASE_A = [("rgate", BRANCH_RW, i) for i in range(KD)] + \
          [("bq", t, 0) for t in range(2)] + [("bk", t, 0) for t in range(2)] + av_jobs("bv") + \
          [("bg", t, 0) for t in range(4)] + \
          [("dq", t, 0) for t in range(4)] + [("dk", 0, 0)] + [("dv", 0, b) for b in range(NB + 1)] + \
          [("aq", t, 0) for t in range(4)] + [("ak", t, 0) for t in range(4)]
PHASE_B = av_jobs("av") + proj_jobs(BRANCH_RW) + gate_jobs(BRANCH_SB)
PHASE_D = proj_jobs(BRANCH_SB) + gate_jobs(BRANCH_RET)
PHASE_E = proj_jobs(BRANCH_RET) + gate_jobs(BRANCH_SW)
PHASE_O = [("wo", c, b) for c in range(4) for b in range(NB)]
FH = DFF // P // 2


def up_jobs(half):
    return [("up", half, f) for f in range(FH)]


def down_jobs(half):
    return [("down", half, (c, kk)) for c in range(2) for kk in range(FH // 2)]


JOBS = (PHASE_C + PHASE_A + PHASE_B + PHASE_D + PHASE_E + proj_jobs(BRANCH_SW) + PHASE_O + up_jobs(0) +
        down_jobs(0) + up_jobs(1) + down_jobs(1))
JOB_NO = {j: n for n, j in enumerate(JOBS)}


def units_of(job):
    kind, a, b = job
    if kind == "c":
        return [("w_in", CIN + a)]
    if kind in ("aq", "ak", "bq", "bk", "bg", "dq", "dk", "dv"):
        base = {"aq": AQ, "ak": AK, "bq": BQ, "bk": BK, "bg": BG, "dq": DQ, "dk": DK, "dv": DV}[kind]
        return [("w_in", base + a)]
    if kind in ("av", "bv"):
        base = {"av": AV, "bv": BV}[kind]
        return [("w_in", base + 2 * a), ("w_in", base + 2 * a + 1)]
    if kind in ("gate", "rgate"):
        return [("w_in", GZ + KD * a + b)]
    if kind == "proj":
        return [("p", a, b // 2)]
    if kind == "wo":
        return [("w_o", 2 * a), ("w_o", 2 * a + 1)]
    if kind == "up":
        return [("w_up", a * FH + b)]
    c, kk = b
    return [("w_down", a * FH // 2 + kk, c)]


UNITS, UNIT_NO, LAST_JOB = [], {}, {}
for _n, _j in enumerate(JOBS):
    for _u in units_of(_j):
        if _u not in UNIT_NO:
            UNIT_NO[_u] = len(UNITS)
            UNITS.append(_u)
        LAST_JOB[UNIT_NO[_u]] = _n
NU = len(UNITS)
KIND_NO, _c = [], {}
for _j in JOBS:
    KIND_NO.append(_c.get(_j[0], 0))
    _c[_j[0]] = KIND_NO[-1] + 1
PIECES = [(n, i, k) for n, j in enumerate(JOBS) for k in [2 if j[0] in ("aq", "ak", "bq", "bk", "bg", "dq", "dk", "gate", "rgate") else 1]
          for i in range(k)]
FIRST_PIECE = {n: i for i, (n, part, _) in enumerate(PIECES) if part == 0}
SPILL_NO = {n: i for i, n in enumerate(n for n, j in enumerate(JOBS) if j[0] in SPILLED)}
assert all(UNIT_NO[units_of(j)[0]] % 2 == 0 for j in JOBS if j[0] in ("av", "bv", "wo"))


def pack_weights(w_in, p_sb, p_ret, p_rw, p_sw, w_o, w_up, w_down):
    ps = (p_sb, p_ret, p_rw, p_sw)
    out = np.empty((NU, P, UW), np.float32)
    for n, u in enumerate(UNITS):
        if u[0] == "p":
            m = ps[u[1]][0][:, 256 * u[2]:256 * u[2] + 256]
        elif u[0] == "w_down":
            m = w_down[0][256 * u[1]:256 * u[1] + 256, 512 * u[2]:512 * u[2] + 512]
        else:
            m = {"w_in": w_in, "w_o": w_o, "w_up": w_up}[u[0]][0][:, P * u[1]:P * u[1] + P]
        out[n] = m.reshape(-1, P, m.shape[1]).transpose(1, 0, 2).reshape(P, UW)
    return out


def constants():
    i = np.arange(P)
    c = {"ident": np.eye(P), "headsum": (i[:, None] // HD == i[None, :] // HD) * 1.0}
    s, t = i[:, None], i[None, :]
    cs, ct = i[:, None] % CH, np.arange(CH)[None, :]
    c["ident_chunk"] = cs == ct
    c["rw_mask"] = np.concatenate([cs < ct, cs <= ct] * 2, 1)
    c["levels"] = np.concatenate(
        [(cs // (2 << l) == ct // (2 << l)) & ((cs >> l) % 2 == 0) & ((ct >> l) % 2 == 1) for l in range(LEVELS)], 1)
    start = np.ones(L)
    start[[0] + [MB + CH * k for k in range(T // CH)]] = 0
    c["scan_keep"] = np.broadcast_to(start, (P, L))
    c["suffix"] = -1.0 * (s >= t)
    c["suffix_meta"] = -1.0 * ((s >= t) & (s // MB == t // MB))
    strip = np.zeros((P, 3 * MB + MB + 3 * MB))
    strip[:, 3 * MB:4 * MB] = -1.0
    c["carry_meta"] = strip
    c["neg_ones"] = -np.ones((P, P))
    g = 1.0 - 2.0 ** (-5.0 - np.arange(RETH))
    diff = t - s
    c["ret_mask"] = np.concatenate([np.where(diff >= 0, gh ** np.maximum(diff, 0), 0) * HD ** -0.5 for gh in g], 1)
    c["ret_kdec"] = np.stack([gh ** (P - 1 - i) for gh in g], 1) * HD ** -0.5
    c["ret_kdec_meta"] = np.stack([gh ** np.maximum(MB - 1 - i, 0) for gh in g], 1) * HD ** -0.5
    c["ret_qdec"] = np.concatenate(
        [np.where(i[:, None] < HD, g[2 * p] ** (t + 1.0), g[2 * p + 1] ** (t + 1.0)) for p in range(2)], 1)
    key = np.arange(2 * P)[None, :]
    dist = (i[:, None] + P) - key
    band = np.where((dist >= 0) & (dist < P), -dist, NEG)
    meta = np.where(np.arange(MB)[None, :] < MB - N_META, NEG, 0.0) + 0.0 * i[:, None]
    c["sw_bias"] = np.concatenate([meta, band], 1)
    return {k: np.ascontiguousarray(v, np.float32) for k, v in c.items()}


RET_CHUNK_DECAY = [float((1.0 - 2.0 ** (-5.0 - h)) ** P) for h in range(RETH)]
CONSTS = constants()
CONST_AT, _o = {}, 0
for _k, _v in CONSTS.items():
    CONST_AT[_k] = (_o, _v.shape[1])
    _o += _v.shape[1]
NCONST = _o

PARAMS = [("norm1_g", 8), ("norm2_g", 8), ("rw_mu", 14), ("rw_w0", 4), ("rw_a0", 4), ("rw_kk", 4), ("rw_ka", 4),
          ("rw_rk", 4), ("rw_ln_g", 4), ("rw_ln_b", 4), ("qn", 1), ("kn", 1), ("sink", 8)]
PARAM_AT, _o = {}, 0
for _k, _n in PARAMS:
    PARAM_AT[_k] = (_o, _n)
    _o += _n
NPARAM = _o

SBUF_BASE, SBUF_END = 16512, 229344


def build(nc, x, meta, weights, lora, consts, params, out, debug=None, upto="all"):
    with ExitStack() as ctx:
        cursor = [SBUF_BASE]

        def place(name, shape, dt=F32, at=None):
            size = 4 * int(np.prod(shape[1:]))
            size = (size + 31) // 32 * 32
            if at is None:
                at = cursor
            t = nc.alloc_sbuf_tensor_at(name, shape, dt, offset=at[0])
            at[0] += size
            assert at[0] <= SBUF_END, (name, at[0])
            return t

        slab = SBUF_BASE
        cst = place("cst", [P, NCONST])
        par = place("par", [P, NPARAM])
        half_wa = place("half_wa", [P, 8])
        one_minus_ka = place("one_minus_ka", [P, 4])
        gain_q = place("gain_q", [P, 1])
        lor = place("lor", [P, 2 * T])
        h_hi = place("h_hi", [P, KD, L], F32R)
        h_lo = place("h_lo", [P, KD, L], F32R)
        raw = place("raw", [P, RAW_SLOTS, UW])
        w_hi = place("w_hi", [P, W_SLOTS, UW], F32R)
        w_lo = place("w_lo", [P, W_SLOTS, UW], F32R)
        region = cursor[0]

        at = [region]
        xt = place("xt", [P, NB, D], at=at)
        xm = place("xm", [MB, D], at=at)
        sq0 = place("sq0", [P, D], at=at)
        ss0 = place("ss0", [P, NB + 1], at=at)
        rs0 = place("rs0", [P, NB + 1], at=at)

        at = [region]
        sb_q = place("sb_q", [P, 4, T], at=at)
        sb_k = place("sb_k", [P, 4, L], at=at)
        sb_at = at[0]
        KR = place("rw_kappa_r", [P, 4, 2, L], at=at)
        KH = place("rw_k", [P, 4, L], at=at)
        BH = place("rw_b", [P, 4, L], at=at)
        RV = place("rw_v", [P, 4, L], at=at)
        BON = place("rw_bonus", [P, 4, L], at=at)
        SG = place("rw_sig_g", [P, L], at=at)
        GC = place("rw_chunk_decay", [P, 4, NCHUNK], at=at)
        mix_at = at[0]
        cbuf = place("cbuf", [P, 3, L + 1], at=at)
        cdif = place("cdif", [P, L], at=at)
        WA = place("rw_wa", [P, L], at=at)
        tmp_names = ["LAM", "AA", "LG", "LGX", "KKR", "T1", "SQ", "RN", "BB", "E1", "E2", "E3"]
        tt = {k: place("rw_" + k, [P, L], at=at) for k in tmp_names}
        at = [mix_at]
        KT = place("rw_k_tok", [P, T], at=at)
        BT = place("rw_b_tok", [P, T], at=at)
        VT = place("rw_v_tok", [P, T], at=at)
        FK = place("rw_wz", [P, RWH, 2, HD], at=at)
        AM = place("rw_scores", [P, RWH, 4, CH], at=at)
        XX = place("rw_x", [P, RWH, CH], at=at)
        TT = place("rw_t", [P, RWH, CH], at=at)
        C1 = place("rw_c1", [P, RWH, CH], at=at)
        MM = place("rw_m", [P, 2, RWH, CH], at=at)
        MD = place("rw_md", [P, 2, 4, P], at=at)
        QD = place("rw_qd", [P, 2, 4, P], at=at)
        QQ = place("rw_q", [P, 4, HD], at=at)
        NG = place("rw_ng", [P, 2, 4, HD], at=at)
        stage = place("stage", [P, 2, L], at=at)
        at = [mix_at]
        post = {k: place("rwp_" + k, [P, T], at=at) for k in ("sq", "rs", "bon")}
        top = SBUF_END - 4 * (2 * T + KD * T + KD * T + 2 * 4 * T)
        at = [top]
        gtmp = place("gtmp", [P, 2, T], at=at)
        gate_t = place("gate_t", [P, KD, T], at=at)
        merged = place("merged", [P, KD, T], at=at)
        y_hi = place("y_hi", [P, 4, T], F32R, at=at)
        y_lo = place("y_lo", [P, 4, T], F32R, at=at)
        SBW = [T, T - P, T - 2 * P, T - 3 * P]
        SB_COL = [0, T, 2 * T - P, 3 * T - 3 * P]
        SB_N = sum(SBW)
        at = [sb_at]
        sb_v = place("sb_v", [P, NB, T], at=at)
        sb_vm = place("sb_vm", [MB, T], at=at)
        sb_kmd = place("sb_kmd", [P, 4, P], at=at)
        sb_vmd = place("sb_vmd", [P, SBH, HD], at=at)
        sb_e = place("sb_e", [P, SB_N], at=at)
        sb_s = place("sb_s", [P, SB_N], at=at)
        sb_cs = place("sb_cs", [P, SB_N - P], at=at)
        sb_em = place("sb_em", [P, T], at=at)
        sb_sm = place("sb_sm", [P, T], at=at)
        sb_end_at = at[0]
        at = [top - 4 * (2 * T + 2 * L + T) - 32]
        assert at[0] >= sb_end_at, (at[0], sb_end_at)
        ret_in_at = at[0]
        rq = place("ret_q", [P, 2, T], at=at)
        rk = place("ret_k", [P, 2, L], at=at)
        rvm = place("ret_vm", [MB, T], at=at)
        assert at[0] <= top
        at = [region]
        rg = place("ret_g", [P, 4, T], at=at)
        ro_at = at[0]
        ro = place("ret_o", [P, RETH, T], at=at)
        rth = place("ret_th", [P, 4, T], at=[ro_at])
        rqd = place("ret_qd", [P, 2, T], at=at)
        rkd = place("ret_kd", [P, RETH, HD], at=at)
        rsc = place("ret_sc", [P, RETH, P], at=at)
        rsz = place("ret_state", [P, RETH, P], at=at)
        rsq = place("ret_sq", [P, 2, T], at=at)
        rv = place("ret_v", [P, NB, T], at=at)
        ret_end = at[0]
        at = [region]
        dk2 = place("sw_k2", [P, 2, L], at=at)
        dsq = place("sw_sq", [P, 2, L], at=at)
        dsc = place("sw_scores", [P, 2, 4, MB + 2 * P], at=at)
        dpt = place("sw_probs_t", [P, 2, 3, T], at=at)
        dst_ = place("sw_stats", [P, 2, 5, 4], at=at)
        at = [max(at[0], ret_end)]
        dq = place("sw_q", [P, 4, T], at=at)
        dk = place("sw_k", [P, L], at=at)
        dv = place("sw_v", [P, NB, P], at=at)
        dvm = place("sw_vm", [MB, P], at=at)
        assert at[0] <= ret_in_at
        ysw = place("sw_y", [P, 4, T], at=at)
        assert at[0] <= top
        at = [region]
        x2 = place("x2", [P, NB, D], at=at)
        u_hi = place("u_hi", [P, FH, T], F32R, at=at)
        u_lo = place("u_lo", [P, FH, T], F32R, at=at)
        ub = place("ub", [P, 2, T], at=at)
        usq = place("usq", [P, 2, T], at=at)
        ss2 = place("ss2", [P, 2, NB], at=at)
        h2n = place("h2n", [P, NB, D], at=at)

        pst = ctx.enter_context(nc.psum_tensor("pst", [P, 8, 512], F32))

        def scratch(name, shape):
            return nc.dram_tensor("wait_" + name, shape, F32).ap()
        spill = {"rgate": scratch("gate", (P, KD, T)), "bq": scratch("ret_q", (P, 2, T)),
                 "bk": scratch("ret_k", (P, 2, L)), "bv": scratch("ret_v", (P, NB, T)),
                 "bvm": scratch("ret_vm", (MB, T)), "bg": scratch("ret_g", (P, 4, T)),
                 "dq": scratch("sw_q", (P, 4, T)), "dk": scratch("sw_k", (P, L)),
                 "dv": scratch("sw_v", (P, NB, P)), "dvm": scratch("sw_vm", (MB, P))}

        def sem(name):
            return ctx.enter_context(nc.semaphore(name))

        const_in, table_in = sem("const_in"), sem("table_in")
        xb_in = [sem(f"xb_in{b}") for b in range(NB)]
        x_in = sem("x_in")
        raw_in = [sem(f"raw_in{i}") for i in range(RAW_SLOTS)]
        hi_ready = sem("hi_ready")
        lo_ready = sem("lo_ready")
        dense_done = sem("dense_done")
        dve_step, act_step, pool_step = sem("dve_step"), sem("act_step"), sem("pool_step")
        ss_ready = sem("ss_ready")
        rs_ready = sem("rs_ready")
        hn_ready = sem("hn_ready")
        ht_done = sem("ht_done")
        hhi_ready = sem("hhi_ready")
        hlo_ready = sem("hlo_ready")
        par_ready = sem("par_ready")
        zeros_ready, cbuf_zeroed, diag_zeroed = sem("zeros_ready"), sem("cbuf_zeroed"), sem("diag_zeroed")
        c_copied, c_mixed = sem("c_copied"), sem("c_mixed")
        wa_tanh, sg_tanh, sg_ready = sem("wa_tanh"), sem("sg_tanh"), sem("sg_ready")
        lora_done, lora_act = sem("lora_done"), sem("lora_act")
        kkr_ready, kksq_ready, kksum_done, kkclamped, rn_ready = (
            sem("kkr_ready"), sem("kksq_ready"), sem("kksum_done"), sem("kkclamped"), sem("rn_ready"))
        lg_ready, e_ready, rw_elem = sem("lg_ready"), sem("e_ready"), sem("rw_elem")
        tok_done, tok_act, tok_dve = sem("tok_done"), sem("tok_act"), sem("tok_dve")
        am_done, am_ready = sem("am_done"), sem("am_ready")
        m_ready = [sem("m_ready0"), sem("m_ready1")]
        c1_done = [sem("c1_done0"), sem("c1_done1")]
        c1_copied = [sem("c1_copied0"), sem("c1_copied1")]
        tu_done = [sem("tu_done0"), sem("tu_done1")]
        x_ready = [sem("x_ready0"), sem("x_ready1")]
        f_done, f_copied, wz_done, wz_ready = sem("f_done"), sem("f_copied"), sem("wz_done"), sem("wz_ready")
        mn_done, mn_ready = sem("mn_done"), sem("mn_ready")
        qn_done, q_ready, qd_ready = sem("qn_done"), sem("q_ready"), sem("qd_ready")
        yy_done, yy_copied = sem("yy_done"), sem("yy_copied")
        post_done, postc_ready, postq_ready, postv_done, postr_ready = (
            sem("post_done"), sem("postc_ready"), sem("postq_ready"), sem("postv_done"), sem("postr_ready"))
        yf_ready, yh_ready, yl_ready = sem("yf_ready"), sem("yh_ready"), sem("yl_ready")
        merged_ready = sem("merged_ready")
        spill_copied = sem("spill_copied")
        spill_out = [sem("spill_out0"), sem("spill_out1")]
        gates_in, ret_qk_in, sw_in = sem("gates_in"), sem("ret_qk_in"), sem("sw_in")
        ret_g_in, ret_v_in = sem("ret_g_in"), sem("ret_v_in")
        out_done = sem("out_done")
        job_out = {k: sem(k + "_out") for k in
                   ("aq", "ak", "av", "gate", "proj", "wo", "up", "down")}
        gate_tanh = sem("gate_tanh")
        sb_diag_zeroed, sb_kmd_ready, sb_vmd_ready = sem("sb_diag_zeroed"), sem("sb_kmd_ready"), sem("sb_vmd_ready")
        zm_done, zm_ln, zm_sp, zm_arg, zm_a = (
            sem("zm_done"), sem("zm_ln"), sem("zm_sp"), sem("zm_arg"), sem("zm_a"))
        z_done, z_ln, z_sp, z_spm, z_cs, z_arg, z_a, z_am, o_done = (
            sem("z_done"), sem("z_ln"), sem("z_sp"), sem("z_spm"), sem("z_cs"), sem("z_arg"),
            sem("z_a"), sem("z_am"), sem("o_done"))
        sb_used = sem("sb_used")
        rg_tanh, rqd_ready, rsz_zeroed = sem("rg_tanh"), sem("rqd_ready"), sem("rsz_zeroed")
        rkt_done, rkd_ready, rs_done, rsc_ready, rkv_done, rstate, ro_done, ro_ready = (
            sem("rkt_done"), sem("rkd_ready"), sem("rs_done"), sem("rsc_ready"), sem("rkv_done"), sem("rstate"),
            sem("ro_done"), sem("ro_ready"))
        rsq_ready, rss_done, rrs_ready, ry_ready = sem("rsq_ready"), sem("rss_done"), sem("rrs_ready"), sem("ry_ready")
        dsq_ready, dss_done, drs_ready, dn_ready, dk2_own, dk2_in = (
            sem("dsq_ready"), sem("dss_done"), sem("drs_ready"), sem("dn_ready"), sem("dk2_own"), sem("dk2_in"))
        ds_done, ds_read, dmx_ready, dexp_ready, dp_ready, dpt_done, dpt_act, dpt_dve, do_done = (
            sem("ds_done"), sem("ds_read"), sem("dmx_ready"), sem("dexp_ready"), sem("dp_ready"), sem("dpt_done"),
            sem("dpt_act"), sem("dpt_dve"), sem("do_done"))
        ysw_ready = sem("ysw_ready")
        x2_in, m_hi, m_lo = sem("x2_in"), sem("m_hi"), sem("m_lo")
        ss2_ready, rs2_ready, h2n_ready, h2t_done, h2hi_ready, h2lo_ready = (
            sem("ss2_ready"), sem("rs2_ready"), sem("h2n_ready"), sem("h2t_done"), sem("h2hi_ready"), sem("h2lo_ready"))
        u_hi_ready, u_lo_ready = sem("u_hi_ready"), sem("u_lo_ready")

        def C(name, lo=0, hi=None, rows=P):
            a, n = CONST_AT[name]
            return cst[0:rows, a + lo:a + (n if hi is None else hi)]

        def PAR(name, t):
            a, _ = PARAM_AT[name]
            return par[:, a + t:a + t + 1]

        ident = C("ident")
        headsum = C("headsum")
        w2, a2, g2 = lor[0:HD, 0:T], lor[HD:P, 0:T], lor[:, T:2 * T]

        def pair(slot):
            return pst[:, 2 * slot:2 * slot + 2, 0:HL]

        def four(row):
            return row.rearrange("p (h d) -> p h d", h=4)

        def halves(row):
            return row.rearrange("p (a b) -> p a b", a=2)

        def job_slot(n):
            return n % 2

        def kind_no(n):
            return KIND_NO[n]

        def emptied(n):
            kind, a, b = JOBS[n]
            if kind == "c":
                return c_copied, kind_no(n) + 1
            if kind in SPILLED:
                return spill_copied, SPILL_NO[n] + 1
            if kind == "down":
                half, (c, kk) = a, b
                return job_out["down"], 4 * (2 * half + c) + 4
            return job_out[kind], kind_no(n) + 1

        def diag23(tile):
            return tile[:, SB_COL[2] - P:SB_N].rearrange("p (a b) -> p a b", a=2)[:, :, P:2 * P]

        def chunks_of(b):
            if b == 0:
                return [(slice(0, MB), 0, MB)]
            return [(slice(CH * i, CH * i + CH), MB + P * (b - 1) + CH * i, CH) for i in range(2)]

        def down_bank(c, blk):
            return (4 if c == 0 else 0) + blk

        def all_out(kind, job):
            return emptied(JOB_NO[job])

        br_order = [BRANCH_RW, BRANCH_SB, BRANCH_RET, BRANCH_SW]

        def y_count(br):
            return 4 * br_order.index(br)

        def y_free(br):
            n = br_order.index(br)
            return JOB_NO[("proj", br_order[n - 1], KD - 1)] + 1

        JOBN = JOB_NO
        NRUN = len(JOBS)
        NUNITS = NU
        ends = {"rw": PHASE_A[-1], "ysb": PHASE_B[-1], "yret": PHASE_D[-1], "ysw": PHASE_E[-1]}
        if upto in ends:
            NRUN = JOB_NO[ends[upto]] + 1
            NUNITS = UNIT_NO[units_of(JOBS[NRUN - 1])[-1]] + 1
        rw_blocks = [(MB, 0)] + [(P, MB + P * b) for b in range(NB)]
        levels_of = [LEVELS - 1] + [LEVELS] * NB
        level0 = [sum(levels_of[:b]) for b in range(NB + 1)]
        tblocks = rw_blocks

        block = ctx.enter_context(nc.Block())

        def debug_srcs():
            cnt = {"rw": 4, "ysb": 8, "yret": 12, "ysw": 16}[upto]
            return {
                "hh": (h_hi[:].bitcast(F32), yl_ready, cnt),
                "yh": (y_hi[:].bitcast(F32), yl_ready, cnt), "yl": (y_lo[:].bitcast(F32), yl_ready, cnt),
            }

        def run_after_rw(pieces, jobs, f):
            def g(name, *a):
                if name in f:
                    f[name](*a)

            if upto == "rw":
                return
            g("reload_early")
            g("sb_prep")
            g("sb_keys")
            for grp in range(2):
                g("sb_meta", grp)
                for h in range(4 * grp, 4 * grp + 4):
                    g("sb_z", h)
                    if h == 0:
                        jobs(2 * (NB + 1))
                        g("sb_values")
                    g("sb_mask", h)
                    g("sb_sums", h)
                    pieces(SB_FILL[h][0])
                    g("sb_arg", h)
                    g("sb_amask", h)
                    pieces(SB_FILL[h][1])
                    g("sb_o", h)
                g("sb_end", grp)
            if upto == "ysb":
                return
            g("reload_late")
            g("ret_prep")
            pieces(2)
            g("ret_gate")
            for b in range(NB + 1):
                g("ret_scores", b)
                pieces(RET_FILL[b][0])
                g("ret_out", b)
                pieces(RET_FILL[b][1])
            for h in range(RETH):
                g("ret_square", h)
                pieces(RET_POST_FILL[h][0])
                g("ret_norm", h)
                pieces(RET_POST_FILL[h][1])
            if upto == "yret":
                return
            for t in range(5):
                g("sw_square", t)
                pieces(1)
                g("sw_norm", t)
            g("sw_keys")
            pieces(1)
            for b in range(NB):
                for kv in range(2):
                    g("sw_scores", b, kv)
                    pieces(SW_FILL[2 * b + kv][0])
                    g("sw_probs", b, kv)
                    g("sw_turn", b, kv)
                    pieces(SW_FILL[2 * b + kv][1])
                    g("sw_out", b, kv)
            g("sw_split")
            if upto == "ysw":
                return
            jobs(KD)
            g("merge_split")
            jobs(len(PHASE_O))
            g("norm2")
            for half in range(2):
                jobs(FH)
                jobs(FH)

        @block.sync
        def _(sp):
            for b in range(NB):
                sp.dma_start(xt[:, b, :], x[0, P * b:P * b + P, :]).then_inc(xb_in[b], 16)
            sp.wait_ge(zeros_ready, 1)
            sp.dma_start(xm[MB - N_META:MB, :], meta).then_inc(x_in, 16)
            sp.dma_start(par[:], params).then_inc(const_in, 16)
            sp.dma_start(cst[:, 0:P], consts[:, 0:P]).then_inc(const_in, 16)
            for u in range(NUNITS):
                if u >= RAW_SLOTS:
                    sp.wait_ge(lo_ready, u - RAW_SLOTS + 1)
                sp.dma_start(raw[:, u % RAW_SLOTS, :], weights[u]).then_inc(raw_in[u % RAW_SLOTS], 16)
                if u == 0:
                    sp.dma_start(cst[:, P:NCONST], consts[:, P:NCONST]).then_inc(table_in, 16)
                    sp.dma_start(lor[:], lora).then_inc(table_in, 16)
            if debug is not None:
                n = 0
                for name, (src_, wait_sem, val) in debug_srcs().items():
                    sp.wait_ge(wait_sem, val)
                    sp.dma_start(debug[name], src_).then_inc(out_done, 16)
                    n += 16
                sp.wait_ge(out_done, n)
                return
            for c in range(2):
                for b in range(NB):
                    sp.wait_ge(job_out["down"], 8 + 4 * c + b + 1)
                    sp.dma_start(out[0, P * b:P * b + P, T * c:T * c + T], x2[:, b, T * c:T * c + T])\
                        .then_inc(out_done, 16)
            sp.wait_ge(out_done, 16 * 2 * NB)

        @block.gpsimd
        def _(pool):
            nc.gpsimd.memset(xm[:], 0.0).then_inc(zeros_ready, 1)
            done = [0]

            def low(upto_unit):
                while done[0] < min(upto_unit, NUNITS):
                    u = done[0]
                    pool.wait_ge(hi_ready, u + 1)
                    nc.gpsimd.tensor_tensor(w_lo[:, u % W_SLOTS, :], raw[:, u % RAW_SLOTS, :],
                                            w_hi[:, u % W_SLOTS, :].bitcast(F32), ALU.subtract).then_inc(lo_ready, 1)
                    done[0] += 1

            def sb_prep():
                pool.wait_ge(yl_ready, 4)
                nc.gpsimd.memset(sb_kmd[:], 0.0).then_inc(sb_diag_zeroed, 1)
                nc.gpsimd.memset(sb_vmd[:], 0.0).then_inc(pool_step, 1)

            def sb_values():
                pool.wait_ge(pool_step, 1)
                pool.wait_ge(*emptied(JOB_NO[("av", 1, 0)]))
                for h in range(SBH):
                    q = MB * (h % 4)
                    pool.dma_start(sb_vmd[q:q + MB, h, :], sb_vm[:, HD * h:HD * h + HD]).then_inc(sb_vmd_ready, 16)

            def sb_diag(tile):
                for v in (tile[:, 0:2 * T].rearrange("p (a b) -> p a b", a=2)[:, :, 0:P],
                          diag23(tile)):
                    last = nc.gpsimd.affine_select(out=v, in_=v, compare_op=ALU.is_gt, fill=0.0, base=0,
                                                   pattern=[[0, 2], [1, P]], channel_multiplier=-1)
                return last

            def sb_mask(h):
                pool.wait_ge(z_sp, h + 1)
                sb_diag(sb_s).then_inc(z_spm, 1)

            def sb_amask(h):
                pool.wait_ge(z_a, h + 1)
                sb_diag(sb_e).then_inc(z_am, 1)

            def ret_prep():
                pool.wait_ge(yl_ready, 8)
                nc.gpsimd.memset(rsz[:], 0.0).then_inc(rsz_zeroed, 1)

            piece = [FIRST_PIECE[len(PHASE_C)]]

            def pieces(k):
                for _ in range(k):
                    n, part, parts = PIECES[piece[0]]
                    if part == parts - 1:
                        low(UNIT_NO[units_of(JOBS[n])[0]] + W_SLOTS)
                    piece[0] += 1

            def jobs(k):
                n = PIECES[piece[0]][0]
                pieces(FIRST_PIECE.get(n + k, len(PIECES)) - FIRST_PIECE[n])

            low(UNIT_NO[units_of(PHASE_C[-1])[0]] + W_SLOTS)
            pool.wait_ge(rw_elem, 4)
            nc.gpsimd.memset(MD[:], 0.0).then_inc(diag_zeroed, 1)
            nc.gpsimd.memset(QD[:], 0.0).then_inc(diag_zeroed, 1)
            pool.wait_ge(table_in, 32)

            def level_mask(b, l):
                n, m = rw_blocks[b][0], chunks_of(b)[0][2]
                step = level0[b] + l
                for g in range(2):
                    if l == 0:
                        pool.wait_ge(am_ready, 4 * b + 2 * g + 2)
                    if step >= 2:
                        pool.wait_ge(x_ready[g], step - 1)
                    nc.gpsimd.tensor_tensor(
                        MM[0:n, step % 2, 4 * g:4 * g + 4, 0:m], AM[0:n, 4 * g:4 * g + 4, 2, 0:m],
                        C("levels", CH * l, CH * l + m, n).unsqueeze(1).broadcast_to([n, 4, m]),
                        ALU.mult).then_inc(m_ready[g], 1)

            for b in range(NB + 1):
                fill = RW_FILL[b]
                pieces(fill["score"])
                level_mask(b, 0)
                for l in range(levels_of[b]):
                    if l + 1 < levels_of[b]:
                        level_mask(b, l + 1)
                    pieces(fill["c1"][l] + fill["tu"][l])
                pieces(fill["f"] + fill["wz"] + fill["mn"] + fill["end"])
            run_after_rw(pieces, jobs, {
                "sb_prep": sb_prep, "sb_mask": sb_mask, "sb_amask": sb_amask,
                "ret_prep": ret_prep, "sb_values": sb_values})
            low(NUNITS)

        @block.scalar
        def _(act):
            steps = [0]

            def link(ins):
                ins.then_inc(act_step, 1)
                steps[0] += 1
                act.wait_ge(act_step, steps[0])

            units = [0]

            def high(upto_unit):
                while units[0] < min(upto_unit, NUNITS):
                    u = units[0]
                    act.wait_ge(raw_in[u % RAW_SLOTS], 16 * (u // RAW_SLOTS + 1))
                    if u >= W_SLOTS:
                        act.wait_ge(dense_done, LAST_JOB[u - W_SLOTS] + 1)
                    nc.scalar.activation(w_hi[:, u % W_SLOTS, :], raw[:, u % RAW_SLOTS, :], ACT.Copy)\
                        .then_inc(hi_ready, 1)
                    units[0] += 1

            def after_job(n):
                high(UNIT_NO[units_of(JOBS[n])[0]] + W_SLOTS)

            A = nc.scalar.activation
            nc.scalar.preload_act_table_set("natural_log_exp_and_others")
            for b in range(NB):
                act.wait_ge(xb_in[b], 16)
                A(sq0[:], xt[:, b, :], ACT.Square, accum_out=ss0[:, b:b + 1]).then_inc(ss_ready, 1)
                act.wait_ge(ss_ready, b + 1)
            act.wait_ge(x_in, 16)
            A(sq0[0:MB, :], xm[:], ACT.Square, accum_out=ss0[0:MB, NB:NB + 1]).then_inc(ss_ready, 1)
            act.wait_ge(ss_ready, NB + 1)
            for r, cc in ((P, slice(0, NB)), (MB, slice(NB, NB + 1))):
                link(A(rs0[0:r, cc], ss0[0:r, cc], ACT.Ln, scale=1.0 / D, bias=EPS))
                A(rs0[0:r, cc], rs0[0:r, cc], ACT.Exp, scale=-0.5).then_inc(rs_ready, 1)
            high(RAW_SLOTS)
            act.wait_ge(const_in, 32)
            for k in range(KD):
                act.wait_ge(ht_done, k + 1)
                A(h_hi[:, k, MB:L], pst[:, k % 4, :], ACT.Copy, scale=PAR("norm1_g", k)).then_inc(hhi_ready, 1)
                A(h_hi[:, k, 0:MB], pst[:, 4 + k % 4, 0:MB], ACT.Copy, scale=PAR("norm1_g", k)).then_inc(hhi_ready, 1)

            nc.scalar.preload_act_table_set("exp_and_others")
            act.wait_ge(cbuf_zeroed, 1)

            def c_copy(i):
                n = JOBN[PHASE_C[i]]
                act.wait_ge(dense_done, n + 1)
                if i >= 3:
                    act.wait_ge(c_mixed, i - 2)
                A(halves(cbuf[:, i % 3, 1:L + 1]), pair(job_slot(n)), ACT.Copy).then_inc(c_copied, 1)
                after_job(n)

            c_copy(0)
            c_copy(1)
            act.wait_ge(c_mixed, 1)
            A(WA[0:HD, :], WA[0:HD, :], ACT.Tanh).then_inc(wa_tanh, 1)
            act.wait_ge(c_mixed, 2)
            A(SG[:], SG[:], ACT.Tanh, scale=0.5).then_inc(sg_tanh, 1)
            act.wait_ge(par_ready, 3)
            for t in range(4):
                for i in range(3):
                    c_copy(2 + 3 * t + i)
                act.wait_ge(lora_done, 2 * t + 1)
                if t >= 1:
                    act.wait_ge(rw_elem, t)
                A(halves(tt["LAM"][:]), pst[:, 4:6, 0:HL], ACT.Tanh, scale=0.5, bias=half_wa[:, t:t + 1])\
                    .then_inc(lora_act, 1)
                act.wait_ge(lora_done, 2 * t + 2)
                A(halves(tt["AA"][:]), pst[:, 6:8, 0:HL], ACT.Tanh, scale=0.5, bias=half_wa[:, 4 + t:5 + t])\
                    .then_inc(lora_act, 1)
                nc.scalar.preload_act_table_set("natural_log_exp_and_others")
                act.wait_ge(kkr_ready, t + 1)
                A(tt["SQ"][:], tt["KKR"][:], ACT.Square).then_inc(kksq_ready, 1)
                act.wait_ge(lg_ready, t + 1)
                A(tt["E1"][:], tt["LG"][:], ACT.Exp).then_inc(e_ready, 1)
                A(tt["E2"][:], tt["LGX"][:], ACT.Exp).then_inc(e_ready, 1)
                A(tt["E3"][:], tt["LG"][:], ACT.Exp, scale=-1.0).then_inc(e_ready, 1)
                act.wait_ge(kkclamped, t + 1)
                link(A(tt["RN"][:], tt["RN"][:], ACT.Ln, scale=2.0 ** 20))
                A(tt["RN"][:], tt["RN"][:], ACT.Exp, scale=-0.5, bias=float(10 * np.log(2.0))).then_inc(rn_ready, 1)
                if t < 3:
                    nc.scalar.preload_act_table_set("exp_and_others")

            piece = [FIRST_PIECE[len(PHASE_C)]]

            def pieces(k):
                for _ in range(k):
                    n, part, parts = PIECES[piece[0]]
                    if part == parts - 1:
                        job(n)
                    piece[0] += 1

            def jobs(k):
                n = PIECES[piece[0]][0]
                pieces(FIRST_PIECE.get(n + k, len(PIECES)) - FIRST_PIECE[n])

            def spill_job(n):
                kind, a, b = JOBS[n]
                i, s = SPILL_NO[n], job_slot(n)
                one, buf = pst[:, 2 * s, :], stage[:, i % 2, :]
                if i >= 2:
                    act.wait_ge(spill_out[i % 2], 16 * (i // 2))
                func, scale, rows, to = ACT.Copy, 1.0, P, spill[kind]
                if kind == "bk" or kind == "dk":
                    src, n_ = pair(s), L
                    buf_in = halves(buf)
                    dst = to[:, a, :] if kind == "bk" else to
                else:
                    n_ = T
                    if kind == "rgate":
                        func, scale, dst = ACT.Tanh, 0.5, to[:, b, :]
                    elif kind in ("bv", "dv"):
                        n_ = 2 * P if kind == "bv" else P
                        cols = slice(n_ * a, n_ * a + n_)
                        if b:
                            dst = to[:, b - 1, cols]
                        else:
                            rows, dst = MB, spill[kind + "m"][:, cols]
                    else:
                        dst = to[:, a, :]
                    src, buf_in = one[0:rows, 0:n_], buf[0:rows, 0:n_]
                A(buf_in, src, func, scale=scale).then_inc(spill_copied, 1)
                after_job(n)
                act.wait_ge(spill_copied, i + 1)
                act.dma_start(dst, buf[0:rows, 0:n_]).then_inc(spill_out[i % 2], 16)

            def reload_early():
                act.wait_ge(yl_ready, 4)
                for i in range(2):
                    act.wait_ge(spill_out[i], 16 * (len(SPILL_NO) // 2))
                act.dma_start(gate_t[:], spill["rgate"]).then_inc(gates_in, 16)
                act.dma_start(rk[:], spill["bk"]).then_inc(ret_qk_in, 16)
                act.dma_start(rq[:], spill["bq"]).then_inc(ret_qk_in, 16)
                act.dma_start(rvm[:], spill["bvm"]).then_inc(ret_qk_in, 16)

            def reload_late():
                act.wait_ge(yl_ready, 8)
                act.dma_start(rg[:], spill["bg"]).then_inc(ret_g_in, 16)
                act.dma_start(rv[:], spill["bv"]).then_inc(ret_v_in, 16)
                for tile, name in ((dq, "dq"), (dk, "dk"), (dv, "dv"), (dvm, "dvm")):
                    act.dma_start(tile[:], spill[name]).then_inc(sw_in, 16)

            def job(n):
                kind, a, b = JOBS[n]
                s = job_slot(n)
                one, two = pst[:, 2 * s, :], pair(s)
                if kind in ("aq", "ak", "gate", "up") + SPILLED:
                    act.wait_ge(dense_done, n + 1)
                if kind in SPILLED:
                    spill_job(n)
                    return
                if kind == "aq":
                    A(sb_q[:, a, :], one, ACT.Copy, scale=float(HD) ** -0.5).then_inc(job_out[kind], 1)
                elif kind == "ak":
                    A(halves(sb_k[:, a, :]), two, ACT.Copy).then_inc(job_out[kind], 1)
                elif kind == "gate":
                    i = kind_no(n)
                    act.wait_ge(job_out["proj"], i + 1)
                    A(gate_t[:, b, :], one, ACT.Copy).then_inc(job_out[kind], 1)
                    if b % 4 == 3:
                        nc.scalar.preload_act_table_set("exp_and_others")
                        act.wait_ge(job_out[kind], i + 1)
                        A(gate_t[:, b - 3:b + 1], gate_t[:, b - 3:b + 1], ACT.Tanh, scale=0.5).then_inc(gate_tanh, 1)
                        nc.scalar.preload_act_table_set("natural_log_exp_and_others")
                elif kind == "up":
                    i = kind_no(n)
                    if i >= 2:
                        act.wait_ge(u_lo_ready, i - 1)
                    A(ub[:, i % 2, :], one, ACT.Relu).then_inc(job_out[kind], 1)
                    act.wait_ge(job_out[kind], i + 1)
                    if a == 1 and b == 0:
                        act.wait_ge(dense_done, n)
                    A(u_hi[:, b, :], ub[:, i % 2, :], ACT.Square).then_inc(u_hi_ready, 1)
                after_job(n)

            def sb_meta(grp):
                act.wait_ge(zm_done, grp + 1)
                link(A(sb_em[:], pst[:, 7, :], ACT.Abs))
                link(A(sb_em[:], sb_em[:], ACT.Exp, scale=-1.0))
                A(sb_em[:], sb_em[:], ACT.Ln, bias=1.0).then_inc(zm_ln, 1)

            def sb_pieces(tile):
                return tile[:, 0:T], tile[:, T:SB_N].rearrange("p (a b) -> p a b", a=2)

            def sb_z(h):
                act.wait_ge(z_done, h + 1)
                if h:
                    act.wait_ge(sb_used, h)
                e0, e1 = sb_pieces(sb_e)
                A(e0, pst[:, 4, :], ACT.Abs)
                link(A(e1, pst[:, 5:7, 0:3 * P], ACT.Abs))
                A(e0, e0, ACT.Exp, scale=-1.0)
                link(A(e1, e1, ACT.Exp, scale=-1.0))
                A(e0, e0, ACT.Ln, bias=1.0)
                A(e1, e1, ACT.Ln, bias=1.0).then_inc(z_ln, 1)

            def sb_arg(h):
                act.wait_ge(z_arg, h + 1)
                e0, e1 = sb_pieces(sb_e)
                A(e0, pst[:, 4, :], ACT.Exp)
                A(e1, pst[:, 5:7, 0:3 * P], ACT.Exp).then_inc(z_a, 1)

            def sb_end(grp):
                act.wait_ge(zm_arg, grp + 1)
                A(sb_em[:], pst[:, 7, :], ACT.Exp).then_inc(zm_a, 1)
                for t in (2 * grp, 2 * grp + 1):
                    act.wait_ge(o_done, t + 1)
                    if t == 0:
                        assert PIECES[piece[0]][0] >= y_free(BRANCH_SB)
                        act.wait_ge(dense_done, y_free(BRANCH_SB))
                    A(y_hi[:, t, :], pst[:, 1 + 2 * (t % 2), :], ACT.Copy).then_inc(yh_ready, 1)

            def ret_gate():
                nc.scalar.preload_act_table_set("exp_and_others")
                act.wait_ge(ret_g_in, 16)
                A(rth[:], rg[:], ACT.Tanh, scale=0.5).then_inc(rg_tanh, 1)
                nc.scalar.preload_act_table_set("natural_log_exp_and_others")

            def ret_out(b):
                if b:
                    act.wait_ge(ro_done, b)
                    A(ro[:, :, P * (b - 1):P * b], pst[:, 7 if b % 2 else 1, :].rearrange("p (h i) -> p h i", h=RETH),
                      ACT.Copy).then_inc(ro_ready, 1)

            def ret_square(h):
                act.wait_ge(ro_ready, NB)
                if h >= 2:
                    act.wait_ge(ry_ready, h - 1)
                A(rsq[:, h % 2, :], ro[:, h, :], ACT.Square).then_inc(rsq_ready, 1)

            def ret_norm(h):
                act.wait_ge(rss_done, h + 1)
                link(A(rsq[:, h % 2, :], pst[:, 4 + h % 2, :], ACT.Ln, scale=-1.0 / P, bias=EPS))
                A(rsq[:, h % 2, :], rsq[:, h % 2, :], ACT.Exp, scale=-0.5).then_inc(rrs_ready, 1)
                act.wait_ge(ry_ready, h + 1)
                if h == 0:
                    assert PIECES[piece[0]][0] >= y_free(BRANCH_RET)
                    act.wait_ge(dense_done, y_free(BRANCH_RET))
                A(y_hi[:, h, :], ro[:, h, :], ACT.Copy).then_inc(yh_ready, 1)

            def sw_square(t):
                n = T if t < 4 else L
                src = dq[:, t, :] if t < 4 else dk[:]
                if t == 0:
                    act.wait_ge(yl_ready, 12)
                    act.wait_ge(sw_in, 64)
                if t >= 2:
                    act.wait_ge(dn_ready, t - 1)
                A(dsq[:, t % 2, 0:n], src, ACT.Square).then_inc(dsq_ready, 1)

            def sw_norm(t):
                sq = dsq[:, t % 2, 0:T if t < 4 else L]
                act.wait_ge(dss_done, t + 1)
                ps = pst[:, 4 + t % 2, :] if t < 4 else pst[:, 6:8, 0:HL]
                link(A(sq if t < 4 else halves(sq), ps, ACT.Ln, scale=1.0 / HD, bias=EPS))
                A(sq, sq, ACT.Exp, scale=-0.5).then_inc(drs_ready, 1)

            def sw_keys():
                act.wait_ge(dn_ready, 5)
                for kv in range(2):
                    own, other = slice(HD * kv, HD * kv + HD), slice(HD - HD * kv, P - HD * kv)
                    act.dma_start(dk2[other, kv, :], dk[own, :]).then_inc(dk2_in, 16)

            def sw_probs(b, kv):
                i = 2 * b + kv
                st = dst_[:, i % 2]
                act.wait_ge(dmx_ready, i + 1)
                A(st[:, 2, :], st[:, 2, :], ACT.Exp).then_inc(dexp_ready, 1)
                w = MB + (2 * P if b else P)
                for j in range(4):
                    A(dsc[:, i % 2, j, 0:w], dsc[:, i % 2, j, 0:w], ACT.Exp, bias=st[:, 0, j:j + 1],
                      accum_out=st[:, 1, j:j + 1]).then_inc(dexp_ready, 1)

            def sw_turn(b, kv):
                i = 2 * b + kv
                act.wait_ge(dpt_done, i + 1)
                A(dpt[:, i % 2, 0, :], pst[:, 1, :], ACT.Copy).then_inc(dpt_act, 1)

            def sw_out(b, kv):
                i = 2 * b + kv
                act.wait_ge(do_done, i + 1)
                A(ysw[:, 2 * kv:2 * kv + 2, P * b:P * b + P], pst[:, 6, 0:2 * P].rearrange("p (t q) -> p t q", t=2),
                  ACT.Copy).then_inc(ysw_ready, 1)

            def sw_split():
                assert PIECES[piece[0]][0] >= y_free(BRANCH_SW)
                act.wait_ge(dense_done, y_free(BRANCH_SW))
                act.wait_ge(ysw_ready, 2 * NB)
                for t in range(4):
                    A(y_hi[:, t, :], ysw[:, t, :], ACT.Copy).then_inc(yh_ready, 1)

            def merge_split():
                act.wait_ge(dense_done, JOB_NO[("gate", BRANCH_SW, KD - 1)] + 1)
                for k in range(KD):
                    act.wait_ge(merged_ready, 2 * KD + k + 1)
                    A(h_hi[:, k, 0:T], merged[:, k, :], ACT.Copy, scale=0.5).then_inc(m_hi, 1)
                act.wait_ge(yl_ready, y_count(BRANCH_SW) + 4)
                act.dma_start(x2[:], x[0].rearrange("(b p) d -> p b d", p=P)).then_inc(x2_in, 16)

            def norm2():
                act.wait_ge(m_lo, KD)
                for b in range(NB):
                    act.wait_ge(*all_out("wo", ("wo", 3, b)))
                    A(h2n[:, b, :], x2[:, b, :], ACT.Square, accum_out=ss2[:, 0, b:b + 1]).then_inc(ss2_ready, 1)
                act.wait_ge(ss2_ready, NB)
                link(A(ss2[:, 1, :], ss2[:, 0, :], ACT.Ln, scale=1.0 / D, bias=EPS))
                A(ss2[:, 1, :], ss2[:, 1, :], ACT.Exp, scale=-0.5).then_inc(rs2_ready, 1)
                for k in range(KD):
                    act.wait_ge(h2t_done, k + 1)
                    A(h_hi[:, k, 0:T], pst[:, 4 + k % 4, :], ACT.Copy, scale=PAR("norm2_g", k)).then_inc(h2hi_ready, 1)

            nc.scalar.preload_act_table_set("exp_and_others")
            for b, (n, c0) in enumerate(rw_blocks):
                m = chunks_of(b)[0][2]
                act.wait_ge(tok_done, 4 * b + 1)
                A(FK[0:n, :, 0, :], pst[0:n, 4, :].rearrange("p (h d) -> p h d", h=RWH), ACT.Copy).then_inc(tok_act, 1)
                act.wait_ge(tok_done, 4 * b + 2)
                A(VT[0:n, :], pst[0:n, 5, :], ACT.Copy).then_inc(tok_act, 1)
                fill = RW_FILL[b]
                pieces(fill["score"])
                for l in range(levels_of[b]):
                    for g in range(2 if l else 0):
                        act.wait_ge(c1_done[g], level0[b] + l + 1)
                        A(C1[0:n, 4 * g:4 * g + 4, 0:m], four(pst[0:n, 4 + 2 * g, 0:256])[:, :, 0:m], ACT.Copy)\
                            .then_inc(c1_copied[g], 1)
                    pieces(fill["c1"][l] + fill["tu"][l])
                for g in range(2):
                    act.wait_ge(f_done, 2 * b + g + 1)
                    A(FK[0:n, 4 * g:4 * g + 4, 1, :], four(pst[0:n, 4 + 2 * g, 0:256]), ACT.Copy).then_inc(f_copied, 1)
                pieces(fill["f"] + fill["wz"] + fill["mn"] + fill["end"])
                if b == 0:
                    continue
                for ci in range(2):
                    c = 2 * b - 1 + ci
                    act.wait_ge(q_ready, c)
                    if b == 1 and ci == 0:
                        act.wait_ge(diag_zeroed, 2)
                    if b >= 2:
                        act.wait_ge(yy_done, 2 * (b - 1))
                    for hf in range(2):
                        r = slice(HD * hf, HD * hf + HD)
                        A(QD[r, ci, :, HD * hf:HD * hf + HD], QQ[r, :, :], ACT.Copy).then_inc(qd_ready, 1)
                for ci, (_, col, _) in enumerate(chunks_of(b)):
                    act.wait_ge(yy_done, 2 * (b - 1) + ci + 1)
                    A(KR[:, :, 0, col:col + CH], four(pst[:, 6 + ci, 0:256]), ACT.Copy).then_inc(yy_copied, 1)
            nc.scalar.preload_act_table_set("natural_log_exp_and_others")
            for t in range(4):
                act.wait_ge(postc_ready, t + 1)
                A(post["sq"][:], KR[:, t, 0, MB:L], ACT.Square).then_inc(postq_ready, 1)
                act.wait_ge(postv_done, t + 1)
                link(A(post["rs"][:], pst[:, 7, :], ACT.Ln, scale=1.0 / HD, bias=RW_LN_EPS))
                A(post["rs"][:], post["rs"][:], ACT.Exp, scale=-0.5).then_inc(postr_ready, 1)
                act.wait_ge(yf_ready, t + 1)
                A(y_hi[:, t, :], KR[:, t, 0, MB:L], ACT.Copy).then_inc(yh_ready, 1)

            run_after_rw(pieces, jobs, dict(
                sb_meta=sb_meta, sb_z=sb_z, sb_arg=sb_arg, sb_end=sb_end, ret_gate=ret_gate, ret_out=ret_out,
                ret_square=ret_square, ret_norm=ret_norm, sw_square=sw_square, sw_norm=sw_norm, sw_keys=sw_keys,
                sw_probs=sw_probs, sw_turn=sw_turn, sw_out=sw_out, sw_split=sw_split, merge_split=merge_split,
                norm2=norm2, reload_early=reload_early, reload_late=reload_late))

        @block.vector
        def _(dve):
            steps = [0]

            def link(ins):
                ins.then_inc(dve_step, 1)
                steps[0] += 1
                dve.wait_ge(dve_step, steps[0])

            V = nc.vector
            for b in range(NB + 1):
                r = P if b < NB else MB
                src = xt[:, b, :] if b < NB else xm[:]
                dve.wait_ge(rs_ready, 1 if b < NB else 2)
                V.tensor_scalar(src, src, rs0[0:r, b:b + 1], None, ALU.mult).then_inc(hn_ready, 1)
            dve.wait_ge(const_in, 32)
            a, _ = PARAM_AT["rw_w0"]
            V.tensor_scalar(half_wa[:], par[:, a:a + 8], 0.5, None, ALU.mult).then_inc(par_ready, 1)
            a, _ = PARAM_AT["rw_ka"]
            V.tensor_scalar(one_minus_ka[:], par[:, a:a + 4], -1.0, 1.0, ALU.mult, ALU.add).then_inc(par_ready, 1)
            V.tensor_scalar(gain_q[:], PAR("qn", 0), float(HD) ** -0.5, None, ALU.mult).then_inc(par_ready, 1)
            for k in range(KD):
                dve.wait_ge(hhi_ready, 2 * k + 2)
                V.scalar_tensor_tensor(out=h_lo[:, k, MB:L], in0=pst[:, k % 4, :], scalar=PAR("norm1_g", k),
                                       in1=h_hi[:, k, MB:L].bitcast(F32), op0=ALU.mult, op1=ALU.subtract)\
                    .then_inc(hlo_ready, 1)
                V.scalar_tensor_tensor(out=h_lo[:, k, 0:MB], in0=pst[:, 4 + k % 4, 0:MB], scalar=PAR("norm1_g", k),
                                       in1=h_hi[:, k, 0:MB].bitcast(F32), op0=ALU.mult, op1=ALU.subtract)\
                    .then_inc(hlo_ready, 1)
            dve.wait_ge(ht_done, KD)
            V.memset(cbuf[:, :, 0:1], 0.0).then_inc(cbuf_zeroed, 1)

            def c_mix(i, dst):
                dve.wait_ge(c_copied, i + 1)
                cur = cbuf[:, i % 3, 1:L + 1]
                link(V.tensor_tensor(cdif[:], cbuf[:, i % 3, 0:L], cur, ALU.subtract))
                V.scalar_tensor_tensor(out=dst, in0=cdif[:], scalar=PAR("rw_mu", PHASE_C[i][1]), in1=cur,
                                       op0=ALU.mult, op1=ALU.add).then_inc(c_mixed, 1)
                dve.wait_ge(c_mixed, i + 1)

            c_mix(0, WA[:])
            c_mix(1, SG[:])
            dve.wait_ge(sg_tanh, 1)
            V.tensor_scalar(SG[:], SG[:], 1.0, 0.5, ALU.add, ALU.mult).then_inc(sg_ready, 1)
            for t in range(4):
                LAM, AA, LG, LGX, KKR, T1, SQ, RN, BB, E1, E2, E3 = (tt[k][:] for k in tmp_names)
                kt, rt = KH[:, t, :], KR[:, t, 1, :]
                c_mix(2 + 3 * t, kt)
                V.tensor_scalar(KKR, kt, PAR("rw_kk", t), None, ALU.mult).then_inc(kkr_ready, 1)
                c_mix(3 + 3 * t, rt)
                c_mix(4 + 3 * t, RV[:, t, :])
                if t == 0:
                    dve.wait_ge(table_in, 32)
                dve.wait_ge(lora_act, 2 * t + 1)
                link(V.tensor_scalar(LAM, LAM, 1.0, -0.5 * float(np.exp(-0.5)), ALU.add, ALU.mult))
                link(V.tensor_tensor_scan(LG, C("scan_keep"), LAM, 0.0, ALU.mult, ALU.add))
                V.tensor_tensor(LGX, LG, LAM, ALU.subtract).then_inc(lg_ready, 1)
                dve.wait_ge(lora_act, 2 * t + 2)
                link(V.tensor_scalar(AA, AA, 1.0, 0.5, ALU.add, ALU.mult))
                link(V.tensor_scalar(T1, AA, PAR("rw_ka", t), one_minus_ka[:, t:t + 1], ALU.mult, ALU.add))
                link(V.tensor_tensor(kt, kt, T1, ALU.mult))
                V.scalar_tensor_tensor(out=BON[:, t, :], in0=rt, scalar=PAR("rw_rk", t), in1=kt,
                                       op0=ALU.mult, op1=ALU.mult)
                dve.wait_ge(kksum_done, t + 1)
                V.tensor_scalar(halves(RN), pst[:, 4:6, 0:HL], 1e-24, None, ALU.max).then_inc(kkclamped, 1)
                dve.wait_ge(e_ready, 3 * t + 3)
                V.tensor_copy(GC[:, t, 0:1], E1[:, MB - 1:MB])
                V.tensor_copy(GC[:, t, 1:NCHUNK], E1[:, MB:L].rearrange("p (c s) -> p c s", s=CH)[:, :, CH - 1])
                V.tensor_tensor(kt, kt, E3, ALU.mult)
                link(V.tensor_tensor(rt, rt, E1, ALU.mult))
                dve.wait_ge(rn_ready, t + 1)
                link(V.tensor_tensor(KKR, KKR, RN, ALU.mult))
                link(V.scalar_tensor_tensor(out=BB, in0=KKR, scalar=-1.0, in1=AA, op0=ALU.mult, op1=ALU.mult))
                V.tensor_tensor(KR[:, t, 0, :], KKR, E2, ALU.mult)
                V.tensor_tensor(BH[:, t, :], BB, E3, ALU.mult).then_inc(rw_elem, 1)

            piece = [FIRST_PIECE[len(PHASE_C) + len(PHASE_A)]]

            def pieces(k):
                for _ in range(k):
                    n, part, parts = PIECES[piece[0]]
                    if part == parts - 1:
                        job(n)
                    piece[0] += 1

            def jobs(k):
                n = PIECES[piece[0]][0]
                pieces(FIRST_PIECE.get(n + k, len(PIECES)) - FIRST_PIECE[n])

            def job(n):
                kind, a, b = JOBS[n]
                s = job_slot(n)
                one = pst[:, 2 * s, :]
                if kind in ("av", "proj", "wo"):
                    dve.wait_ge(dense_done, n + 1)
                if kind == "av":
                    cols = slice(2 * P * a, 2 * P * a + 2 * P)
                    if b == 0:
                        dve.wait_ge(yl_ready, 4)
                        V.tensor_copy(sb_vm[:, cols], pst[0:MB, 2 * s, 0:2 * P]).then_inc(job_out[kind], 1)
                    else:
                        V.tensor_copy(sb_v[:, b - 1, cols], pst[:, 2 * s, 0:2 * P]).then_inc(job_out[kind], 1)
                elif kind == "proj":
                    if a == br_order[0]:
                        dve.wait_ge(gates_in, 16)
                    else:
                        dve.wait_ge(gate_tanh, kind_no(n) // 4 - 1)
                    if a == br_order[0]:
                        V.scalar_tensor_tensor(out=merged[:, b, :], in0=gate_t[:, b, :], scalar=1.0, in1=one,
                                               op0=ALU.add, op1=ALU.mult).then_inc(job_out[kind], 1)
                    else:
                        V.scalar_tensor_tensor(out=gtmp[:, b % 2, :], in0=gate_t[:, b, :], scalar=1.0, in1=one,
                                               op0=ALU.add, op1=ALU.mult).then_inc(job_out[kind], 1)
                        dve.wait_ge(job_out[kind], kind_no(n) + 1)
                        V.tensor_tensor(merged[:, b, :], merged[:, b, :], gtmp[:, b % 2, :], ALU.add)\
                            .then_inc(merged_ready, 1)
                elif kind == "wo":
                    dve.wait_ge(x2_in, 16)
                    dst = x2[:, b, 2 * P * a:2 * P * a + 2 * P]
                    V.tensor_tensor(dst, pst[:, 2 * s, 0:2 * P], dst, ALU.add).then_inc(job_out[kind], 1)
                elif kind == "up":
                    i = kind_no(n)
                    r, q = ub[:, i % 2, :], usq[:, i % 2, :]
                    dve.wait_ge(job_out[kind], i + 1)
                    link(V.tensor_tensor(q, r, r, ALU.mult))
                    dve.wait_ge(u_hi_ready, i + 1)
                    V.tensor_tensor(u_lo[:, b, :], q, u_hi[:, b, :].bitcast(F32), ALU.subtract).then_inc(u_lo_ready, 1)
                elif kind == "down":
                    c, kk = b
                    if kk == FH // 2 - 1:
                        dve.wait_ge(dense_done, n + 1)
                        for blk in range(NB):
                            dst = x2[:, blk, T * c:T * c + T]
                            V.tensor_tensor(dst, pst[:, down_bank(c, blk), :], dst, ALU.add)\
                                .then_inc(job_out["down"], 1)

            def sb_keys():
                dve.wait_ge(sb_diag_zeroed, 1)
                dve.wait_ge(*all_out("ak", ("ak", 3, 0)))
                for h in range(SBH):
                    r = slice(HD * (h % 2), HD * (h % 2) + HD)
                    V.tensor_copy(sb_kmd[r, h // 2, MB * (h % 4):MB * (h % 4) + MB], sb_k[r, h // 2, 0:MB])\
                        .then_inc(sb_kmd_ready, 1)

            def sb_meta(grp):
                dve.wait_ge(zm_ln, grp + 1)
                V.scalar_tensor_tensor(out=sb_sm[:], in0=pst[:, 7, :], scalar=0.0, in1=sb_em[:], op0=ALU.max,
                                       op1=ALU.add).then_inc(zm_sp, 1)

            def sb_z(h):
                dve.wait_ge(z_ln, h + 1)
                V.scalar_tensor_tensor(out=sb_s[:, 0:T], in0=pst[:, 4, :], scalar=0.0, in1=sb_e[:, 0:T],
                                       op0=ALU.max, op1=ALU.add)
                V.scalar_tensor_tensor(out=halves(sb_s[:, T:SB_N]), in0=pst[:, 5:7, 0:3 * P], scalar=0.0,
                                       in1=halves(sb_e[:, T:SB_N]), op0=ALU.max, op1=ALU.add).then_inc(z_sp, 1)

            def sb_sums(h):
                dve.wait_ge(z_spm, h + 1)
                V.tensor_copy(sb_cs[:, 0:2 * T].rearrange("p (a b) -> p a b", a=2)[:, :, 0:P],
                              sb_s[:, 0:2 * T].rearrange("p (a b) -> p a b", a=2)[:, :, 0:P])
                c2, c1 = SB_COL[2], SB_COL[1]
                V.tensor_copy(sb_cs[:, c2:c2 + P], sb_s[:, c2:c2 + P])
                link(V.tensor_tensor(sb_cs[:, c2 + P:c2 + 2 * P], sb_s[:, c2 + P:c2 + 2 * P], sb_s[:, SB_COL[3]:SB_N],
                                     ALU.add))
                link(V.tensor_tensor(sb_cs[:, c1 + P:c2], sb_s[:, c1 + P:c2], sb_cs[:, c2:c2 + 2 * P], ALU.add))
                V.tensor_tensor(sb_cs[:, P:T], sb_s[:, P:T], sb_cs[:, c1:c2], ALU.add).then_inc(z_cs, 1)

            def sb_end(grp):
                for t in (2 * grp, 2 * grp + 1):
                    dve.wait_ge(yh_ready, y_count(BRANCH_SB) + t + 1)
                    V.tensor_tensor(y_lo[:, t, :], pst[:, 1 + 2 * (t % 2), :], y_hi[:, t, :].bitcast(F32),
                                    ALU.subtract).then_inc(yl_ready, 1)

            def ret_gate():
                dve.wait_ge(ret_qk_in, 48)
                for t in range(2):
                    V.tensor_tensor(rqd[:, t, :].rearrange("p (b i) -> p b i", b=NB),
                                    rq[:, t, :].rearrange("p (b i) -> p b i", b=NB),
                                    C("ret_qdec", P * t, P * t + P).unsqueeze(1).broadcast_to([P, NB, P]),
                                    ALU.mult).then_inc(rqd_ready, 1)
                dve.wait_ge(rg_tanh, 1)
                V.scalar_tensor_tensor(out=rg[:], in0=rth[:], scalar=1.0, in1=rg[:], op0=ALU.add, op1=ALU.mult)

            def ret_scores(b):
                n = P if b else MB
                dve.wait_ge(rkt_done, b + 1)
                V.tensor_tensor(rkd[0:n], pst[0:n, 4, 0:2 * P].rearrange("p (h d) -> p h d", h=RETH),
                                C("ret_kdec" if b else "ret_kdec_meta", rows=n).unsqueeze(2).broadcast_to([n, RETH, HD]),
                                ALU.mult).then_inc(rkd_ready, 1)
                if b:
                    dve.wait_ge(rs_done, b)
                    m = C("ret_mask").rearrange("p (h i) -> p h i", h=RETH)
                    for par_ in range(2):
                        V.tensor_tensor(rsc[:, par_:RETH:2, :], pst[:, 5 + par_, 0:2 * P].rearrange("p (h i) -> p h i", h=2),
                                        m[:, par_:RETH:2, :], ALU.mult).then_inc(rsc_ready, 1)

            def ret_out(b):
                if b < NB:
                    dve.wait_ge(rkv_done, b + 1)
                    if b == 0:
                        dve.wait_ge(rsz_zeroed, 1)
                    else:
                        dve.wait_ge(ro_done, b)
                    for h in range(RETH):
                        r = slice(HD * (h % 2), HD * (h % 2) + HD)
                        V.scalar_tensor_tensor(out=rsz[r, h, :], in0=rsz[r, h, :], scalar=RET_CHUNK_DECAY[h],
                                               in1=pst[r, 4, 2 * P + P * (h // 2):3 * P + P * (h // 2)],
                                               op0=ALU.mult, op1=ALU.add).then_inc(rstate, 1)
                    dve.wait_ge(rstate, 4 * b + 4)

            def ret_norm(h):
                y = ro[:, h, :]
                dve.wait_ge(rrs_ready, h + 1)
                link(V.tensor_tensor(y, y, rsq[:, h % 2, :], ALU.mult))
                V.scalar_tensor_tensor(out=y, in0=y, scalar=0.5, in1=rg[:, h, :], op0=ALU.mult, op1=ALU.mult)\
                    .then_inc(ry_ready, 1)
                dve.wait_ge(yh_ready, y_count(BRANCH_RET) + h + 1)
                V.tensor_tensor(y_lo[:, h, :], y, y_hi[:, h, :].bitcast(F32), ALU.subtract).then_inc(yl_ready, 1)

            def sw_norm(t):
                dve.wait_ge(drs_ready, t + 1)
                y = dq[:, t, :] if t < 4 else dk[:]
                V.scalar_tensor_tensor(out=y, in0=y, scalar=gain_q[:] if t < 4 else PAR("kn", 0),
                                       in1=dsq[:, t % 2, 0:T if t < 4 else L], op0=ALU.mult, op1=ALU.mult)\
                    .then_inc(dn_ready, 1)

            def sw_keys():
                dve.wait_ge(dn_ready, 5)
                for kv in range(2):
                    own = slice(HD * kv, HD * kv + HD)
                    V.tensor_copy(dk2[own, kv, :], dk[own, :]).then_inc(dk2_own, 1)

            def sw_scores(b, kv):
                i = 2 * b + kv
                w = MB + (2 * P if b else P)
                st = dst_[:, i % 2]
                if i >= 2:
                    dve.wait_ge(dpt_done, i - 1)
                for j in range(4):
                    h = 4 * kv + j
                    dve.wait_ge(ds_done, 4 * i + j + 1)
                    slope = 2.0 ** (-8.0 * (h + 1) / SWH)
                    if b:
                        V.scalar_tensor_tensor(out=dsc[:, i % 2, j, 0:w], in0=C("sw_bias"), scalar=slope,
                                               in1=pst[:, 4 + j, 0:w], op0=ALU.mult, op1=ALU.add).then_inc(ds_read, 1)
                    else:
                        V.scalar_tensor_tensor(out=dsc[:, i % 2, j, 0:MB], in0=C("sw_bias", 0, MB), scalar=slope,
                                               in1=pst[:, 4 + j, 0:MB], op0=ALU.mult, op1=ALU.add)
                        V.scalar_tensor_tensor(out=dsc[:, i % 2, j, MB:w], in0=C("sw_bias", MB + P, MB + 2 * P),
                                               scalar=slope, in1=pst[:, 4 + j, MB:w], op0=ALU.mult, op1=ALU.add)\
                            .then_inc(ds_read, 1)
                dve.wait_ge(ds_read, 4 * i + 4)
                sink = par[:, PARAM_AT["sink"][0] + 4 * kv:PARAM_AT["sink"][0] + 4 * kv + 4]
                link(V.tensor_reduce(st[:, 0, :], dsc[:, i % 2, :, 0:w], AX.X, ALU.max))
                link(V.tensor_tensor(st[:, 0, :], st[:, 0, :], sink, ALU.max))
                link(V.tensor_scalar(st[:, 0, :], st[:, 0, :], -1.0, None, ALU.mult))
                V.tensor_tensor(st[:, 2, :], st[:, 0, :], sink, ALU.add).then_inc(dmx_ready, 1)

            def sw_probs(b, kv):
                i = 2 * b + kv
                w = MB + (2 * P if b else P)
                st = dst_[:, i % 2]
                dve.wait_ge(dexp_ready, 5 * i + 5)
                link(V.tensor_tensor(st[:, 3, :], st[:, 1, :], st[:, 2, :], ALU.add))
                link(V.reciprocal(st[:, 4, :], st[:, 3, :]))
                V.tensor_tensor(dsc[:, i % 2, :, 0:w], dsc[:, i % 2, :, 0:w],
                                st[:, 4, :].unsqueeze(2).broadcast_to([P, 4, w]), ALU.mult).then_inc(dp_ready, 1)

            def sw_turn(b, kv):
                i = 2 * b + kv
                dve.wait_ge(dpt_done, i + 1)
                if b:
                    V.tensor_copy(dpt[:, i % 2, 1, :], pst[:, 3, :])
                V.tensor_copy(dpt[0:MB, i % 2, 2, :], pst[0:MB, 7, :]).then_inc(dpt_dve, 1)

            def sw_split():
                for t in range(4):
                    dve.wait_ge(yh_ready, y_count(BRANCH_SW) + t + 1)
                    V.tensor_tensor(y_lo[:, t, :], ysw[:, t, :], y_hi[:, t, :].bitcast(F32), ALU.subtract)\
                        .then_inc(yl_ready, 1)

            def merge_split():
                for k in range(KD):
                    dve.wait_ge(m_hi, k + 1)
                    dve.wait_ge(merged_ready, 3 * KD)
                    V.scalar_tensor_tensor(out=h_lo[:, k, 0:T], in0=merged[:, k, :], scalar=0.5,
                                           in1=h_hi[:, k, 0:T].bitcast(F32), op0=ALU.mult, op1=ALU.subtract)\
                        .then_inc(m_lo, 1)

            def norm2():
                dve.wait_ge(rs2_ready, 1)
                for b in range(NB):
                    V.tensor_scalar(h2n[:, b, :], x2[:, b, :], ss2[:, 1, b:b + 1], None, ALU.mult).then_inc(h2n_ready, 1)
                for k in range(KD):
                    dve.wait_ge(h2hi_ready, k + 1)
                    V.scalar_tensor_tensor(out=h_lo[:, k, 0:T], in0=pst[:, 4 + k % 4, :], scalar=PAR("norm2_g", k),
                                           in1=h_hi[:, k, 0:T].bitcast(F32), op0=ALU.mult, op1=ALU.subtract)\
                        .then_inc(h2lo_ready, 1)

            dve.wait_ge(table_in, 32)
            for b, (n, c0) in enumerate(rw_blocks):
                m = chunks_of(b)[0][2]
                dve.wait_ge(tok_done, 4 * b + 3)
                V.tensor_copy(KT[0:n, :], pst[0:n, 6, :]).then_inc(tok_dve, 1)
                dve.wait_ge(tok_done, 4 * b + 4)
                V.tensor_copy(BT[0:n, :], pst[0:n, 7, :]).then_inc(tok_dve, 1)
                for g in range(2):
                    for par_ in range(2):
                        dve.wait_ge(am_done, 4 * b + 2 * g + par_ + 1)
                        V.tensor_tensor(
                            AM[0:n, 4 * g + par_:4 * g + 4:2, :, 0:m],
                            pst[0:n, 4 + 2 * g + par_, :].rearrange("p (h q c) -> p h q c", h=2, q=4)[:, :, :, 0:m],
                            four(C("rw_mask", rows=n))[:, :, 0:m].unsqueeze(1).broadcast_to([n, 2, 4, m]),
                            ALU.mult).then_inc(am_ready, 1)
                idb = C("ident_chunk", 0, m, n).unsqueeze(1).broadcast_to([n, 4, m])
                for l in range(levels_of[b]):
                    for g in range(2):
                        hs = slice(4 * g, 4 * g + 4)
                        step = level0[b] + l
                        if l == 0:
                            dve.wait_ge(m_ready[g], step + 1)
                            V.tensor_tensor(XX[0:n, hs, 0:m], MM[0:n, step % 2, hs, 0:m], idb, ALU.add)
                            dve.wait_ge(c1_done[g], step + 1)
                            V.tensor_tensor(TT[0:n, hs, 0:m], four(pst[0:n, 4 + 2 * g, 0:256])[:, :, 0:m],
                                            idb, ALU.add).then_inc(x_ready[g], 1)
                            dve.wait_ge(x_ready[g], step + 1)
                            continue
                        dve.wait_ge(tu_done[g], step - b)
                        if l < levels_of[b] - 1:
                            V.tensor_tensor(TT[0:n, hs, 0:m], TT[0:n, hs, 0:m],
                                            four(pst[0:n, 4 + 2 * g, 256:512])[:, :, 0:m], ALU.add)
                        V.tensor_tensor(XX[0:n, hs, 0:m], XX[0:n, hs, 0:m],
                                        four(pst[0:n, 5 + 2 * g, 0:256])[:, :, 0:m], ALU.add).then_inc(x_ready[g], 1)
                        dve.wait_ge(x_ready[g], step + 1)
                for g in range(2):
                    dve.wait_ge(wz_done, 2 * b + g + 1)
                    V.tensor_copy(FK[0:n, 4 * g:4 * g + 4, :, :],
                                  pst[0:n, 5 + 2 * g, :].rearrange("p (h a d) -> p h a d", h=4, a=2)).then_inc(wz_ready, 1)
                for g in range(2):
                    ts = slice(2 * g, 2 * g + 2)
                    for ci, (_, col, _) in enumerate(chunks_of(b)):
                        c = 2 * b - 1 + ci if b else 0
                        bank = 4 + 2 * g + ci
                        dve.wait_ge(mn_done, 2 + 4 * (b - 1) + 2 * g + ci + 1 if b else g + 1)
                        gcb = GC[:, ts, c:c + 1].broadcast_to([P, 2, HD])
                        nps = pst[:, bank, 256:384].rearrange("p (h d) -> p h d", h=2)
                        if b == 0:
                            V.tensor_tensor(QQ[:, ts, :], nps, gcb, ALU.mult).then_inc(q_ready if g else mn_ready, 1)
                            continue
                        rr = KR[:, ts, 1, col:col + CH]
                        V.tensor_tensor(rr, rr, pst[:, bank, 0:128].rearrange("p (h d) -> p h d", h=2), ALU.add)
                        for hf in range(2):
                            r = slice(HD * hf, HD * hf + HD)
                            V.tensor_tensor(MD[r, ci, ts, HD * hf:HD * hf + HD],
                                            pst[r, bank, 128:256].rearrange("p (h d) -> p h d", h=2),
                                            C("ident_chunk")[r].unsqueeze(1).broadcast_to([HD, 2, HD]), ALU.add)
                        V.tensor_tensor(NG[:, ci, ts, :], nps, gcb, ALU.mult).then_inc(mn_ready, 1)
                if b == 0:
                    dve.wait_ge(q_ready, 1)
                    dve.wait_ge(diag_zeroed, 2)
                    continue
                for ci in range(2):
                    c = 2 * b - 1 + ci
                    if c == NCHUNK - 1:
                        continue
                    dve.wait_ge(qn_done, c)
                    dve.wait_ge(qd_ready, 2 * c)
                    dve.wait_ge(mn_ready, 1 + 4 * b)
                    link(V.tensor_tensor(QQ[:], four(pst[:, 4 + ci, 0:256]),
                                         GC[:, :, c:c + 1].broadcast_to([P, 4, HD]), ALU.mult))
                    V.tensor_tensor(QQ[:], QQ[:], NG[:, ci], ALU.add).then_inc(q_ready, 1)
                    dve.wait_ge(q_ready, c + 1)
            for t in range(4):
                y = KR[:, t, 0, MB:L]
                dve.wait_ge(post_done, 3 * t + 1)
                V.scalar_tensor_tensor(out=y, in0=pst[:, 4, :], scalar=-1.0 / HD, in1=y, op0=ALU.mult,
                                       op1=ALU.add).then_inc(postc_ready, 1)
                dve.wait_ge(post_done, 3 * t + 2)
                V.tensor_tensor(post["bon"][:], pst[:, 5, :], RV[:, t, MB:L], ALU.mult)
                dve.wait_ge(postr_ready, t + 1)
                link(V.tensor_tensor(y, y, post["rs"][:], ALU.mult))
                link(V.tensor_scalar(y, y, PAR("rw_ln_g", t), PAR("rw_ln_b", t), ALU.mult, ALU.add))
                link(V.tensor_tensor(y, y, post["bon"][:], ALU.add))
                dve.wait_ge(post_done, 3 * t + 3)
                V.tensor_tensor(y, y, pst[:, 6, :], ALU.mult).then_inc(yf_ready, 1)
                dve.wait_ge(yh_ready, t + 1)
                if t == 0:
                    for i in range(2):
                        dve.wait_ge(spill_out[i], 16 * (len(SPILL_NO) // 2))
                V.tensor_tensor(y_lo[:, t, :], y, y_hi[:, t, :].bitcast(F32), ALU.subtract).then_inc(yl_ready, 1)

            run_after_rw(pieces, jobs, dict(
                sb_keys=sb_keys, sb_meta=sb_meta, sb_z=sb_z, sb_sums=sb_sums, sb_end=sb_end, ret_gate=ret_gate,
                ret_scores=ret_scores, ret_out=ret_out, ret_norm=ret_norm, sw_norm=sw_norm, sw_keys=sw_keys,
                sw_scores=sw_scores, sw_probs=sw_probs, sw_turn=sw_turn, sw_split=sw_split,
                merge_split=merge_split, norm2=norm2))

        @block.tensor
        def _(pe):
            M = nc.tensor.matmul

            def wslice(tile, u, k):
                return tile[:, u % W_SLOTS, P * k:P * k + P]

            def product3(out, terms, first=True, final=True):
                for i, ((lh, ll), (rh, rl)) in enumerate(terms):
                    M(out, lh, rh, start=(first and i == 0), stop=False)
                    M(out, lh, rl, start=False, stop=False)
                    last = M(out, ll, rh, start=False, stop=(final and i == len(terms) - 1))
                return last

            def job_begin(n):
                s = job_slot(n)
                if n >= 2:
                    pe.wait_ge(*emptied(n - 2))
                pe.wait_ge(lo_ready, UNIT_NO[units_of(JOBS[n])[-1]] + 1)
                return s

            def feature_job(job, cols, part=0, parts=1):
                n = JOBN[job]
                s = job_begin(n) if part == 0 else job_slot(n)
                u = UNIT_NO[units_of(job)[0]]
                for i, (c0, c1) in enumerate(cols):
                    if len(cols) == parts == 2 and i != part:
                        continue
                    ks = range(KD) if len(cols) == 2 else range(KD * part // parts, KD * (part + 1) // parts)
                    last = product3(pst[:, 2 * s + i, 0:c1 - c0],
                                    [((wslice(w_hi, u, k), wslice(w_lo, u, k)),
                                      (h_hi[:, k, c0:c1], h_lo[:, k, c0:c1])) for k in ks],
                                    ks[0] == 0, ks[-1] == KD - 1)
                if part == parts - 1:
                    last.then_inc(dense_done, 1)

            ALL = [(0, HL), (HL, L)]
            pe.wait_ge(const_in, 32)
            pe.wait_ge(hn_ready, NB + 1)
            for k in range(KD):
                if k >= 4:
                    pe.wait_ge(hlo_ready, 2 * (k - 4) + 2)
                nc.tensor.transpose(pst[:, 4 + k % 4, 0:MB], xm[:, P * k:P * k + P], cst[0:MB, 0:MB])
                for b in range(NB):
                    last = nc.tensor.transpose(pst[:, k % 4, P * b:P * b + P], xt[:, b, P * k:P * k + P], ident)
                last.then_inc(ht_done, 1)
            pe.wait_ge(hlo_ready, 2 * KD)

            def lora(t):
                if t == 0:
                    pe.wait_ge(wa_tanh, 1)
                    pe.wait_ge(table_in, 32)
                else:
                    pe.wait_ge(kkclamped, t)
                    pe.wait_ge(lora_act, 2 * t)
                for i in range(2):
                    last = M(pst[:, 4 + i, 0:HL], w2[:, P * t:P * t + P], WA[0:HD, HL * i:HL * i + HL],
                             start=True, stop=True)
                last.then_inc(lora_done, 1)
                for i in range(2):
                    last = M(pst[:, 6 + i, 0:HL], a2[:, P * t:P * t + P], WA[HD:P, HL * i:HL * i + HL],
                             start=True, stop=True)
                last.then_inc(lora_done, 1)

            def kksum(t):
                pe.wait_ge(kksq_ready, t + 1)
                pe.wait_ge(lora_act, 2 * t + 1)
                for i in range(2):
                    last = M(pst[:, 4 + i, 0:HL], headsum, tt["SQ"][:, HL * i:HL * i + HL], start=True, stop=True)
                last.then_inc(kksum_done, 1)

            feature_job(PHASE_C[0], ALL)
            feature_job(PHASE_C[1], ALL)
            for t in range(4):
                for i in range(3):
                    feature_job(PHASE_C[2 + 3 * t + i], ALL)
                    if t >= 1 and i == 0:
                        kksum(t - 1)
                lora(t)
            kksum(3)

            piece = [FIRST_PIECE[len(PHASE_C)]]

            def pieces(k):
                for _ in range(k):
                    n, part, parts = PIECES[piece[0]]
                    job(n, part, parts)
                    piece[0] += 1

            def jobs(k):
                n = PIECES[piece[0]][0]
                pieces(FIRST_PIECE.get(n + k, len(PIECES)) - FIRST_PIECE[n])

            def job(n, part, parts):
                kind, a, b = JOBS[n]
                u = UNIT_NO[units_of(JOBS[n])[0]]
                if kind in ("aq", "bq", "bg", "dq", "gate", "rgate"):
                    feature_job(JOBS[n], [(MB, L)], part, parts)
                elif kind in ("ak", "bk", "dk"):
                    feature_job(JOBS[n], ALL, part, parts)
                elif kind in ("av", "bv", "dv"):
                    s = job_begin(n)
                    r, toks = (P, slice(MB + P * (b - 1), MB + P * b)) if b else (MB, slice(0, MB))
                    us = u % W_SLOTS
                    if kind == "dv":
                        o = pst[0:r, 2 * s, 0:P]
                        wsl = lambda w, k: wslice(w, u, k)
                    else:
                        o = pst[0:r, 2 * s, 0:2 * P].rearrange("p (a f) -> p a f", a=2)
                        wsl = lambda w, k: w[:, us:us + 2, P * k:P * k + P]
                    product3(o, [((h_hi[:, k, toks], h_lo[:, k, toks]), (wsl(w_hi, k), wsl(w_lo, k)))
                                 for k in range(KD)]).then_inc(dense_done, 1)
                elif kind == "proj":
                    s = job_begin(n)
                    pe.wait_ge(yl_ready, y_count(a) + 4)
                    us = u % W_SLOTS
                    ws = [slice(2 * P * k + P * (b % 2), 2 * P * k + P * (b % 2) + P) for k in range(4)]
                    product3(pst[:, 2 * s, :], [((w_hi[:, us, ws[k]], w_lo[:, us, ws[k]]), (y_hi[:, k, :], y_lo[:, k, :]))
                                                for k in range(4)]).then_inc(dense_done, 1)
                elif kind == "wo":
                    s = job_begin(n)
                    pe.wait_ge(m_lo, KD)
                    us = u % W_SLOTS
                    toks = slice(P * b, P * b + P)
                    product3(pst[:, 2 * s, 0:2 * P].rearrange("p (a f) -> p a f", a=2),
                             [((h_hi[:, k, toks], h_lo[:, k, toks]),
                               (w_hi[:, us:us + 2, P * k:P * k + P], w_lo[:, us:us + 2, P * k:P * k + P]))
                              for k in range(KD)]).then_inc(dense_done, 1)
                elif kind == "up":
                    if a == 1 and b < 2:
                        pe.wait_ge(job_out["down"], 8)
                    s = job_begin(n)
                    product3(pst[:, 2 * s, :], [((wslice(w_hi, u, k), wslice(w_lo, u, k)),
                                                 (h_hi[:, k, 0:T], h_lo[:, k, 0:T])) for k in range(KD)])\
                        .then_inc(dense_done, 1)
                elif kind == "down":
                    c, kk = b
                    if kk == 0:
                        pe.wait_ge(u_lo_ready, FH * (a + 1))
                        if a == 1:
                            pe.wait_ge(job_out["down"], 8)
                    pe.wait_ge(lo_ready, u + 1)
                    us = u % W_SLOTS
                    for j in range(2):
                        f = 2 * kk + j
                        ws = slice(T * j, T * j + T)
                        for blk in range(NB):
                            o = pst[:, down_bank(c, blk), :]
                            toks = slice(P * blk, P * blk + P)
                            M(o, u_hi[:, f, toks], w_hi[:, us, ws], start=(f == 0), stop=False)
                            M(o, u_hi[:, f, toks], w_lo[:, us, ws], start=False, stop=False)
                            last = M(o, u_lo[:, f, toks], w_hi[:, us, ws], start=False, stop=(f == FH - 1))
                    last.then_inc(dense_done, 1)

            def sb_rows(h):
                return slice(HD * (h % 2), HD * (h % 2) + HD)

            def sb_meta(grp):
                if grp == 0:
                    pe.wait_ge(sb_kmd_ready, SBH)
                else:
                    pe.wait_ge(zm_a, grp)
                for t in (2 * grp, 2 * grp + 1):
                    last = M(pst[:, 7, :], sb_kmd[:, t, :], sb_q[:, t, :], start=(t == 2 * grp), stop=(t == 2 * grp + 1))
                last.then_inc(zm_done, 1)

            SB_AT = [(4, 0), (5, 0), (6, 0), (6, 2 * P)]

            def sb_z(h):
                if h:
                    pe.wait_ge(z_a, h)
                r = sb_rows(h)
                for kb in range(NB):
                    bank, c = SB_AT[kb]
                    last = M(pst[:, bank, c:c + T - P * kb], sb_k[r, h // 2, MB + P * kb:MB + P * kb + P],
                             sb_q[r, h // 2, P * kb:T], start=(kb < 3), stop=True, skip_group_check=(kb == 3))
                last.then_inc(z_done, 1)

            def sb_arg(h):
                pe.wait_ge(z_cs, h + 1)
                for kb in range(NB):
                    bank, c = SB_AT[kb]
                    w = SBW[kb]
                    last = M(pst[:, bank, c:c + w], C("suffix"), sb_s[:, SB_COL[kb]:SB_COL[kb] + w], start=False,
                             stop=True, skip_group_check=True)
                    if kb < 3:
                        rhs = (sb_s if kb == 2 else sb_cs)[:, SB_COL[kb + 1]:SB_COL[kb + 1] + w - P]
                        last = M(pst[:, bank, c + P:c + w], C("neg_ones"), rhs, start=False, stop=True,
                                 skip_group_check=True)
                last.then_inc(z_arg, 1)
                grp, j = h // 4, h % 4
                if j == 0:
                    pe.wait_ge(zm_sp, grp + 1)
                    M(pst[:, 7, :], C("suffix_meta"), sb_sm[:], start=False, stop=True, skip_group_check=True)
                o = 3 * MB - MB * j
                last = M(pst[:, 7, :], C("carry_meta", o, o + P), sb_cs[:, 0:T], start=False, stop=True,
                         skip_group_check=True)
                if j == 3:
                    last.then_inc(zm_arg, 1)

            def sb_o(h):
                pe.wait_ge(z_am, h + 1)
                grp, t = h // 4, h // 2
                if h % 4 == 0 and grp:
                    pe.wait_ge(yl_ready, y_count(BRANCH_SB) + 2 * grp)
                if h == 0:
                    pe.wait_ge(*all_out("av", ("av", 1, NB)))
                r = sb_rows(h)
                bank = 1 + 2 * (t % 2)
                for kb in range(NB):
                    last = M(pst[r, bank, P * kb:T], sb_v[:, kb, HD * h:HD * h + HD],
                             sb_e[:, SB_COL[kb]:SB_COL[kb] + SBW[kb]],
                             start=(kb == 0), stop=False)
                last.then_inc(sb_used, 1)

            def sb_end(grp):
                pe.wait_ge(sb_vmd_ready, 16 * SBH)
                pe.wait_ge(zm_a, grp + 1)
                for h in range(4 * grp, 4 * grp + 4):
                    last = M(pst[sb_rows(h), 1 + 2 * (h // 2 % 2), :], sb_vmd[:, h, :], sb_em[:], start=False, stop=True)
                    if h % 2:
                        last.then_inc(o_done, 1)

            def ret_scores(b):
                n, c0 = rw_blocks[b]
                toks = slice(c0, c0 + n)
                if b == 0:
                    pe.wait_ge(ret_qk_in, 48)
                    pe.wait_ge(yl_ready, y_count(BRANCH_RET))
                else:
                    pe.wait_ge(rstate, 4 * b)
                for t in range(2):
                    last = nc.tensor.transpose(pst[0:n, 4, P * t:P * t + P], rk[:, t, toks], ident)
                last.then_inc(rkt_done, 1)
                if b:
                    if b > 1:
                        pe.wait_ge(rsc_ready, 2 * (b - 1))
                    for h in range(RETH):
                        r = slice(HD * (h % 2), HD * (h % 2) + HD)
                        last = M(pst[:, 5 + h % 2, P * (h // 2):P * (h // 2) + P], rk[r, h // 2, toks],
                                 rq[r, h // 2, P * (b - 1):P * b], start=True, stop=True)
                    last.then_inc(rs_done, 1)

            def ret_out(b):
                n, c0 = rw_blocks[b]
                if b < NB:
                    pe.wait_ge(rkd_ready, b + 1)
                    if b == 0:
                        pe.wait_ge(ret_v_in, 16)
                    vv = rv[:, b - 1, :] if b else rvm[:]
                    for h in range(RETH):
                        last = M(pst[HD * (h % 2):HD * (h % 2) + HD, 4, 2 * P + P * (h // 2):3 * P + P * (h // 2)],
                                 rkd[0:n, h, :], vv[:, P * h:P * h + P], start=True, stop=True)
                    last.then_inc(rkv_done, 1)
                if b:
                    pe.wait_ge(rsc_ready, 2 * b)
                    if b == 1:
                        pe.wait_ge(rqd_ready, 2)
                    if b >= 3:
                        pe.wait_ge(ro_ready, b - 2)
                    for h in range(RETH):
                        o = pst[:, 7 if b % 2 else 1, P * h:P * h + P]
                        M(o, rv[:, b - 1, P * h:P * h + P], rsc[:, h, :], start=True, stop=False)
                        last = M(o, rsz[:, h, :], rqd[:, h // 2, P * (b - 1):P * b], start=False, stop=True)
                    last.then_inc(ro_done, 1)

            def ret_square(h):
                pe.wait_ge(rsq_ready, h + 1)
                M(pst[:, 4 + h % 2, :], C("neg_ones"), rsq[:, h % 2, :], start=True, stop=True).then_inc(rss_done, 1)

            def sw_square(t):
                pe.wait_ge(dsq_ready, t + 1)
                if t < 4:
                    last = M(pst[:, 4 + t % 2, :], headsum, dsq[:, t % 2, 0:T], start=True, stop=True)
                else:
                    for i in range(2):
                        last = M(pst[:, 6 + i, 0:HL], headsum, dsq[:, t % 2, HL * i:HL * i + HL], start=True, stop=True)
                last.then_inc(dss_done, 1)

            def sw_scores(b, kv):
                i = 2 * b + kv
                if i == 0:
                    pe.wait_ge(dn_ready, 5)
                    pe.wait_ge(dk2_own, 2)
                    pe.wait_ge(dk2_in, 32)
                else:
                    pe.wait_ge(dpt_dve, i)
                    pe.wait_ge(ysw_ready, i)
                for j in range(4):
                    h = 4 * kv + j
                    r = slice(HD * (h % 2), HD * (h % 2) + HD)
                    q = dq[r, h // 2, P * b:P * b + P]
                    if b:
                        M(pst[:, 4 + j, 0:MB], q, dk2[r, kv, 0:MB], start=True, stop=True)
                        last = M(pst[:, 4 + j, MB:MB + 2 * P], q, dk2[r, kv, MB + P * (b - 1):MB + P * (b + 1)],
                                 start=True, stop=True)
                    else:
                        last = M(pst[:, 4 + j, 0:MB + P], q, dk2[r, kv, 0:MB + P], start=True, stop=True)
                    last.then_inc(ds_done, 1)

            def sw_turn(b, kv):
                i = 2 * b + kv
                pe.wait_ge(dp_ready, i + 1)
                own = MB + (P if b else 0)
                if i:
                    pe.wait_ge(dpt_act, i)
                for j in range(4):
                    p_ = dsc[:, i % 2, j, :]
                    c = slice(P * j, P * j + P)
                    nc.tensor.transpose(pst[:, 1, c], p_[:, own:own + P], ident)
                    if b:
                        nc.tensor.transpose(pst[:, 3, c], p_[:, MB:MB + P], ident)
                    last = nc.tensor.transpose(pst[0:MB, 7, c], p_[:, 0:MB], ident)
                last.then_inc(dpt_done, 1)

            def sw_out(b, kv):
                i = 2 * b + kv
                pe.wait_ge(dpt_act, i + 1)
                pe.wait_ge(dpt_dve, i + 1)
                if i == 0:
                    pe.wait_ge(sw_in, 64)
                vc = slice(HD * kv, HD * kv + HD)
                for par_ in range(2):
                    o = pst[HD * par_:HD * par_ + HD, 6, 0:2 * P].rearrange("p (t q) -> p t q", t=2)

                    def pick(which, rows=P):
                        return dpt[0:rows, i % 2, which, :].rearrange("p (t s q) -> p s t q", t=2, s=2)[:, par_]
                    M(o, dv[:, b, vc], pick(0), start=True, stop=False)
                    if b:
                        M(o, dv[:, b - 1, vc], pick(1), start=False, stop=False)
                    last = M(o, dvm[:, vc], pick(2, MB), start=False, stop=True)
                last.then_inc(do_done, 1)

            def norm2():
                pe.wait_ge(h2n_ready, NB)
                for k in range(KD):
                    if k >= 4:
                        pe.wait_ge(h2lo_ready, k - 3)
                    for b in range(NB):
                        last = nc.tensor.transpose(pst[:, 4 + k % 4, P * b:P * b + P], h2n[:, b, P * k:P * k + P], ident)
                    last.then_inc(h2t_done, 1)
                pe.wait_ge(h2lo_ready, KD)

            pe.wait_ge(rw_elem, 4)
            for b, (n, c0) in enumerate(rw_blocks):
                toks = slice(c0, c0 + n)
                chunks = chunks_of(b)
                m = chunks[0][2]
                for q, tile in enumerate((lambda t: KR[:, t, 0, toks], lambda t: RV[:, t, toks],
                                          lambda t: KH[:, t, toks], lambda t: BH[:, t, toks])):
                    if b >= 1:
                        pe.wait_ge(mn_ready, 1 + 4 * (b - 1))
                        pe.wait_ge(q_ready, min(2 * b - 1, NCHUNK - 1))
                    if q == 2 and b >= 2:
                        pe.wait_ge(yy_copied, 2 * (b - 1))
                    for t in range(4):
                        last = nc.tensor.transpose(pst[0:n, 4 + q, P * t:P * t + P], tile(t), ident)
                    last.then_inc(tok_done, 1)
                fill = RW_FILL[b]
                pe.wait_ge(tok_act, 2 * b + 2)
                pe.wait_ge(tok_dve, 2 * b + 2)
                for g in range(2):
                    for ab, keys in ((0, KH), (1, BH)):
                        for t in (2 * g, 2 * g + 1):
                            for par_ in range(2):
                                r = slice(HD * par_, HD * par_ + HD)
                                o = 256 * (t % 2) + 128 * ab
                                for rows, col, _ in chunks:
                                    last = M(pst[rows, 4 + 2 * g + par_, o:o + 128]
                                             .rearrange("p (a c) -> p a c", a=2)[:, :, 0:m],
                                             keys[r, t, col:col + m], KR[r, t, :, col:col + m], start=True, stop=True)
                                if ab == 1 and t % 2:
                                    last.then_inc(am_done, 1)
                    if g == 0:
                        pieces(fill["score"])
                for l in range(levels_of[b]):
                    step = level0[b] + l
                    for g in range(2):
                        pe.wait_ge(m_ready[g], step + 1)
                        if l:
                            pe.wait_ge(x_ready[g], step)
                        for h in range(4 * g, 4 * g + 4):
                            o = CH * (h % 4)
                            for rows, _, _ in chunks:
                                last = M(pst[rows, 4 + 2 * g, o:o + m], MM[rows, step % 2, h, 0:m],
                                         TT[rows, h, 0:m] if l else C("ident_chunk", 0, m)[rows],
                                         start=True, stop=True)
                        last.then_inc(c1_done[g], 1)
                    pieces(fill["c1"][l])
                    for g in range(2 if l else 0):
                        pe.wait_ge(c1_copied[g], step - b)
                        for h in range(4 * g, 4 * g + 4):
                            o = CH * (h % 4)
                            if l < levels_of[b] - 1:
                                for rows, _, _ in chunks:
                                    M(pst[rows, 4 + 2 * g, 256 + o:256 + o + m], XX[rows, h, 0:m], C1[rows, h, 0:m],
                                      start=True, stop=True)
                        for h in range(4 * g, 4 * g + 4):
                            o = CH * (h % 4)
                            for rows, _, _ in chunks:
                                last = M(pst[rows, 5 + 2 * g, o:o + m], C1[rows, h, 0:m], XX[rows, h, 0:m],
                                         start=True, stop=True)
                        last.then_inc(tu_done[g], 1)
                    pieces(fill["tu"][l])
                for g in range(2):
                    pe.wait_ge(x_ready[g], level0[b] + levels_of[b])
                    for h in range(4 * g, 4 * g + 4):
                        for rows, _, _ in chunks:
                            last = M(pst[rows, 4 + 2 * g, HD * (h % 4):HD * (h % 4) + HD], AM[rows, h, 0, 0:m],
                                     VT[rows, HD * h:HD * h + HD], start=True, stop=True)
                    last.then_inc(f_done, 1)
                pieces(fill["f"])
                for g in range(2):
                    pe.wait_ge(f_copied, 2 * b + g + 1)
                    for h in range(4 * g, 4 * g + 4):
                        for rows, _, _ in chunks:
                            last = M(pst[rows, 5 + 2 * g, P * (h % 4):P * (h % 4) + P].rearrange("p (a d) -> p a d", a=2),
                                     XX[rows, h, 0:m], FK[rows, h, :, :], start=True, stop=True)
                    last.then_inc(wz_done, 1)
                pieces(fill["wz"])
                for g in range(2):
                    pe.wait_ge(wz_ready, 2 * b + g + 1)
                    for ci, (rows, _, _) in enumerate(chunks):
                        bank = 4 + 2 * g + ci
                        for h in range(4 * g, 4 * g + 4):
                            out_rows = slice(HD * (h % 2), HD * (h % 2) + HD)
                            cc = HD * (h // 2 % 2)
                            hc = slice(HD * h, HD * h + HD)
                            if b:
                                M(pst[out_rows, bank, cc:cc + CH], FK[rows, h, 0, :], AM[rows, h, 3, :],
                                  start=True, stop=True)
                                M(pst[out_rows, bank, 128 + cc:128 + cc + HD], FK[rows, h, 0, :], BT[rows, hc],
                                  start=True, stop=True)
                            M(pst[out_rows, bank, 256 + cc:256 + cc + HD], KT[rows, hc], VT[rows, hc],
                              start=True, stop=False)
                            last = M(pst[out_rows, bank, 256 + cc:256 + cc + HD], BT[rows, hc], FK[rows, h, 1, :],
                                     start=False, stop=True)
                        last.then_inc(mn_done, 1)
                    pieces(fill["end" if g else "mn"])
                if b == 0:
                    continue
                pe.wait_ge(mn_ready, 1 + 4 * b)
                for ci, (rows, _, _) in enumerate(chunks):
                    for h in range(RWH):
                        dst = pst[HD * (h % 2):HD * (h % 2) + HD, 6 + ci, CH * (h // 2):CH * (h // 2) + CH]
                        M(dst, VT[rows, HD * h:HD * h + HD], AM[rows, h, 1, :], start=(h < 2), stop=True,
                          skip_group_check=True)
                        M(dst, FK[rows, h, 1, :], AM[rows, h, 3, :], start=False, stop=True, skip_group_check=True)
                for ci, (_, col, _) in enumerate(chunks):
                    c = 2 * b - 1 + ci
                    pe.wait_ge(q_ready, c)
                    if c < NCHUNK - 1:
                        for t in range(4):
                            last = M(pst[:, 4 + ci, HD * t:HD * t + HD], MD[:, ci, t, :], QQ[:, t, :],
                                     start=True, stop=True)
                        last.then_inc(qn_done, 1)
                    pe.wait_ge(qd_ready, 2 * c)
                    for t in range(4):
                        last = M(pst[:, 6 + ci, CH * t:CH * t + CH], QD[:, ci, t, :], KR[:, t, 1, col:col + CH],
                                 start=False, stop=True, skip_group_check=True)
                    last.then_inc(yy_done, 1)
            pe.wait_ge(yy_copied, 2 * NB)
            pe.wait_ge(sg_ready, 1)
            for t in range(4):
                if t:
                    pe.wait_ge(yf_ready, t)
                M(pst[:, 4, :], headsum, KR[:, t, 0, MB:L], start=True, stop=True).then_inc(post_done, 1)
                M(pst[:, 5, :], headsum, BON[:, t, MB:L], start=True, stop=True).then_inc(post_done, 1)
                M(pst[:, 6, :], g2[:, P * t:P * t + P], SG[:, MB:L], start=True, stop=True).then_inc(post_done, 1)
                pe.wait_ge(postq_ready, t + 1)
                M(pst[:, 7, :], headsum, post["sq"][:], start=True, stop=True).then_inc(postv_done, 1)
            pe.wait_ge(yf_ready, 4)

            run_after_rw(pieces, jobs, dict(
                sb_meta=sb_meta, sb_z=sb_z, sb_arg=sb_arg, sb_o=sb_o, sb_end=sb_end, ret_scores=ret_scores,
                ret_out=ret_out, ret_square=ret_square, sw_square=sw_square, sw_scores=sw_scores,
                sw_turn=sw_turn, sw_out=sw_out, norm2=norm2))


def host_layout(inp):
    f = lambda a: np.asarray(a)
    weights = pack_weights(*(f(inp[k]) for k in ("w_in", "p_sb", "p_ret", "p_rw", "p_sw", "w_o", "w_up", "w_down")))
    lora = np.concatenate([np.concatenate([f(inp["rw_w2"])[0], f(inp["rw_a2"])[0]], 0), f(inp["rw_g2"])[0]], 1)
    cols = []
    for name, n in PARAMS:
        if name in ("qn", "kn"):
            v = f(inp[{"qn": "sw_qn_g", "kn": "sw_kn_g"}[name]])[0]
            cols.append(np.concatenate([v, v])[:, None])
        elif name == "sink":
            cols.append(np.broadcast_to(f(inp["sw_sink"])[0][None, :], (P, SWH)))
        else:
            cols.append(f(inp[name]).reshape(n, P).T)
    params = np.ascontiguousarray(np.concatenate(cols, 1))
    return {"weights": weights, "lora": np.ascontiguousarray(lora), "params": params,
            "consts": np.concatenate(list(CONSTS.values()), 1)}


def kernel(**inputs):
    import concourse.bacc as bacc
    from concourse.bass_utils import run_bass_kernel_spmd

    nc = bacc.Bacc("TRN2", target_bir_lowering=False, num_devices=1)
    arrays = {"x": np.asarray(inputs["x"]), "meta": np.asarray(inputs["meta"]), **host_layout(inputs)}
    aps = {k: nc.dram_tensor("in_" + k, a.shape, mybir.dt.from_np(a.dtype), kind="ExternalInput").ap()
           for k, a in arrays.items()}
    out = nc.dram_tensor("out_0", (1, T, D), F32, kind="ExternalOutput").ap()
    build(nc, out=out, **aps)
    r = run_bass_kernel_spmd(nc, [{"in_" + k: a for k, a in arrays.items()}], core_ids=[0])
    return r.results[0]["out_0"]
```

```python
from contextlib import ExitStack

import numpy as np
import concourse.bass as bass
from concourse import mybir

ALU = mybir.AluOpType
ACT = mybir.ActivationFunctionType
AX = mybir.AxisListType
F32 = mybir.dt.float32
F32R = mybir.dt.float32r

P = 128
D = 1024
KD = D // P
T = 512
NB = T // P
N_META = 16
MB = 32
L = MB + T
HL = L // 2
DFF = 4 * D
EPS = 1e-6
RW_LN_EPS = 64e-5
HD = 64
SBH = 8
RWH = 8
RETH = 4
SWH = 8
CH = 64
NCHUNK = 1 + T // CH
LEVELS = 6
NEG = -1.0e30

AQ, AK, AV, BQ, BK, BV, BG, CIN, DQ, DK, DV, GZ = 0, 4, 8, 12, 14, 16, 20, 24, 38, 42, 43, 44
CR, CK, CV, CWA, CG = 0, 4, 8, 12, 13
BRANCH_SB, BRANCH_RET, BRANCH_RW, BRANCH_SW = 0, 1, 2, 3

RW_FILL = [dict(score=1, c1=[1, 1, 1, 1, 1], tu=[0, 1, 1, 1, 1], f=0, wz=0, mn=0, end=0)] + \
          [dict(score=1, c1=[1] * 6, tu=[0, 1, 1, 1, 1, 1], f=1, wz=0, mn=1, end=1)] * NB
RW_NORM_FILL = [1, 1, 1, 0]
SB_FILL = [(3, 0), (2, 0)] * 4
RET_FILL = [(2, 1)] * 5
RET_POST_FILL = [(0, 1), (1, 2), (1, 2), (2, 2)]
SW_FILL = [(2, 1)] * 6 + [(1, 1)] * 2
SW_END_FILL = 2

RAW_SLOTS = 3
W_SLOTS = 4
UW = KD * P


def proj_jobs(br):
    return [("proj", br, i) for i in range(KD)]


def gate_jobs(br):
    return [("gate", br, i) for i in range(KD)]


def av_jobs(name):
    return [(name, pair, blk) for pair in range(2) for blk in range(NB + 1)]


PHASE_C = [("c", i, 0) for i in (CWA, CG)] + [("c", i, 0) for i in (CK, CR, CV)] + \
          [("c", i + t, 0) for t in range(1, 4) for i in (CK, CR, CV)]
SPILLED = ("rgate", "bq", "bk", "bv", "bg", "dq", "dk", "dv")
PHASE_A = [("rgate", BRANCH_RW, i) for i in range(KD)] + \
          [("bq", t, 0) for t in range(2)] + [("bk", t, 0) for t in range(2)] + av_jobs("bv") + \
          [("bg", t, 0) for t in range(4)] + \
          [("dq", t, 0) for t in range(4)] + [("dk", 0, 0)] + [("dv", 0, b) for b in range(NB + 1)] + \
          [("ak", t, 0) for t in range(4)] + [("aq", t, 0) for t in range(4)]
PHASE_B = av_jobs("av") + proj_jobs(BRANCH_RW) + gate_jobs(BRANCH_SB)
PHASE_D = proj_jobs(BRANCH_SB) + gate_jobs(BRANCH_RET)
PHASE_E = proj_jobs(BRANCH_RET) + gate_jobs(BRANCH_SW)
PHASE_O = [("wo", c, b) for c in range(4) for b in range(NB)]
FH = DFF // P // 2


def up_jobs(half):
    return [("up", half, f) for f in range(FH)]


def down_jobs(half):
    return [("down", half, (c, kk)) for c in range(2) for kk in range(FH // 2)]


JOBS = (PHASE_C + PHASE_A + PHASE_B + PHASE_D + PHASE_E + proj_jobs(BRANCH_SW) + PHASE_O + up_jobs(0) +
        down_jobs(0) + up_jobs(1) + down_jobs(1))
JOB_NO = {j: n for n, j in enumerate(JOBS)}


def units_of(job):
    kind, a, b = job
    if kind == "c":
        return [("w_in", CIN + a)]
    if kind in ("aq", "ak", "bq", "bk", "bg", "dq", "dk", "dv"):
        base = {"aq": AQ, "ak": AK, "bq": BQ, "bk": BK, "bg": BG, "dq": DQ, "dk": DK, "dv": DV}[kind]
        return [("w_in", base + a)]
    if kind in ("av", "bv"):
        base = {"av": AV, "bv": BV}[kind]
        return [("w_in", base + 2 * a), ("w_in", base + 2 * a + 1)]
    if kind in ("gate", "rgate"):
        return [("w_in", GZ + KD * a + b)]
    if kind == "proj":
        return [("p", a, b // 2)]
    if kind == "wo":
        return [("w_o", 2 * a), ("w_o", 2 * a + 1)]
    if kind == "up":
        return [("w_up", a * FH + b)]
    c, kk = b
    return [("w_down", a * FH // 2 + kk, c)]


UNITS, UNIT_NO, LAST_JOB = [], {}, {}
for _n, _j in enumerate(JOBS):
    for _u in units_of(_j):
        if _u not in UNIT_NO:
            UNIT_NO[_u] = len(UNITS)
            UNITS.append(_u)
        LAST_JOB[UNIT_NO[_u]] = _n
NU = len(UNITS)
KIND_NO, _c = [], {}
for _j in JOBS:
    KIND_NO.append(_c.get(_j[0], 0))
    _c[_j[0]] = KIND_NO[-1] + 1
PIECES = [(n, i, k) for n, j in enumerate(JOBS) for k in [2 if j[0] in ("aq", "ak", "bq", "bk", "bg", "dq", "dk", "gate", "rgate") else 1]
          for i in range(k)]
FIRST_PIECE = {n: i for i, (n, part, _) in enumerate(PIECES) if part == 0}
SPILL_NO = {n: i for i, n in enumerate(n for n, j in enumerate(JOBS) if j[0] in SPILLED)}
assert all(UNIT_NO[units_of(j)[0]] % 2 == 0 for j in JOBS if j[0] in ("av", "bv", "wo"))


def pack_weights(w_in, p_sb, p_ret, p_rw, p_sw, w_o, w_up, w_down):
    ps = (p_sb, p_ret, p_rw, p_sw)
    out = np.empty((NU, P, UW), np.float32)
    for n, u in enumerate(UNITS):
        if u[0] == "p":
            m = ps[u[1]][0][:, 256 * u[2]:256 * u[2] + 256]
        elif u[0] == "w_down":
            m = w_down[0][256 * u[1]:256 * u[1] + 256, 512 * u[2]:512 * u[2] + 512]
        else:
            m = {"w_in": w_in, "w_o": w_o, "w_up": w_up}[u[0]][0][:, P * u[1]:P * u[1] + P]
        out[n] = m.reshape(-1, P, m.shape[1]).transpose(1, 0, 2).reshape(P, UW)
    return out


def constants():
    i = np.arange(P)
    c = {"ident": np.eye(P), "headsum": (i[:, None] // HD == i[None, :] // HD) * 1.0}
    s, t = i[:, None], i[None, :]
    cs, ct = i[:, None] % CH, np.arange(CH)[None, :]
    c["ident_chunk"] = cs == ct
    c["rw_mask"] = np.concatenate([cs < ct, cs <= ct] * 2, 1)
    c["levels"] = np.concatenate(
        [(cs // (2 << l) == ct // (2 << l)) & ((cs >> l) % 2 == 0) & ((ct >> l) % 2 == 1) for l in range(LEVELS)], 1)
    start = np.ones(L)
    start[[0] + [MB + CH * k for k in range(T // CH)]] = 0
    c["scan_keep"] = np.broadcast_to(start, (P, L))
    c["suffix"] = -1.0 * (s >= t)
    c["suffix_meta"] = -1.0 * ((s >= t) & (s // MB == t // MB))
    strip = np.zeros((P, 3 * MB + MB + 3 * MB))
    strip[:, 3 * MB:4 * MB] = -1.0
    c["carry_meta"] = strip
    c["neg_ones"] = -np.ones((P, P))
    g = 1.0 - 2.0 ** (-5.0 - np.arange(RETH))
    diff = t - s
    c["ret_mask"] = np.concatenate([np.where(diff >= 0, gh ** np.maximum(diff, 0), 0) * HD ** -0.5 for gh in g], 1)
    c["ret_kdec"] = np.stack([gh ** (P - 1 - i) for gh in g], 1) * HD ** -0.5
    c["ret_kdec_meta"] = np.stack([gh ** np.maximum(MB - 1 - i, 0) for gh in g], 1) * HD ** -0.5
    c["ret_qdec"] = np.concatenate(
        [np.where(i[:, None] < HD, g[2 * p] ** (t + 1.0), g[2 * p + 1] ** (t + 1.0)) for p in range(2)], 1)
    key = np.arange(2 * P)[None, :]
    dist = (i[:, None] + P) - key
    band = np.where((dist >= 0) & (dist < P), -dist, NEG)
    meta = np.where(np.arange(MB)[None, :] < MB - N_META, NEG, 0.0) + 0.0 * i[:, None]
    c["sw_bias"] = np.concatenate([meta, band], 1)
    return {k: np.ascontiguousarray(v, np.float32) for k, v in c.items()}


RET_CHUNK_DECAY = [float((1.0 - 2.0 ** (-5.0 - h)) ** P) for h in range(RETH)]
CONSTS = constants()
CONST_AT, _o = {}, 0
for _k, _v in CONSTS.items():
    CONST_AT[_k] = (_o, _v.shape[1])
    _o += _v.shape[1]
NCONST = _o

PARAMS = [("norm1_g", 8), ("norm2_g", 8), ("rw_mu", 14), ("rw_w0", 4), ("rw_a0", 4), ("rw_kk", 4), ("rw_ka", 4),
          ("rw_rk", 4), ("rw_ln_g", 4), ("rw_ln_b", 4), ("qn", 1), ("kn", 1), ("sink", 8)]
PARAM_AT, _o = {}, 0
for _k, _n in PARAMS:
    PARAM_AT[_k] = (_o, _n)
    _o += _n
NPARAM = _o

SBUF_BASE, SBUF_END = 16512, 229344


def build(nc, x, meta, weights, lora, consts, params, out):
    with ExitStack() as ctx:
        cursor = [SBUF_BASE]

        def place(name, shape, dt=F32, at=None):
            size = 4 * int(np.prod(shape[1:]))
            size = (size + 31) // 32 * 32
            if at is None:
                at = cursor
            t = nc.alloc_sbuf_tensor_at(name, shape, dt, offset=at[0])
            at[0] += size
            assert at[0] <= SBUF_END, (name, at[0])
            return t

        cst = place("cst", [P, NCONST])
        par = place("par", [P, NPARAM])
        half_wa = place("half_wa", [P, 8])
        one_minus_ka = place("one_minus_ka", [P, 4])
        gain_q = place("gain_q", [P, 1])
        lor = place("lor", [P, 2 * T])
        h_hi = place("h_hi", [P, KD, L], F32R)
        h_lo = place("h_lo", [P, KD, L], F32R)
        raw = place("raw", [P, RAW_SLOTS, UW])
        w_hi = place("w_hi", [P, W_SLOTS, UW], F32R)
        w_lo = place("w_lo", [P, W_SLOTS, UW], F32R)
        region = cursor[0]

        at = [region]
        xt = place("xt", [P, NB, D], at=at)
        xm = place("xm", [MB, D], at=at)
        sq0 = place("sq0", [P, D], at=at)
        ss0 = place("ss0", [P, NB + 1], at=at)
        rs0 = place("rs0", [P, NB + 1], at=at)

        at = [region]
        sb_q = place("sb_q", [P, 4, T], at=at)
        sb_k = place("sb_k", [P, 4, L], at=at)
        sb_at = at[0]
        KR = place("rw_kappa_r", [P, 4, 2, L], at=at)
        KH = place("rw_k", [P, 4, L], at=at)
        BH = place("rw_b", [P, 4, L], at=at)
        RV = place("rw_v", [P, 4, L], at=at)
        BON = place("rw_bonus", [P, 4, L], at=at)
        SG = place("rw_sig_g", [P, L], at=at)
        GC = place("rw_chunk_decay", [P, 4, NCHUNK], at=at)
        mix_at = at[0]
        cbuf = place("cbuf", [P, 3, L + 1], at=at)
        cdif = place("cdif", [P, L], at=at)
        WA = place("rw_wa", [P, L], at=at)
        tmp_names = ["LAM", "AA", "LG", "LGX", "KKR", "T1", "SQ", "RN", "BB", "E1", "E2", "E3"]
        tt = {k: place("rw_" + k, [P, L], at=at) for k in tmp_names}
        at = [mix_at]
        KT = place("rw_k_tok", [P, T], at=at)
        BT = place("rw_b_tok", [P, T], at=at)
        VT = place("rw_v_tok", [P, T], at=at)
        FK = place("rw_wz", [P, RWH, 2, HD], at=at)
        AM = place("rw_scores", [P, RWH, 4, CH], at=at)
        XX = place("rw_x", [P, RWH, CH], at=at)
        TT = place("rw_t", [P, RWH, CH], at=at)
        C1 = place("rw_c1", [P, RWH, CH], at=at)
        MM = place("rw_m", [P, 2, RWH, CH], at=at)
        MD = place("rw_md", [P, 2, 4, P], at=at)
        QD = place("rw_qd", [P, 2, 4, P], at=at)
        QQ = place("rw_q", [P, 4, HD], at=at)
        NG = place("rw_ng", [P, 2, 4, HD], at=at)
        stage = place("stage", [P, 2, L], at=at)
        at = [mix_at]
        post = {k: place("rwp_" + k, [P, T], at=at) for k in ("sq", "rs", "bon")}
        top = SBUF_END - 4 * (2 * T + KD * T + KD * T + 2 * 4 * T)
        at = [top]
        gtmp = place("gtmp", [P, 2, T], at=at)
        gate_t = place("gate_t", [P, KD, T], at=at)
        merged = place("merged", [P, KD, T], at=at)
        y_hi = place("y_hi", [P, 4, T], F32R, at=at)
        y_lo = place("y_lo", [P, 4, T], F32R, at=at)
        SBW = [T, T - P, T - 2 * P, T - 3 * P]
        SB_COL = [0, T, 2 * T - P, 3 * T - 3 * P]
        SB_N = sum(SBW)
        at = [sb_at]
        sb_v = place("sb_v", [P, NB, T], at=at)
        sb_vm = place("sb_vm", [MB, T], at=at)
        sb_kmd = place("sb_kmd", [P, 4, P], at=at)
        sb_vmd = place("sb_vmd", [P, SBH, HD], at=at)
        sb_e0 = place("sb_e0", [P, SB_N], at=at)
        sb_s = place("sb_s", [P, SB_N], at=at)
        sb_cs = place("sb_cs", [P, SB_N - P], at=at)
        sb_em = place("sb_em", [P, T], at=at)
        sb_sm = place("sb_sm", [P, T], at=at)
        sb_end_at = at[0]
        at = [top - 4 * (2 * T + 2 * L + T) - 32]
        assert at[0] >= sb_end_at, (at[0], sb_end_at)
        ret_in_at = at[0]
        sb_e = [sb_e0, place("sb_e1", [P, SB_N], at=[ret_in_at])]
        rq = place("ret_q", [P, 2, T], at=at)
        rk = place("ret_k", [P, 2, L], at=at)
        rvm = place("ret_vm", [MB, T], at=at)
        assert at[0] <= top
        at = [region]
        rg = place("ret_g", [P, 4, T], at=at)
        ro_at = at[0]
        ro = place("ret_o", [P, RETH, T], at=at)
        rth = place("ret_th", [P, 4, T], at=[ro_at])
        rqd = place("ret_qd", [P, 2, T], at=at)
        rkd = place("ret_kd", [P, RETH, HD], at=at)
        rsc = place("ret_sc", [P, RETH, P], at=at)
        rsz = place("ret_state", [P, RETH, P], at=at)
        rsq = place("ret_sq", [P, 2, T], at=at)
        rv = place("ret_v", [P, NB, T], at=at)
        ret_end = at[0]
        at = [region]
        dsc = place("sw_scores", [P, 2, 4, MB + 2 * P], at=at)
        dpm = place("sw_probs_meta", [P, 2, 4, MB], at=at)
        dpt = place("sw_probs_t", [P, 2, 2, T], at=at)
        dpmt = place("sw_probs_meta_t", [P, 2, P], at=at)
        dvmd = place("sw_vmd", [P, 2, 4, HD], at=at)
        dst_ = place("sw_stats", [P, 2, 5, 4], at=at)
        ysw = place("sw_y", [P, 4, T // 2], at=at)
        at = [max(at[0], ret_end)]
        dq = place("sw_q", [P, 4, T], at=at)
        dk = place("sw_k", [P, L], at=at)
        dv = place("sw_v", [P, NB, P], at=at)
        assert at[0] <= ret_in_at
        dk2 = place("sw_k2", [P, 2, L], at=[ret_in_at])
        table_at = SBUF_BASE + 4 * CONST_AT["rw_mask"][0]
        assert [k for k in CONSTS][3:6] == ["rw_mask", "levels", "scan_keep"] and \
            CONST_AT["suffix"][0] - CONST_AT["rw_mask"][0] >= 2 * L
        dsq = place("sw_sq", [P, 2, L], at=[table_at])
        assert at[0] <= top
        at = [region]
        x2 = place("x2", [P, NB, D], at=at)
        u_hi = place("u_hi", [P, FH, T], F32R, at=at)
        u_lo = place("u_lo", [P, FH, T], F32R, at=at)
        ub = place("ub", [P, 2, T], at=at)
        usq = place("usq", [P, 2, T], at=at)
        ss2 = place("ss2", [P, 2, NB], at=at)
        h2n = place("h2n", [P, NB, D], at=at)

        pst = ctx.enter_context(nc.psum_tensor("pst", [P, 8, 512], F32))

        def scratch(name, shape):
            return nc.dram_tensor("wait_" + name, shape, F32).ap()
        spill = {"rgate": scratch("gate", (P, KD, T)), "bq": scratch("ret_q", (P, 2, T)),
                 "bk": scratch("ret_k", (P, 2, L)), "bv": scratch("ret_v", (P, NB, T)),
                 "bvm": scratch("ret_vm", (MB, T)), "bg": scratch("ret_g", (P, 4, T)),
                 "dq": scratch("sw_q", (P, 4, T)), "dk": scratch("sw_k", (P, L)),
                 "dv": scratch("sw_v", (P, NB, P)), "dvm": scratch("sw_vm", (MB, P))}

        def sem(name):
            return ctx.enter_context(nc.semaphore(name))

        const_in, table_in = sem("const_in"), sem("table_in")
        xb_in = [sem(f"xb_in{b}") for b in range(NB)]
        x_in = sem("x_in")
        raw_in = [sem(f"raw_in{i}") for i in range(RAW_SLOTS)]
        hi_ready = sem("hi_ready")
        lo_ready = sem("lo_ready")
        dense_done = sem("dense_done")
        dve_step, act_step, pool_step = sem("dve_step"), sem("act_step"), sem("pool_step")
        rs_ready = sem("rs_ready")
        hn_ready = sem("hn_ready")
        ht_done = sem("ht_done")
        hhi_ready = sem("hhi_ready")
        hlo_ready = sem("hlo_ready")
        par_ready = sem("par_ready")
        zeros_ready, cbuf_zeroed, diag_zeroed = sem("zeros_ready"), sem("cbuf_zeroed"), sem("diag_zeroed")
        c_copied, c_mixed = sem("c_copied"), sem("c_mixed")
        wa_tanh, sg_tanh, sg_ready = sem("wa_tanh"), sem("sg_tanh"), sem("sg_ready")
        lora_done, lora_act = sem("lora_done"), sem("lora_act")
        kkr_ready, kksq_ready, kksum_done, kkclamped, rn_ready = (
            sem("kkr_ready"), sem("kksq_ready"), sem("kksum_done"), sem("kkclamped"), sem("rn_ready"))
        lg_ready, e_ready, rw_elem = sem("lg_ready"), sem("e_ready"), sem("rw_elem")
        tok_done, tok_act, tok_dve = sem("tok_done"), sem("tok_act"), sem("tok_dve")
        am_done, am_ready = sem("am_done"), sem("am_ready")
        m_ready = [sem("m_ready0"), sem("m_ready1")]
        c1_done = [sem("c1_done0"), sem("c1_done1")]
        c1_copied = [sem("c1_copied0"), sem("c1_copied1")]
        tu_done = [sem("tu_done0"), sem("tu_done1")]
        x_ready = [sem("x_ready0"), sem("x_ready1")]
        f_done, f_copied, wz_done, wz_ready = sem("f_done"), sem("f_copied"), sem("wz_done"), sem("wz_ready")
        mn_done, mn_ready = sem("mn_done"), sem("mn_ready")
        qn_done, q_ready, qd_ready = sem("qn_done"), sem("q_ready"), sem("qd_ready")
        yy_done, yy_copied = sem("yy_done"), sem("yy_copied")
        post_done, postc_ready, postq_ready, postv_done, postr_ready = (
            sem("post_done"), sem("postc_ready"), sem("postq_ready"), sem("postv_done"), sem("postr_ready"))
        yf_ready, yh_ready, yl_ready = sem("yf_ready"), sem("yh_ready"), sem("yl_ready")
        merged_ready = sem("merged_ready")
        spill_copied = sem("spill_copied")
        spill_out = [sem("spill_out0"), sem("spill_out1")]
        gates_in, ret_qk_in, sw_in = sem("gates_in"), sem("ret_qk_in"), sem("sw_in")
        ret_g_in, ret_v_in = sem("ret_g_in"), sem("ret_v_in")
        out_done = sem("out_done")
        job_out = {k: sem(k + "_out") for k in
                   ("aq", "ak", "av", "gate", "proj", "wo", "up", "down")}
        gate_tanh = sem("gate_tanh")
        sb_diag_zeroed, sb_kmd_ready, sb_vmd_ready = sem("sb_diag_zeroed"), sem("sb_kmd_ready"), sem("sb_vmd_ready")
        zm_done, zm_ln, zm_sp, zm_arg, zm_a = (
            sem("zm_done"), sem("zm_ln"), sem("zm_sp"), sem("zm_arg"), sem("zm_a"))
        z_done, z_ln, z_sp, z_spm, z_cs, z_arg, z_a, z_am, o_done = (
            sem("z_done"), sem("z_ln"), sem("z_sp"), sem("z_spm"), sem("z_cs"), sem("z_arg"),
            sem("z_a"), sem("z_am"), sem("o_done"))
        sb_used = sem("sb_used")
        rg_tanh, rqd_ready, rsz_zeroed = sem("rg_tanh"), sem("rqd_ready"), sem("rsz_zeroed")
        rkt_done, rkd_ready, rs_done, rsc_ready, rkv_done, rstate, ro_done, ro_ready = (
            sem("rkt_done"), sem("rkd_ready"), sem("rs_done"), sem("rsc_ready"), sem("rkv_done"), sem("rstate"),
            sem("ro_done"), sem("ro_ready"))
        rsq_ready, rss_done, rrs_ready, ry_ready = sem("rsq_ready"), sem("rss_done"), sem("rrs_ready"), sem("ry_ready")
        dsq_ready, dss_done, drs_ready, dn_ready, dk2_own, dk2_in = (
            sem("dsq_ready"), sem("dss_done"), sem("drs_ready"), sem("dn_ready"), sem("dk2_own"), sem("dk2_in"))
        ds_done, ds_read, dmx_ready, dexp_ready, dp_ready, dpt_done, dpt_act, dpt_dve, do_done = (
            sem("ds_done"), sem("ds_read"), sem("dmx_ready"), sem("dexp_ready"), sem("dp_ready"), sem("dpt_done"),
            sem("dpt_act"), sem("dpt_dve"), sem("do_done"))
        ysw_ready = sem("ysw_ready")
        sw_vmd_ready = sem("sw_vmd_ready")
        x2_in, m_hi, m_lo = sem("x2_in"), sem("m_hi"), sem("m_lo")
        rs2_ready, h2n_ready, h2t_done, h2hi_ready, h2lo_ready = (
            sem("rs2_ready"), sem("h2n_ready"), sem("h2t_done"), sem("h2hi_ready"), sem("h2lo_ready"))
        u_hi_ready, u_lo_ready = sem("u_hi_ready"), sem("u_lo_ready")

        def C(name, lo=0, hi=None, rows=P):
            a, n = CONST_AT[name]
            return cst[0:rows, a + lo:a + (n if hi is None else hi)]

        def PAR(name, t):
            a, _ = PARAM_AT[name]
            return par[:, a + t:a + t + 1]

        ident = C("ident")
        headsum = C("headsum")
        w2, a2, g2 = lor[0:HD, 0:T], lor[HD:P, 0:T], lor[:, T:2 * T]

        def pair(slot):
            return pst[:, 2 * slot:2 * slot + 2, 0:HL]

        def four(row):
            return row.rearrange("p (h d) -> p h d", h=4)

        def halves(row):
            return row.rearrange("p (a b) -> p a b", a=2)

        def job_slot(n):
            return n % 2

        def kind_no(n):
            return KIND_NO[n]

        def emptied(n):
            kind, a, b = JOBS[n]
            if kind == "c":
                return c_copied, kind_no(n) + 1
            if kind in SPILLED:
                return spill_copied, SPILL_NO[n] + 1
            if kind == "down":
                half, (c, kk) = a, b
                return job_out["down"], 4 * (2 * half + c) + 4
            return job_out[kind], kind_no(n) + 1

        def diag23(tile):
            return tile[:, SB_COL[2] - P:SB_N].rearrange("p (a b) -> p a b", a=2)[:, :, P:2 * P]

        def chunks_of(b):
            if b == 0:
                return [(slice(0, MB), 0, MB)]
            return [(slice(CH * i, CH * i + CH), MB + P * (b - 1) + CH * i, CH) for i in range(2)]

        def norm2_psum(b, k):
            return pst[:, 4 + 2 * (b % 2) + k // 4, P * (k % 4):P * (k % 4) + P]

        def down_bank(c, blk):
            return (4 if c == 0 else 0) + blk

        def all_out(kind, job):
            return emptied(JOB_NO[job])

        YSW_STEPS = NB
        br_order = [BRANCH_RW, BRANCH_SB, BRANCH_RET, BRANCH_SW]

        def y_count(br):
            return 4 * br_order.index(br)

        def y_free(br):
            n = br_order.index(br)
            return JOB_NO[("proj", br_order[n - 1], KD - 1)] + 1

        rw_blocks = [(MB, 0)] + [(P, MB + P * b) for b in range(NB)]
        levels_of = [LEVELS - 1] + [LEVELS] * NB
        level0 = [sum(levels_of[:b]) for b in range(NB + 1)]

        block = ctx.enter_context(nc.Block())

        def run_after_rw(pieces, jobs, f):
            def g(name, *a):
                if name in f:
                    f[name](*a)

            g("reload_early")
            g("sb_prep")
            g("sb_keys")
            g("sb_z", 0)
            jobs(NB)
            g("sb_meta", 0)
            jobs(NB + 2)
            g("sb_values")
            for h in range(SBH):
                g("sb_mask", h)
                g("sb_sums", h)
                pieces(SB_FILL[h][0])
                g("sb_arg", h)
                if h + 1 < SBH:
                    g("sb_z", h + 1)
                g("sb_amask", h)
                pieces(SB_FILL[h][1])
                g("sb_o", h)
                if h % 4 == 3:
                    g("sb_end", h // 4)
                if h == 3:
                    g("sb_meta", 1)
            g("reload_late")
            g("ret_prep")
            pieces(2)
            g("ret_gate")
            for b in range(NB + 1):
                g("ret_scores", b)
                pieces(RET_FILL[b][0])
                g("ret_out", b)
                g("sw_square", b)
                pieces(RET_FILL[b][1])
                g("sw_sum", b)
                g("sw_norm", b)
            g("sw_keys")
            g("ret_square", 0)
            g("ret_square", 1)
            for h in range(RETH):
                pieces(RET_POST_FILL[h][0])
                g("ret_sum", h)
                g("ret_norm", h)
                pieces(RET_POST_FILL[h][1])
                if h + 2 < RETH:
                    g("ret_square", h + 2)
            g("sw_values")
            g("sw_scores", 0)
            for i in range(2 * NB):
                if i + 1 < 2 * NB:
                    g("sw_scores", i + 1)
                g("sw_probs", i)
                pieces(SW_FILL[i][0])
                g("sw_turn", i)
                pieces(SW_FILL[i][1])
                g("sw_out", i)
            pieces(SW_END_FILL)
            g("load_x2")
            for k in range(KD):
                jobs(1)
                g("merge_tile", k)
            jobs(len(PHASE_O) - NB)
            for b in range(NB):
                jobs(1)
                g("norm2", b)
                if b:
                    g("norm2_turn", b - 1)
            g("norm2_turn", NB - 1)
            jobs(4 * FH)

        @block.sync
        def _(sp):
            for b in range(NB):
                if b == NB - 1:
                    sp.wait_ge(zeros_ready, 1)
                    sp.dma_start(xm[MB - N_META:MB, :], meta).then_inc(x_in, 16)
                sp.dma_start(xt[:, b, :], x[0, P * b:P * b + P, :]).then_inc(xb_in[b], 16)
            sp.dma_start(par[:], params).then_inc(const_in, 16)
            sp.dma_start(cst[:, 0:P], consts[:, 0:P]).then_inc(const_in, 16)
            for u in range(NU):
                if u >= RAW_SLOTS:
                    sp.wait_ge(lo_ready, u - RAW_SLOTS + 1)
                sp.dma_start(raw[:, u % RAW_SLOTS, :], weights[u]).then_inc(raw_in[u % RAW_SLOTS], 16)
                if u == 0:
                    sp.dma_start(cst[:, P:NCONST], consts[:, P:NCONST]).then_inc(table_in, 16)
                    sp.dma_start(lor[:], lora).then_inc(table_in, 16)
            for c in range(2):
                for b in range(NB):
                    sp.wait_ge(job_out["down"], 8 + 4 * c + b + 1)
                    sp.dma_start(out[0, P * b:P * b + P, T * c:T * c + T], x2[:, b, T * c:T * c + T])\
                        .then_inc(out_done, 16)
            sp.wait_ge(out_done, 16 * 2 * NB)

        @block.gpsimd
        def _(pool):
            nc.gpsimd.memset(xm[:], 0.0).then_inc(zeros_ready, 1)
            done = [0]

            def low(upto_unit):
                while done[0] < min(upto_unit, NU):
                    u = done[0]
                    pool.wait_ge(hi_ready, u + 1)
                    nc.gpsimd.tensor_tensor(w_lo[:, u % W_SLOTS, :], raw[:, u % RAW_SLOTS, :],
                                            w_hi[:, u % W_SLOTS, :].bitcast(F32), ALU.subtract).then_inc(lo_ready, 1)
                    done[0] += 1

            def sb_prep():
                pool.wait_ge(yl_ready, 4)
                nc.gpsimd.memset(sb_kmd[:], 0.0).then_inc(sb_diag_zeroed, 1)
                nc.gpsimd.memset(sb_vmd[:], 0.0).then_inc(pool_step, 1)

            def sb_values():
                pool.wait_ge(pool_step, 1)
                pool.wait_ge(*emptied(JOB_NO[("av", 1, 0)]))
                for h in range(SBH):
                    q = MB * (h % 4)
                    pool.dma_start(sb_vmd[q:q + MB, h, :], sb_vm[:, HD * h:HD * h + HD]).then_inc(sb_vmd_ready, 16)

            def sb_diag(tile):
                for v in (tile[:, 0:2 * T].rearrange("p (a b) -> p a b", a=2)[:, :, 0:P],
                          diag23(tile)):
                    last = nc.gpsimd.affine_select(out=v, in_=v, compare_op=ALU.is_gt, fill=0.0, base=0,
                                                   pattern=[[0, 2], [1, P]], channel_multiplier=-1)
                return last

            def sb_mask(h):
                pool.wait_ge(z_sp, h + 1)
                sb_diag(sb_s).then_inc(z_spm, 1)

            def sb_amask(h):
                pool.wait_ge(z_a, h + 1)
                sb_diag(sb_e[h % 2]).then_inc(z_am, 1)

            def sw_values():
                pool.wait_ge(yl_ready, 12)
                pool.wait_ge(rsz_zeroed, 1)
                nc.gpsimd.memset(dvmd[:], 0.0).then_inc(pool_step, 1)
                pool.wait_ge(pool_step, 2)
                for kv in range(2):
                    for j in range(4):
                        pool.dma_start(dvmd[MB * j:MB * j + MB, kv, j, :], spill["dvm"][:, HD * kv:HD * kv + HD])\
                            .then_inc(sw_vmd_ready, 16)

            def ret_prep():
                pool.wait_ge(yl_ready, 8)
                nc.gpsimd.memset(rsz[:], 0.0).then_inc(rsz_zeroed, 1)

            piece = [FIRST_PIECE[len(PHASE_C)]]

            def pieces(k):
                for _ in range(k):
                    n, part, parts = PIECES[piece[0]]
                    if part == parts - 1:
                        low(UNIT_NO[units_of(JOBS[n])[0]] + W_SLOTS)
                    piece[0] += 1

            def jobs(k):
                n = PIECES[piece[0]][0]
                pieces(FIRST_PIECE.get(n + k, len(PIECES)) - FIRST_PIECE[n])

            low(UNIT_NO[units_of(PHASE_C[-1])[0]] + W_SLOTS)
            pool.wait_ge(rw_elem, 4)
            nc.gpsimd.memset(MD[:], 0.0).then_inc(diag_zeroed, 1)
            nc.gpsimd.memset(QD[:], 0.0).then_inc(diag_zeroed, 1)
            pool.wait_ge(table_in, 32)

            def level_mask(b, l):
                n, m = rw_blocks[b][0], chunks_of(b)[0][2]
                step = level0[b] + l
                for g in range(2):
                    if l == 0:
                        pool.wait_ge(am_ready, 4 * b + 2 * g + 2)
                    if step >= 2:
                        pool.wait_ge(x_ready[g], step - 1)
                    nc.gpsimd.tensor_tensor(
                        MM[0:n, step % 2, 4 * g:4 * g + 4, 0:m], AM[0:n, 4 * g:4 * g + 4, 2, 0:m],
                        C("levels", CH * l, CH * l + m, n).unsqueeze(1).broadcast_to([n, 4, m]),
                        ALU.mult).then_inc(m_ready[g], 1)

            for b in range(NB + 1):
                fill = RW_FILL[b]
                pieces(fill["score"])
                level_mask(b, 0)
                for l in range(levels_of[b]):
                    if l + 1 < levels_of[b]:
                        level_mask(b, l + 1)
                    pieces(fill["c1"][l] + fill["tu"][l])
                pieces(fill["f"] + fill["wz"] + fill["mn"] + fill["end"])
            pieces(sum(RW_NORM_FILL))
            run_after_rw(pieces, jobs, {
                "sb_prep": sb_prep, "sb_mask": sb_mask, "sb_amask": sb_amask,
                "ret_prep": ret_prep, "sb_values": sb_values, "sw_values": sw_values})
            low(NU)

        @block.scalar
        def _(act):
            steps = [0]

            def link(ins):
                ins.then_inc(act_step, 1)
                steps[0] += 1
                act.wait_ge(act_step, steps[0])

            units = [0]

            def high(upto_unit):
                while units[0] < min(upto_unit, NU):
                    u = units[0]
                    act.wait_ge(raw_in[u % RAW_SLOTS], 16 * (u // RAW_SLOTS + 1))
                    if u >= W_SLOTS:
                        act.wait_ge(dense_done, LAST_JOB[u - W_SLOTS] + 1)
                    nc.scalar.activation(w_hi[:, u % W_SLOTS, :], raw[:, u % RAW_SLOTS, :], ACT.Copy)\
                        .then_inc(hi_ready, 1)
                    units[0] += 1

            def after_job(n):
                high(UNIT_NO[units_of(JOBS[n])[0]] + W_SLOTS)

            A = nc.scalar.activation
            nc.scalar.preload_act_table_set("natural_log_exp_and_others")
            for b in list(range(NB - 1)) + [NB, NB - 1]:
                r, src = (P, xt[:, b, :]) if b < NB else (MB, xm[:])
                act.wait_ge(xb_in[b] if b < NB else x_in, 16)
                link(A(sq0[0:r], src, ACT.Square, accum_out=ss0[0:r, b:b + 1]))
                link(A(rs0[0:r, b:b + 1], ss0[0:r, b:b + 1], ACT.Ln, scale=1.0 / D, bias=EPS))
                A(rs0[0:r, b:b + 1], rs0[0:r, b:b + 1], ACT.Exp, scale=-0.5).then_inc(rs_ready, 1)
            act.wait_ge(const_in, 32)
            for k in range(KD):
                act.wait_ge(ht_done, k + 1)
                A(h_hi[:, k, MB:L], pst[:, 2 + k % 4, :], ACT.Copy, scale=PAR("norm1_g", k)).then_inc(hhi_ready, 1)
                A(h_hi[:, k, 0:MB], pst[:, 6 + k % 2, 0:MB], ACT.Copy, scale=PAR("norm1_g", k)).then_inc(hhi_ready, 1)
                if k in (2, 4):
                    high(k // 2)
            high(RAW_SLOTS)

            nc.scalar.preload_act_table_set("exp_and_others")
            act.wait_ge(cbuf_zeroed, 1)

            def c_copy(i):
                n = JOB_NO[PHASE_C[i]]
                act.wait_ge(dense_done, n + 1)
                if i >= 3:
                    act.wait_ge(c_mixed, i - 2)
                A(halves(cbuf[:, i % 3, 1:L + 1]), pair(job_slot(n)), ACT.Copy).then_inc(c_copied, 1)
                after_job(n)

            c_copy(0)
            c_copy(1)
            act.wait_ge(c_mixed, 1)
            A(WA[0:HD, :], WA[0:HD, :], ACT.Tanh).then_inc(wa_tanh, 1)
            act.wait_ge(c_mixed, 2)
            A(SG[:], SG[:], ACT.Tanh, scale=0.5).then_inc(sg_tanh, 1)
            act.wait_ge(par_ready, 3)
            for t in range(4):
                for i in range(3):
                    c_copy(2 + 3 * t + i)
                act.wait_ge(lora_done, 2 * t + 1)
                if t >= 1:
                    act.wait_ge(rw_elem, t)
                A(halves(tt["LAM"][:]), pst[:, 4:6, 0:HL], ACT.Tanh, scale=0.5, bias=half_wa[:, t:t + 1])\
                    .then_inc(lora_act, 1)
                act.wait_ge(lora_done, 2 * t + 2)
                A(halves(tt["AA"][:]), pst[:, 6:8, 0:HL], ACT.Tanh, scale=0.5, bias=half_wa[:, 4 + t:5 + t])\
                    .then_inc(lora_act, 1)
                nc.scalar.preload_act_table_set("natural_log_exp_and_others")
                act.wait_ge(kkr_ready, t + 1)
                A(tt["SQ"][:], tt["KKR"][:], ACT.Square).then_inc(kksq_ready, 1)
                act.wait_ge(lg_ready, t + 1)
                A(tt["E1"][:], tt["LG"][:], ACT.Exp).then_inc(e_ready, 1)
                A(tt["E2"][:], tt["LGX"][:], ACT.Exp).then_inc(e_ready, 1)
                A(tt["E3"][:], tt["LG"][:], ACT.Exp, scale=-1.0).then_inc(e_ready, 1)
                act.wait_ge(kkclamped, t + 1)
                link(A(tt["RN"][:], tt["RN"][:], ACT.Ln, scale=2.0 ** 20))
                A(tt["RN"][:], tt["RN"][:], ACT.Exp, scale=-0.5, bias=float(10 * np.log(2.0))).then_inc(rn_ready, 1)
                if t < 3:
                    nc.scalar.preload_act_table_set("exp_and_others")

            piece = [FIRST_PIECE[len(PHASE_C)]]

            def pieces(k):
                for _ in range(k):
                    n, part, parts = PIECES[piece[0]]
                    if part == parts - 1:
                        job(n)
                    piece[0] += 1

            def jobs(k):
                n = PIECES[piece[0]][0]
                pieces(FIRST_PIECE.get(n + k, len(PIECES)) - FIRST_PIECE[n])

            def spill_job(n):
                kind, a, b = JOBS[n]
                i, s = SPILL_NO[n], job_slot(n)
                one, buf = pst[:, 2 * s, :], stage[:, i % 2, :]
                if i >= 2:
                    act.wait_ge(spill_out[i % 2], 16 * (i // 2))
                func, scale, rows, to = ACT.Copy, 1.0, P, spill[kind]
                if kind == "bk" or kind == "dk":
                    src, n_ = pair(s), L
                    buf_in = halves(buf)
                    dst = to[:, a, :] if kind == "bk" else to
                else:
                    n_ = T
                    if kind == "rgate":
                        func, scale, dst = ACT.Tanh, 0.5, to[:, b, :]
                    elif kind in ("bv", "dv"):
                        n_ = 2 * P if kind == "bv" else P
                        cols = slice(n_ * a, n_ * a + n_)
                        if b:
                            dst = to[:, b - 1, cols]
                        else:
                            rows, dst = MB, spill[kind + "m"][:, cols]
                    else:
                        dst = to[:, a, :]
                    src, buf_in = one[0:rows, 0:n_], buf[0:rows, 0:n_]
                A(buf_in, src, func, scale=scale).then_inc(spill_copied, 1)
                after_job(n)
                act.wait_ge(spill_copied, i + 1)
                act.dma_start(dst, buf[0:rows, 0:n_]).then_inc(spill_out[i % 2], 16)

            def reload_early():
                act.wait_ge(yl_ready, 4)
                for i in range(2):
                    act.wait_ge(spill_out[i], 16 * (len(SPILL_NO) // 2))
                act.dma_start(gate_t[:], spill["rgate"]).then_inc(gates_in, 16)

            def reload_late():
                act.wait_ge(yl_ready, 8)
                act.dma_start(rk[:], spill["bk"]).then_inc(ret_qk_in, 16)
                act.dma_start(rq[:], spill["bq"]).then_inc(ret_qk_in, 16)
                act.dma_start(rvm[:], spill["bvm"]).then_inc(ret_qk_in, 16)
                act.dma_start(rg[:], spill["bg"]).then_inc(ret_g_in, 16)
                act.dma_start(rv[:], spill["bv"]).then_inc(ret_v_in, 16)
                for tile, name in ((dq, "dq"), (dk, "dk"), (dv, "dv")):
                    act.dma_start(tile[:], spill[name]).then_inc(sw_in, 16)

            def job(n):
                kind, a, b = JOBS[n]
                s = job_slot(n)
                one, two = pst[:, 2 * s, :], pair(s)
                if kind in ("aq", "ak", "gate", "up") + SPILLED:
                    act.wait_ge(dense_done, n + 1)
                if kind in SPILLED:
                    spill_job(n)
                    return
                if kind == "aq":
                    A(sb_q[:, a, :], one, ACT.Copy, scale=float(HD) ** -0.5).then_inc(job_out[kind], 1)
                elif kind == "ak":
                    A(halves(sb_k[:, a, :]), two, ACT.Copy).then_inc(job_out[kind], 1)
                elif kind == "gate":
                    i = kind_no(n)
                    act.wait_ge(job_out["proj"], i + 1)
                    A(gate_t[:, b, :], one, ACT.Copy).then_inc(job_out[kind], 1)
                    if b % 4 == 3:
                        nc.scalar.preload_act_table_set("exp_and_others")
                        act.wait_ge(job_out[kind], i + 1)
                        A(gate_t[:, b - 3:b + 1], gate_t[:, b - 3:b + 1], ACT.Tanh, scale=0.5).then_inc(gate_tanh, 1)
                        nc.scalar.preload_act_table_set("natural_log_exp_and_others")
                elif kind == "up":
                    i = kind_no(n)
                    if i >= 2:
                        act.wait_ge(u_lo_ready, i - 1)
                    A(ub[:, i % 2, :], one, ACT.Relu).then_inc(job_out[kind], 1)
                    act.wait_ge(job_out[kind], i + 1)
                    if a == 1 and b == 0:
                        act.wait_ge(dense_done, n)
                    A(u_hi[:, b, :], ub[:, i % 2, :], ACT.Square).then_inc(u_hi_ready, 1)
                after_job(n)

            def sb_meta(grp):
                act.wait_ge(zm_done, grp + 1)
                link(A(sb_em[:], pst[:, 7, :], ACT.Abs))
                link(A(sb_em[:], sb_em[:], ACT.Exp, scale=-1.0))
                A(sb_em[:], sb_em[:], ACT.Ln, bias=1.0).then_inc(zm_ln, 1)

            def sb_pieces(tile):
                return tile[:, 0:T], tile[:, T:SB_N].rearrange("p (a b) -> p a b", a=2)

            def sb_z(h):
                act.wait_ge(z_done, h + 1)
                if h >= 2:
                    act.wait_ge(sb_used, h - 1)
                e0, e1 = sb_pieces(sb_e[h % 2])
                A(e0, pst[:, 4, :], ACT.Abs)
                link(A(e1, pst[:, 5:7, 0:3 * P], ACT.Abs))
                A(e0, e0, ACT.Exp, scale=-1.0)
                link(A(e1, e1, ACT.Exp, scale=-1.0))
                A(e0, e0, ACT.Ln, bias=1.0)
                A(e1, e1, ACT.Ln, bias=1.0).then_inc(z_ln, 1)

            def sb_arg(h):
                act.wait_ge(z_arg, h + 1)
                e0, e1 = sb_pieces(sb_e[h % 2])
                A(e0, pst[:, 4, :], ACT.Exp)
                A(e1, pst[:, 5:7, 0:3 * P], ACT.Exp).then_inc(z_a, 1)
                if h % 4 == 3:
                    act.wait_ge(zm_arg, h // 4 + 1)
                    A(sb_em[:], pst[:, 7, :], ACT.Exp).then_inc(zm_a, 1)

            def sb_end(grp):
                for t in (2 * grp, 2 * grp + 1):
                    act.wait_ge(o_done, t + 1)
                    if t == 0:
                        assert PIECES[piece[0]][0] >= y_free(BRANCH_SB)
                        act.wait_ge(dense_done, y_free(BRANCH_SB))
                    A(y_hi[:, t, :], pst[:, 1 + 2 * (t % 2), :], ACT.Copy).then_inc(yh_ready, 1)

            def ret_gate():
                nc.scalar.preload_act_table_set("exp_and_others")
                act.wait_ge(ret_g_in, 16)
                A(rth[:], rg[:], ACT.Tanh, scale=0.5).then_inc(rg_tanh, 1)
                nc.scalar.preload_act_table_set("natural_log_exp_and_others")

            def ret_out(b):
                if b:
                    act.wait_ge(ro_done, b)
                    A(ro[:, :, P * (b - 1):P * b], pst[:, 7 if b % 2 else 1, :].rearrange("p (h i) -> p h i", h=RETH),
                      ACT.Copy).then_inc(ro_ready, 1)

            def ret_square(h):
                act.wait_ge(ro_ready, NB)
                if h >= 2:
                    act.wait_ge(ry_ready, h - 1)
                A(rsq[:, h % 2, :], ro[:, h, :], ACT.Square).then_inc(rsq_ready, 1)

            def ret_norm(h):
                act.wait_ge(rss_done, h + 1)
                link(A(rsq[:, h % 2, :], pst[:, 4 + h % 2, :], ACT.Ln, scale=-1.0 / P, bias=EPS))
                A(rsq[:, h % 2, :], rsq[:, h % 2, :], ACT.Exp, scale=-0.5).then_inc(rrs_ready, 1)
                act.wait_ge(ry_ready, h + 1)
                if h == 0:
                    assert PIECES[piece[0]][0] >= y_free(BRANCH_RET)
                    act.wait_ge(dense_done, y_free(BRANCH_RET))
                A(y_hi[:, h, :], ro[:, h, :], ACT.Copy).then_inc(yh_ready, 1)

            def sw_square(i):
                n, src = (T, dq[:, i - 1, :]) if i else (L, dk[:])
                if i == 0:
                    act.wait_ge(sw_in, 48)
                if i >= 2:
                    act.wait_ge(dn_ready, i - 1)
                A(dsq[:, i % 2, 0:n], src, ACT.Square).then_inc(dsq_ready, 1)

            def sw_norm(i):
                sq = dsq[:, i % 2, 0:T if i else L]
                act.wait_ge(dss_done, i + 1)
                if i:
                    link(A(sq, pst[:, 3, :], ACT.Ln, scale=1.0 / HD, bias=EPS))
                else:
                    A(sq[:, 0:HL], pst[:, 1, 0:HL], ACT.Ln, scale=1.0 / HD, bias=EPS)
                    link(A(sq[:, HL:L], pst[:, 3, 0:HL], ACT.Ln, scale=1.0 / HD, bias=EPS))
                A(sq, sq, ACT.Exp, scale=-0.5).then_inc(drs_ready, 1)

            def sw_keys():
                act.wait_ge(dn_ready, 1)
                act.wait_ge(ro_done, NB)
                for kv in range(2):
                    own, other = slice(HD * kv, HD * kv + HD), slice(HD - HD * kv, P - HD * kv)
                    act.dma_start(dk2[other, kv, :], dk[own, :]).then_inc(dk2_in, 16)

            def sw_values():
                act.wait_ge(yl_ready, 12)

            def sw_probs(i):
                st = dst_[:, i % 2]
                act.wait_ge(dmx_ready, i + 1)
                A(st[:, 2, :], st[:, 2, :], ACT.Exp).then_inc(dexp_ready, 1)
                w = MB + (2 * P if i // 2 else P)
                for j in range(4):
                    A(dsc[:, i % 2, j, 0:w], dsc[:, i % 2, j, 0:w], ACT.Exp, bias=st[:, 0, j:j + 1],
                      accum_out=st[:, 1, j:j + 1]).then_inc(dexp_ready, 1)

            def sw_turn(i):
                act.wait_ge(dpt_done, i + 1)
                A(dpt[:, i % 2, 0, :], pst[:, 1, :], ACT.Copy).then_inc(dpt_act, 1)

            def sw_out(i):
                b, kv = i // 2, i % 2
                act.wait_ge(do_done, i + 1)
                o = pst[:, 6, P:3 * P].rearrange("p (t q) -> p t q", t=2)
                if i < YSW_STEPS:
                    A(ysw[:, 2 * kv:2 * kv + 2, P * b:P * b + P], o, ACT.Copy).then_inc(ysw_ready, 1)
                    return
                if i == YSW_STEPS:
                    assert PIECES[piece[0]][0] >= y_free(BRANCH_SW)
                    act.wait_ge(dense_done, y_free(BRANCH_SW))
                A(y_hi[:, 2 * kv:2 * kv + 2, P * b:P * b + P], o, ACT.Copy).then_inc(yh_ready, 1)
                if i == YSW_STEPS:
                    act.wait_ge(ysw_ready, YSW_STEPS)
                    A(y_hi[:, :, 0:P * b], ysw[:], ACT.Copy).then_inc(yh_ready, 1)

            def load_x2():
                act.wait_ge(yl_ready, y_count(BRANCH_SW) + 4)
                act.dma_start(x2[:], x[0].rearrange("(b p) d -> p b d", p=P)).then_inc(x2_in, 16)

            def merge_tile(k):
                if k == 0:
                    act.wait_ge(dense_done, JOB_NO[("gate", BRANCH_SW, KD - 1)] + 1)
                act.wait_ge(merged_ready, 2 * KD + k + 1)
                A(h_hi[:, k, 0:T], merged[:, k, :], ACT.Copy, scale=0.5).then_inc(m_hi, 1)

            def norm2(b):
                if b == 0:
                    act.wait_ge(m_lo, KD)
                act.wait_ge(*all_out("wo", ("wo", 3, b)))
                link(A(h2n[:, b, :], x2[:, b, :], ACT.Square, accum_out=ss2[:, 0, b:b + 1]))
                link(A(ss2[:, 1, b:b + 1], ss2[:, 0, b:b + 1], ACT.Ln, scale=1.0 / D, bias=EPS))
                A(ss2[:, 1, b:b + 1], ss2[:, 1, b:b + 1], ACT.Exp, scale=-0.5).then_inc(rs2_ready, 1)

            def norm2_turn(b):
                for k in range(KD):
                    if k % 4 == 0:
                        act.wait_ge(h2t_done, 2 * b + k // 4 + 1)
                    A(h_hi[:, k, P * b:P * b + P], norm2_psum(b, k), ACT.Copy, scale=PAR("norm2_g", k))\
                        .then_inc(h2hi_ready, 1)

            nc.scalar.preload_act_table_set("exp_and_others")
            for b, (n, c0) in enumerate(rw_blocks):
                m = chunks_of(b)[0][2]
                act.wait_ge(tok_done, 4 * b + 1)
                A(FK[0:n, :, 0, :], pst[0:n, 4, :].rearrange("p (h d) -> p h d", h=RWH), ACT.Copy).then_inc(tok_act, 1)
                act.wait_ge(tok_done, 4 * b + 2)
                A(VT[0:n, :], pst[0:n, 5, :], ACT.Copy).then_inc(tok_act, 1)
                fill = RW_FILL[b]
                pieces(fill["score"])
                for l in range(levels_of[b]):
                    for g in range(2 if l else 0):
                        act.wait_ge(c1_done[g], level0[b] + l + 1)
                        A(C1[0:n, 4 * g:4 * g + 4, 0:m], four(pst[0:n, 4 + 2 * g, 0:256])[:, :, 0:m], ACT.Copy)\
                            .then_inc(c1_copied[g], 1)
                    pieces(fill["c1"][l] + fill["tu"][l])
                for g in range(2):
                    act.wait_ge(f_done, 2 * b + g + 1)
                    A(FK[0:n, 4 * g:4 * g + 4, 1, :], four(pst[0:n, 4 + 2 * g, 0:256]), ACT.Copy).then_inc(f_copied, 1)
                pieces(fill["f"] + fill["wz"] + fill["mn"] + fill["end"])
                if b == 0:
                    continue
                for ci in range(2):
                    c = 2 * b - 1 + ci
                    act.wait_ge(q_ready, c)
                    if b == 1 and ci == 0:
                        act.wait_ge(diag_zeroed, 2)
                    if b >= 2:
                        act.wait_ge(yy_done, 2 * (b - 1))
                    for hf in range(2):
                        r = slice(HD * hf, HD * hf + HD)
                        A(QD[r, ci, :, HD * hf:HD * hf + HD], QQ[r, :, :], ACT.Copy).then_inc(qd_ready, 1)
                for ci, (_, col, _) in enumerate(chunks_of(b)):
                    act.wait_ge(yy_done, 2 * (b - 1) + ci + 1)
                    A(KR[:, :, 0, col:col + CH], four(pst[:, 6 + ci, 0:256]), ACT.Copy).then_inc(yy_copied, 1)
            nc.scalar.preload_act_table_set("natural_log_exp_and_others")

            def post_square(t):
                act.wait_ge(postc_ready, t + 1)
                A(post["sq"][:], KR[:, t, 0, MB:L], ACT.Square).then_inc(postq_ready, 1)

            post_square(0)
            for t in range(4):
                act.wait_ge(postv_done, t + 1)
                link(A(post["rs"][:], pst[:, 7 - 4 * (t % 2), :], ACT.Ln, scale=1.0 / HD, bias=RW_LN_EPS))
                A(post["rs"][:], post["rs"][:], ACT.Exp, scale=-0.5).then_inc(postr_ready, 1)
                if t < 3:
                    post_square(t + 1)
                pieces(RW_NORM_FILL[t])
                act.wait_ge(yf_ready, t + 1)
                A(y_hi[:, t, :], KR[:, t, 0, MB:L], ACT.Copy).then_inc(yh_ready, 1)

            run_after_rw(pieces, jobs, dict(
                sb_meta=sb_meta, sb_z=sb_z, sb_arg=sb_arg, sb_end=sb_end, ret_gate=ret_gate, ret_out=ret_out,
                ret_square=ret_square, ret_norm=ret_norm, sw_square=sw_square, sw_norm=sw_norm, sw_keys=sw_keys, sw_values=sw_values,
                sw_probs=sw_probs, sw_turn=sw_turn, sw_out=sw_out, merge_tile=merge_tile,
                norm2=norm2, norm2_turn=norm2_turn, load_x2=load_x2, reload_early=reload_early, reload_late=reload_late))

        @block.vector
        def _(dve):
            steps = [0]

            def link(ins):
                ins.then_inc(dve_step, 1)
                steps[0] += 1
                dve.wait_ge(dve_step, steps[0])

            V = nc.vector
            for i, b in enumerate(list(range(NB - 1)) + [NB, NB - 1]):
                r, src = (P, xt[:, b, :]) if b < NB else (MB, xm[:])
                dve.wait_ge(rs_ready, i + 1)
                V.tensor_scalar(src, src, rs0[0:r, b:b + 1], None, ALU.mult).then_inc(hn_ready, 1)
            dve.wait_ge(const_in, 32)
            a, _ = PARAM_AT["rw_w0"]
            V.tensor_scalar(half_wa[:], par[:, a:a + 8], 0.5, None, ALU.mult).then_inc(par_ready, 1)
            a, _ = PARAM_AT["rw_ka"]
            V.tensor_scalar(one_minus_ka[:], par[:, a:a + 4], -1.0, 1.0, ALU.mult, ALU.add).then_inc(par_ready, 1)
            V.tensor_scalar(gain_q[:], PAR("qn", 0), float(HD) ** -0.5, None, ALU.mult).then_inc(par_ready, 1)
            for k in range(KD):
                dve.wait_ge(hhi_ready, 2 * k + 2)
                V.scalar_tensor_tensor(out=h_lo[:, k, MB:L], in0=pst[:, 2 + k % 4, :], scalar=PAR("norm1_g", k),
                                       in1=h_hi[:, k, MB:L].bitcast(F32), op0=ALU.mult, op1=ALU.subtract)\
                    .then_inc(hlo_ready, 1)
                V.scalar_tensor_tensor(out=h_lo[:, k, 0:MB], in0=pst[:, 6 + k % 2, 0:MB], scalar=PAR("norm1_g", k),
                                       in1=h_hi[:, k, 0:MB].bitcast(F32), op0=ALU.mult, op1=ALU.subtract)\
                    .then_inc(hlo_ready, 1)
            dve.wait_ge(ht_done, KD)
            V.memset(cbuf[:, :, 0:1], 0.0).then_inc(cbuf_zeroed, 1)

            def c_mix(i, dst):
                dve.wait_ge(c_copied, i + 1)
                cur = cbuf[:, i % 3, 1:L + 1]
                link(V.tensor_tensor(cdif[:], cbuf[:, i % 3, 0:L], cur, ALU.subtract))
                V.scalar_tensor_tensor(out=dst, in0=cdif[:], scalar=PAR("rw_mu", PHASE_C[i][1]), in1=cur,
                                       op0=ALU.mult, op1=ALU.add).then_inc(c_mixed, 1)
                dve.wait_ge(c_mixed, i + 1)

            c_mix(0, WA[:])
            c_mix(1, SG[:])
            dve.wait_ge(sg_tanh, 1)
            V.tensor_scalar(SG[:], SG[:], 1.0, 0.5, ALU.add, ALU.mult).then_inc(sg_ready, 1)
            for t in range(4):
                LAM, AA, LG, LGX, KKR, T1, SQ, RN, BB, E1, E2, E3 = (tt[k][:] for k in tmp_names)
                kt, rt = KH[:, t, :], KR[:, t, 1, :]
                c_mix(2 + 3 * t, kt)
                V.tensor_scalar(KKR, kt, PAR("rw_kk", t), None, ALU.mult).then_inc(kkr_ready, 1)
                c_mix(3 + 3 * t, rt)
                c_mix(4 + 3 * t, RV[:, t, :])
                if t == 0:
                    dve.wait_ge(table_in, 32)
                dve.wait_ge(lora_act, 2 * t + 1)
                link(V.tensor_scalar(LAM, LAM, 1.0, -0.5 * float(np.exp(-0.5)), ALU.add, ALU.mult))
                link(V.tensor_tensor_scan(LG, C("scan_keep"), LAM, 0.0, ALU.mult, ALU.add))
                V.tensor_tensor(LGX, LG, LAM, ALU.subtract).then_inc(lg_ready, 1)
                dve.wait_ge(lora_act, 2 * t + 2)
                link(V.tensor_scalar(AA, AA, 1.0, 0.5, ALU.add, ALU.mult))
                link(V.tensor_scalar(T1, AA, PAR("rw_ka", t), one_minus_ka[:, t:t + 1], ALU.mult, ALU.add))
                link(V.tensor_tensor(kt, kt, T1, ALU.mult))
                V.scalar_tensor_tensor(out=BON[:, t, :], in0=rt, scalar=PAR("rw_rk", t), in1=kt,
                                       op0=ALU.mult, op1=ALU.mult)
                dve.wait_ge(kksum_done, t + 1)
                V.tensor_scalar(halves(RN), pst[:, 4:6, 0:HL], 1e-24, None, ALU.max).then_inc(kkclamped, 1)
                dve.wait_ge(e_ready, 3 * t + 3)
                V.tensor_copy(GC[:, t, 0:1], E1[:, MB - 1:MB])
                V.tensor_copy(GC[:, t, 1:NCHUNK], E1[:, MB:L].rearrange("p (c s) -> p c s", s=CH)[:, :, CH - 1])
                V.tensor_tensor(kt, kt, E3, ALU.mult)
                link(V.tensor_tensor(rt, rt, E1, ALU.mult))
                dve.wait_ge(rn_ready, t + 1)
                link(V.tensor_tensor(KKR, KKR, RN, ALU.mult))
                link(V.scalar_tensor_tensor(out=BB, in0=KKR, scalar=-1.0, in1=AA, op0=ALU.mult, op1=ALU.mult))
                V.tensor_tensor(KR[:, t, 0, :], KKR, E2, ALU.mult)
                V.tensor_tensor(BH[:, t, :], BB, E3, ALU.mult).then_inc(rw_elem, 1)

            piece = [FIRST_PIECE[len(PHASE_C) + len(PHASE_A)]]

            def pieces(k):
                for _ in range(k):
                    n, part, parts = PIECES[piece[0]]
                    if part == parts - 1:
                        job(n)
                    piece[0] += 1

            def jobs(k):
                n = PIECES[piece[0]][0]
                pieces(FIRST_PIECE.get(n + k, len(PIECES)) - FIRST_PIECE[n])

            def job(n):
                kind, a, b = JOBS[n]
                s = job_slot(n)
                one = pst[:, 2 * s, :]
                if kind in ("av", "proj", "wo"):
                    dve.wait_ge(dense_done, n + 1)
                if kind == "av":
                    cols = slice(2 * P * a, 2 * P * a + 2 * P)
                    if b == 0:
                        dve.wait_ge(yl_ready, 4)
                        V.tensor_copy(sb_vm[:, cols], pst[0:MB, 2 * s, 0:2 * P]).then_inc(job_out[kind], 1)
                    else:
                        V.tensor_copy(sb_v[:, b - 1, cols], pst[:, 2 * s, 0:2 * P]).then_inc(job_out[kind], 1)
                elif kind == "proj":
                    if a == br_order[0]:
                        dve.wait_ge(gates_in, 16)
                    else:
                        dve.wait_ge(gate_tanh, kind_no(n) // 4 - 1)
                    if a == br_order[0]:
                        V.scalar_tensor_tensor(out=merged[:, b, :], in0=gate_t[:, b, :], scalar=1.0, in1=one,
                                               op0=ALU.add, op1=ALU.mult).then_inc(job_out[kind], 1)
                    else:
                        V.scalar_tensor_tensor(out=gtmp[:, b % 2, :], in0=gate_t[:, b, :], scalar=1.0, in1=one,
                                               op0=ALU.add, op1=ALU.mult).then_inc(job_out[kind], 1)
                        dve.wait_ge(job_out[kind], kind_no(n) + 1)
                        V.tensor_tensor(merged[:, b, :], merged[:, b, :], gtmp[:, b % 2, :], ALU.add)\
                            .then_inc(merged_ready, 1)
                elif kind == "wo":
                    dve.wait_ge(x2_in, 16)
                    dst = x2[:, b, 2 * P * a:2 * P * a + 2 * P]
                    V.tensor_tensor(dst, pst[:, 2 * s, 0:2 * P], dst, ALU.add).then_inc(job_out[kind], 1)
                elif kind == "up":
                    i = kind_no(n)
                    r, q = ub[:, i % 2, :], usq[:, i % 2, :]
                    dve.wait_ge(job_out[kind], i + 1)
                    link(V.tensor_tensor(q, r, r, ALU.mult))
                    dve.wait_ge(u_hi_ready, i + 1)
                    V.tensor_tensor(u_lo[:, b, :], q, u_hi[:, b, :].bitcast(F32), ALU.subtract).then_inc(u_lo_ready, 1)
                elif kind == "down":
                    c, kk = b
                    if kk == FH // 2 - 1:
                        dve.wait_ge(dense_done, n + 1)
                        for blk in range(NB):
                            dst = x2[:, blk, T * c:T * c + T]
                            V.tensor_tensor(dst, pst[:, down_bank(c, blk), :], dst, ALU.add)\
                                .then_inc(job_out["down"], 1)

            def sb_keys():
                dve.wait_ge(sb_diag_zeroed, 1)
                dve.wait_ge(*all_out("ak", ("ak", 3, 0)))
                for h in range(SBH):
                    r = slice(HD * (h % 2), HD * (h % 2) + HD)
                    V.tensor_copy(sb_kmd[r, h // 2, MB * (h % 4):MB * (h % 4) + MB], sb_k[r, h // 2, 0:MB])\
                        .then_inc(sb_kmd_ready, 1)

            def sb_meta(grp):
                dve.wait_ge(zm_ln, grp + 1)
                V.scalar_tensor_tensor(out=sb_sm[:], in0=pst[:, 7, :], scalar=0.0, in1=sb_em[:], op0=ALU.max,
                                       op1=ALU.add).then_inc(zm_sp, 1)

            def sb_z(h):
                dve.wait_ge(z_ln, h + 1)
                V.scalar_tensor_tensor(out=sb_s[:, 0:T], in0=pst[:, 4, :], scalar=0.0, in1=sb_e[h % 2][:, 0:T],
                                       op0=ALU.max, op1=ALU.add)
                V.scalar_tensor_tensor(out=halves(sb_s[:, T:SB_N]), in0=pst[:, 5:7, 0:3 * P], scalar=0.0,
                                       in1=halves(sb_e[h % 2][:, T:SB_N]), op0=ALU.max, op1=ALU.add).then_inc(z_sp, 1)

            def sb_sums(h):
                dve.wait_ge(z_spm, h + 1)
                V.tensor_copy(sb_cs[:, 0:2 * T].rearrange("p (a b) -> p a b", a=2)[:, :, 0:P],
                              sb_s[:, 0:2 * T].rearrange("p (a b) -> p a b", a=2)[:, :, 0:P])
                c2, c1 = SB_COL[2], SB_COL[1]
                V.tensor_copy(sb_cs[:, c2:c2 + P], sb_s[:, c2:c2 + P])
                link(V.tensor_tensor(sb_cs[:, c2 + P:c2 + 2 * P], sb_s[:, c2 + P:c2 + 2 * P], sb_s[:, SB_COL[3]:SB_N],
                                     ALU.add))
                link(V.tensor_tensor(sb_cs[:, c1 + P:c2], sb_s[:, c1 + P:c2], sb_cs[:, c2:c2 + 2 * P], ALU.add))
                V.tensor_tensor(sb_cs[:, P:T], sb_s[:, P:T], sb_cs[:, c1:c2], ALU.add).then_inc(z_cs, 1)

            def sb_end(grp):
                for t in (2 * grp, 2 * grp + 1):
                    dve.wait_ge(yh_ready, y_count(BRANCH_SB) + t + 1)
                    V.tensor_tensor(y_lo[:, t, :], pst[:, 1 + 2 * (t % 2), :], y_hi[:, t, :].bitcast(F32),
                                    ALU.subtract).then_inc(yl_ready, 1)

            def ret_gate():
                dve.wait_ge(ret_qk_in, 48)
                for t in range(2):
                    V.tensor_tensor(rqd[:, t, :].rearrange("p (b i) -> p b i", b=NB),
                                    rq[:, t, :].rearrange("p (b i) -> p b i", b=NB),
                                    C("ret_qdec", P * t, P * t + P).unsqueeze(1).broadcast_to([P, NB, P]),
                                    ALU.mult).then_inc(rqd_ready, 1)
                dve.wait_ge(rg_tanh, 1)
                V.scalar_tensor_tensor(out=rg[:], in0=rth[:], scalar=1.0, in1=rg[:], op0=ALU.add, op1=ALU.mult)

            def ret_scores(b):
                n = P if b else MB
                dve.wait_ge(rkt_done, b + 1)
                V.tensor_tensor(rkd[0:n], pst[0:n, 4, 0:2 * P].rearrange("p (h d) -> p h d", h=RETH),
                                C("ret_kdec" if b else "ret_kdec_meta", rows=n).unsqueeze(2).broadcast_to([n, RETH, HD]),
                                ALU.mult).then_inc(rkd_ready, 1)
                if b:
                    dve.wait_ge(rs_done, b)
                    m = C("ret_mask").rearrange("p (h i) -> p h i", h=RETH)
                    for par_ in range(2):
                        V.tensor_tensor(rsc[:, par_:RETH:2, :], pst[:, 5 + par_, 0:2 * P].rearrange("p (h i) -> p h i", h=2),
                                        m[:, par_:RETH:2, :], ALU.mult).then_inc(rsc_ready, 1)

            def ret_out(b):
                if b < NB:
                    dve.wait_ge(rkv_done, b + 1)
                    if b == 0:
                        dve.wait_ge(rsz_zeroed, 1)
                    else:
                        dve.wait_ge(ro_done, b)
                    for h in range(RETH):
                        r = slice(HD * (h % 2), HD * (h % 2) + HD)
                        V.scalar_tensor_tensor(out=rsz[r, h, :], in0=rsz[r, h, :], scalar=RET_CHUNK_DECAY[h],
                                               in1=pst[r, 4, 2 * P + P * (h // 2):3 * P + P * (h // 2)],
                                               op0=ALU.mult, op1=ALU.add).then_inc(rstate, 1)
                    dve.wait_ge(rstate, 4 * b + 4)

            def ret_norm(h):
                y = ro[:, h, :]
                dve.wait_ge(rrs_ready, h + 1)
                link(V.tensor_tensor(y, y, rsq[:, h % 2, :], ALU.mult))
                V.scalar_tensor_tensor(out=y, in0=y, scalar=0.5, in1=rg[:, h, :], op0=ALU.mult, op1=ALU.mult)\
                    .then_inc(ry_ready, 1)
                dve.wait_ge(yh_ready, y_count(BRANCH_RET) + h + 1)
                V.tensor_tensor(y_lo[:, h, :], y, y_hi[:, h, :].bitcast(F32), ALU.subtract).then_inc(yl_ready, 1)

            def sw_norm(i):
                dve.wait_ge(drs_ready, i + 1)
                y = dq[:, i - 1, :] if i else dk[:]
                V.scalar_tensor_tensor(out=y, in0=y, scalar=gain_q[:] if i else PAR("kn", 0),
                                       in1=dsq[:, i % 2, 0:T if i else L], op0=ALU.mult, op1=ALU.mult)\
                    .then_inc(dn_ready, 1)

            def sw_keys():
                dve.wait_ge(dn_ready, 1)
                dve.wait_ge(ro_done, NB)
                for kv in range(2):
                    own = slice(HD * kv, HD * kv + HD)
                    V.tensor_copy(dk2[own, kv, :], dk[own, :]).then_inc(dk2_own, 1)

            def sw_scores(i):
                b, kv = i // 2, i % 2
                w = MB + (2 * P if b else P)
                st, sc = dst_[:, i % 2], dsc[:, i % 2]
                if i >= 2:
                    dve.wait_ge(dpt_done, i - 1)
                dve.wait_ge(ds_done, i + 1)
                for j in range(4):
                    slope = 2.0 ** (-8.0 * (4 * kv + j + 1) / SWH)
                    V.scalar_tensor_tensor(out=sc[:, j, MB:w], in0=C("sw_bias", MB if b else MB + P, MB + 2 * P),
                                           scalar=slope, in1=pst[:, 4 + j % 2, 2 * P * (j // 2):2 * P * (j // 2) + w - MB],
                                           op0=ALU.mult, op1=ALU.add)
                for par_ in range(2):
                    last = V.tensor_tensor(sc[:, par_:4:2, 0:MB],
                                           pst[:, 6 + par_, 0:2 * MB].rearrange("p (h m) -> p h m", h=2),
                                           C("sw_bias", 0, MB).unsqueeze(1).broadcast_to([P, 2, MB]), ALU.add)
                last.then_inc(ds_read, 1)
                dve.wait_ge(ds_read, i + 1)
                sink = par[:, PARAM_AT["sink"][0] + 4 * kv:PARAM_AT["sink"][0] + 4 * kv + 4]
                link(V.tensor_reduce(st[:, 0, :], sc[:, :, 0:w], AX.X, ALU.max))
                link(V.tensor_tensor(st[:, 0, :], st[:, 0, :], sink, ALU.max))
                link(V.tensor_scalar(st[:, 0, :], st[:, 0, :], -1.0, None, ALU.mult))
                V.tensor_tensor(st[:, 2, :], st[:, 0, :], sink, ALU.add).then_inc(dmx_ready, 1)

            def sw_probs(i):
                w = MB + (2 * P if i // 2 else P)
                st, sc = dst_[:, i % 2], dsc[:, i % 2]
                dve.wait_ge(dexp_ready, 5 * i + 5)
                link(V.tensor_tensor(st[:, 3, :], st[:, 1, :], st[:, 2, :], ALU.add))
                link(V.reciprocal(st[:, 4, :], st[:, 3, :]))
                inv = st[:, 4, :].unsqueeze(2)
                V.tensor_tensor(dpm[:, i % 2], sc[:, :, 0:MB], inv.broadcast_to([P, 4, MB]), ALU.mult)
                V.tensor_tensor(sc[:, :, MB:w], sc[:, :, MB:w], inv.broadcast_to([P, 4, w - MB]), ALU.mult)\
                    .then_inc(dp_ready, 1)

            def sw_turn(i):
                dve.wait_ge(dpt_done, i + 1)
                if i // 2:
                    V.tensor_copy(dpt[:, i % 2, 1, :], pst[:, 3, :])
                V.tensor_copy(dpmt[:, i % 2, :], pst[:, 7, P:2 * P]).then_inc(dpt_dve, 1)

            def sw_out(i):
                b, kv = i // 2, i % 2
                if i < YSW_STEPS:
                    return
                ts, cols = slice(2 * kv, 2 * kv + 2), slice(P * b, P * b + P)
                dve.wait_ge(yh_ready, y_count(BRANCH_SW) + i - YSW_STEPS + (1 if i == YSW_STEPS else 2))
                V.tensor_tensor(y_lo[:, ts, cols], pst[:, 6, P:3 * P].rearrange("p (t q) -> p t q", t=2),
                                y_hi[:, ts, cols].bitcast(F32), ALU.subtract)\
                    .then_inc(*((ysw_ready, 1) if i < 2 * NB - 1 else (yl_ready, 4)))
                if i == YSW_STEPS:
                    dve.wait_ge(yh_ready, y_count(BRANCH_SW) + 2)
                    V.tensor_tensor(y_lo[:, :, 0:P * b], ysw[:], y_hi[:, :, 0:P * b].bitcast(F32), ALU.subtract)

            def merge_tile(k):
                dve.wait_ge(m_hi, k + 1)
                V.scalar_tensor_tensor(out=h_lo[:, k, 0:T], in0=merged[:, k, :], scalar=0.5,
                                       in1=h_hi[:, k, 0:T].bitcast(F32), op0=ALU.mult, op1=ALU.subtract)\
                    .then_inc(m_lo, 1)

            def norm2(b):
                dve.wait_ge(rs2_ready, b + 1)
                V.tensor_scalar(h2n[:, b, :], x2[:, b, :], ss2[:, 1, b:b + 1], None, ALU.mult).then_inc(h2n_ready, 1)

            def norm2_turn(b):
                for k in range(KD):
                    if k % 4 == 0:
                        dve.wait_ge(h2hi_ready, KD * b + k + 4)
                    V.scalar_tensor_tensor(out=h_lo[:, k, P * b:P * b + P], in0=norm2_psum(b, k),
                                           scalar=PAR("norm2_g", k), in1=h_hi[:, k, P * b:P * b + P].bitcast(F32),
                                           op0=ALU.mult, op1=ALU.subtract).then_inc(h2lo_ready, 1)

            dve.wait_ge(table_in, 32)
            for b, (n, c0) in enumerate(rw_blocks):
                m = chunks_of(b)[0][2]
                dve.wait_ge(tok_done, 4 * b + 3)
                V.tensor_copy(KT[0:n, :], pst[0:n, 6, :]).then_inc(tok_dve, 1)
                dve.wait_ge(tok_done, 4 * b + 4)
                V.tensor_copy(BT[0:n, :], pst[0:n, 7, :]).then_inc(tok_dve, 1)
                for g in range(2):
                    for par_ in range(2):
                        dve.wait_ge(am_done, 4 * b + 2 * g + par_ + 1)
                        V.tensor_tensor(
                            AM[0:n, 4 * g + par_:4 * g + 4:2, :, 0:m],
                            pst[0:n, 4 + 2 * g + par_, :].rearrange("p (h q c) -> p h q c", h=2, q=4)[:, :, :, 0:m],
                            four(C("rw_mask", rows=n))[:, :, 0:m].unsqueeze(1).broadcast_to([n, 2, 4, m]),
                            ALU.mult).then_inc(am_ready, 1)
                idb = C("ident_chunk", 0, m, n).unsqueeze(1).broadcast_to([n, 4, m])
                for l in range(levels_of[b]):
                    for g in range(2):
                        hs = slice(4 * g, 4 * g + 4)
                        step = level0[b] + l
                        if l == 0:
                            dve.wait_ge(m_ready[g], step + 1)
                            V.tensor_tensor(XX[0:n, hs, 0:m], MM[0:n, step % 2, hs, 0:m], idb, ALU.add)
                            dve.wait_ge(c1_done[g], step + 1)
                            V.tensor_tensor(TT[0:n, hs, 0:m], four(pst[0:n, 4 + 2 * g, 0:256])[:, :, 0:m],
                                            idb, ALU.add).then_inc(x_ready[g], 1)
                            dve.wait_ge(x_ready[g], step + 1)
                            continue
                        dve.wait_ge(tu_done[g], step - b)
                        if l < levels_of[b] - 1:
                            V.tensor_tensor(TT[0:n, hs, 0:m], TT[0:n, hs, 0:m],
                                            four(pst[0:n, 4 + 2 * g, 256:512])[:, :, 0:m], ALU.add)
                        V.tensor_tensor(XX[0:n, hs, 0:m], XX[0:n, hs, 0:m],
                                        four(pst[0:n, 5 + 2 * g, 0:256])[:, :, 0:m], ALU.add).then_inc(x_ready[g], 1)
                        dve.wait_ge(x_ready[g], step + 1)
                for g in range(2):
                    dve.wait_ge(wz_done, 2 * b + g + 1)
                    V.tensor_copy(FK[0:n, 4 * g:4 * g + 4, :, :],
                                  pst[0:n, 5 + 2 * g, :].rearrange("p (h a d) -> p h a d", h=4, a=2)).then_inc(wz_ready, 1)
                for g in range(2):
                    ts = slice(2 * g, 2 * g + 2)
                    for ci, (_, col, _) in enumerate(chunks_of(b)):
                        c = 2 * b - 1 + ci if b else 0
                        bank = 4 + 2 * g + ci
                        dve.wait_ge(mn_done, 2 + 4 * (b - 1) + 2 * g + ci + 1 if b else g + 1)
                        gcb = GC[:, ts, c:c + 1].broadcast_to([P, 2, HD])
                        nps = pst[:, bank, 256:384].rearrange("p (h d) -> p h d", h=2)
                        if b == 0:
                            V.tensor_tensor(QQ[:, ts, :], nps, gcb, ALU.mult).then_inc(q_ready if g else mn_ready, 1)
                            continue
                        rr = KR[:, ts, 1, col:col + CH]
                        V.tensor_tensor(rr, rr, pst[:, bank, 0:128].rearrange("p (h d) -> p h d", h=2), ALU.add)
                        for hf in range(2):
                            r = slice(HD * hf, HD * hf + HD)
                            V.tensor_tensor(MD[r, ci, ts, HD * hf:HD * hf + HD],
                                            pst[r, bank, 128:256].rearrange("p (h d) -> p h d", h=2),
                                            C("ident_chunk")[r].unsqueeze(1).broadcast_to([HD, 2, HD]), ALU.add)
                        V.tensor_tensor(NG[:, ci, ts, :], nps, gcb, ALU.mult).then_inc(mn_ready, 1)
                if b == 0:
                    dve.wait_ge(q_ready, 1)
                    dve.wait_ge(diag_zeroed, 2)
                    continue
                for ci in range(2):
                    c = 2 * b - 1 + ci
                    if c == NCHUNK - 1:
                        continue
                    dve.wait_ge(qn_done, c)
                    dve.wait_ge(qd_ready, 2 * c)
                    dve.wait_ge(mn_ready, 1 + 4 * b)
                    link(V.tensor_tensor(QQ[:], four(pst[:, 4 + ci, 0:256]),
                                         GC[:, :, c:c + 1].broadcast_to([P, 4, HD]), ALU.mult))
                    V.tensor_tensor(QQ[:], QQ[:], NG[:, ci], ALU.add).then_inc(q_ready, 1)
                    dve.wait_ge(q_ready, c + 1)
            def post_center(t):
                dve.wait_ge(post_done, 3 * t + 1)
                V.scalar_tensor_tensor(out=KR[:, t, 0, MB:L], in0=pst[:, 4 - 3 * (t % 2), :], scalar=-1.0 / HD,
                                       in1=KR[:, t, 0, MB:L], op0=ALU.mult, op1=ALU.add).then_inc(postc_ready, 1)

            post_center(0)
            for t in range(4):
                y = KR[:, t, 0, MB:L]
                dve.wait_ge(post_done, 3 * t + 2)
                V.tensor_tensor(post["bon"][:], pst[:, 5, :], RV[:, t, MB:L], ALU.mult)
                if t < 3:
                    post_center(t + 1)
                dve.wait_ge(postr_ready, t + 1)
                link(V.tensor_tensor(y, y, post["rs"][:], ALU.mult))
                link(V.tensor_scalar(y, y, PAR("rw_ln_g", t), PAR("rw_ln_b", t), ALU.mult, ALU.add))
                link(V.tensor_tensor(y, y, post["bon"][:], ALU.add))
                dve.wait_ge(post_done, 3 * t + 3)
                V.tensor_tensor(y, y, pst[:, 6, :], ALU.mult).then_inc(yf_ready, 1)
                dve.wait_ge(yh_ready, t + 1)
                if t == 0:
                    for i in range(2):
                        dve.wait_ge(spill_out[i], 16 * (len(SPILL_NO) // 2))
                V.tensor_tensor(y_lo[:, t, :], y, y_hi[:, t, :].bitcast(F32), ALU.subtract).then_inc(yl_ready, 1)

            run_after_rw(pieces, jobs, dict(
                sb_keys=sb_keys, sb_meta=sb_meta, sb_z=sb_z, sb_sums=sb_sums, sb_end=sb_end, ret_gate=ret_gate,
                ret_scores=ret_scores, ret_out=ret_out, ret_norm=ret_norm, sw_norm=sw_norm, sw_keys=sw_keys,
                sw_scores=sw_scores, sw_probs=sw_probs, sw_turn=sw_turn, sw_out=sw_out,
                merge_tile=merge_tile, norm2=norm2, norm2_turn=norm2_turn))

        @block.tensor
        def _(pe):
            M = nc.tensor.matmul

            def wslice(tile, u, k):
                return tile[:, u % W_SLOTS, P * k:P * k + P]

            def product3(out, terms, first=True, final=True):
                for i, ((lh, ll), (rh, rl)) in enumerate(terms):
                    M(out, lh, rh, start=(first and i == 0), stop=False)
                    M(out, lh, rl, start=False, stop=False)
                    last = M(out, ll, rh, start=False, stop=(final and i == len(terms) - 1))
                return last

            def job_begin(n):
                s = job_slot(n)
                if n >= 2:
                    pe.wait_ge(*emptied(n - 2))
                pe.wait_ge(lo_ready, UNIT_NO[units_of(JOBS[n])[-1]] + 1)
                return s

            def feature_job(job, cols, part=0, parts=1):
                n = JOB_NO[job]
                s = job_begin(n) if part == 0 else job_slot(n)
                u = UNIT_NO[units_of(job)[0]]
                for i, (c0, c1) in enumerate(cols):
                    if len(cols) == parts == 2 and i != part:
                        continue
                    ks = range(KD) if len(cols) == 2 else range(KD * part // parts, KD * (part + 1) // parts)
                    for k in ks:
                        if n == 0:
                            pe.wait_ge(hlo_ready, 2 * k + 2)
                        last = product3(pst[:, 2 * s + i, 0:c1 - c0],
                                        [((wslice(w_hi, u, k), wslice(w_lo, u, k)),
                                          (h_hi[:, k, c0:c1], h_lo[:, k, c0:c1]))], k == 0, k == KD - 1)
                if part == parts - 1:
                    last.then_inc(dense_done, 1)

            ALL = [(0, HL), (HL, L)]
            pe.wait_ge(const_in, 32)
            pe.wait_ge(hn_ready, NB + 1)
            for k in range(KD):
                if k >= 4:
                    pe.wait_ge(hlo_ready, 2 * (k - 4) + 2)
                for b in range(NB):
                    nc.tensor.transpose(pst[:, 2 + k % 4, P * b:P * b + P], xt[:, b, P * k:P * k + P], ident)
                if k >= 2:
                    pe.wait_ge(hlo_ready, 2 * (k - 2) + 2)
                nc.tensor.transpose(pst[:, 6 + k % 2, 0:MB], xm[:, P * k:P * k + P], cst[0:MB, 0:MB])\
                    .then_inc(ht_done, 1)

            def lora(t):
                if t == 0:
                    pe.wait_ge(wa_tanh, 1)
                    pe.wait_ge(table_in, 32)
                else:
                    pe.wait_ge(kkclamped, t)
                    pe.wait_ge(lora_act, 2 * t)
                for i in range(2):
                    last = M(pst[:, 4 + i, 0:HL], w2[:, P * t:P * t + P], WA[0:HD, HL * i:HL * i + HL],
                             start=True, stop=True)
                last.then_inc(lora_done, 1)
                for i in range(2):
                    last = M(pst[:, 6 + i, 0:HL], a2[:, P * t:P * t + P], WA[HD:P, HL * i:HL * i + HL],
                             start=True, stop=True)
                last.then_inc(lora_done, 1)

            def kksum(t):
                pe.wait_ge(kksq_ready, t + 1)
                pe.wait_ge(lora_act, 2 * t + 1)
                for i in range(2):
                    last = M(pst[:, 4 + i, 0:HL], headsum, tt["SQ"][:, HL * i:HL * i + HL], start=True, stop=True)
                last.then_inc(kksum_done, 1)

            feature_job(PHASE_C[0], ALL)
            feature_job(PHASE_C[1], ALL)
            for t in range(4):
                for i in range(3):
                    feature_job(PHASE_C[2 + 3 * t + i], ALL)
                    if t >= 1 and i == 0:
                        kksum(t - 1)
                lora(t)

            piece = [FIRST_PIECE[len(PHASE_C)]]

            def pieces(k):
                for _ in range(k):
                    n, part, parts = PIECES[piece[0]]
                    job(n, part, parts)
                    piece[0] += 1

            def jobs(k):
                n = PIECES[piece[0]][0]
                pieces(FIRST_PIECE.get(n + k, len(PIECES)) - FIRST_PIECE[n])

            def job(n, part, parts):
                kind, a, b = JOBS[n]
                u = UNIT_NO[units_of(JOBS[n])[0]]
                if kind in ("aq", "bq", "bg", "dq", "gate", "rgate"):
                    feature_job(JOBS[n], [(MB, L)], part, parts)
                elif kind in ("ak", "bk", "dk"):
                    feature_job(JOBS[n], ALL, part, parts)
                elif kind in ("av", "bv", "dv"):
                    s = job_begin(n)
                    r, toks = (P, slice(MB + P * (b - 1), MB + P * b)) if b else (MB, slice(0, MB))
                    us = u % W_SLOTS
                    if kind == "dv":
                        o = pst[0:r, 2 * s, 0:P]
                        wsl = lambda w, k: wslice(w, u, k)
                    else:
                        o = pst[0:r, 2 * s, 0:2 * P].rearrange("p (a f) -> p a f", a=2)
                        wsl = lambda w, k: w[:, us:us + 2, P * k:P * k + P]
                    product3(o, [((h_hi[:, k, toks], h_lo[:, k, toks]), (wsl(w_hi, k), wsl(w_lo, k)))
                                 for k in range(KD)]).then_inc(dense_done, 1)
                elif kind == "proj":
                    s = job_begin(n)
                    us = u % W_SLOTS
                    for k in range(4):
                        if b == 0:
                            pe.wait_ge(yl_ready, y_count(a) + k + 1)
                        ws = slice(2 * P * k + P * (b % 2), 2 * P * k + P * (b % 2) + P)
                        last = product3(pst[:, 2 * s, :], [((w_hi[:, us, ws], w_lo[:, us, ws]),
                                                            (y_hi[:, k, :], y_lo[:, k, :]))], k == 0, k == 3)
                    last.then_inc(dense_done, 1)
                elif kind == "wo":
                    s = job_begin(n)
                    us = u % W_SLOTS
                    toks = slice(P * b, P * b + P)
                    for k in range(KD):
                        if a == b == 0:
                            pe.wait_ge(m_lo, k + 1)
                        last = product3(pst[:, 2 * s, 0:2 * P].rearrange("p (a f) -> p a f", a=2),
                                        [((h_hi[:, k, toks], h_lo[:, k, toks]),
                                          (w_hi[:, us:us + 2, P * k:P * k + P], w_lo[:, us:us + 2, P * k:P * k + P]))],
                                        k == 0, k == KD - 1)
                    last.then_inc(dense_done, 1)
                elif kind == "up":
                    if a == 1 and b < 2:
                        pe.wait_ge(job_out["down"], 4 + 2 * job_slot(n) + 1)
                    s = job_begin(n)
                    for k in range(KD):
                        if a == b == 0:
                            pe.wait_ge(h2lo_ready, KD * (NB - 1) + k + 1)
                        last = product3(pst[:, 2 * s, :], [((wslice(w_hi, u, k), wslice(w_lo, u, k)),
                                                            (h_hi[:, k, 0:T], h_lo[:, k, 0:T]))], k == 0, k == KD - 1)
                    last.then_inc(dense_done, 1)
                elif kind == "down":
                    c, kk = b
                    pe.wait_ge(u_lo_ready, FH * a + 2 * kk + 2)
                    if kk == 0 and a == 1:
                        pe.wait_ge(job_out["down"], 8)
                    pe.wait_ge(lo_ready, u + 1)
                    us = u % W_SLOTS
                    for j in range(2):
                        f = 2 * kk + j
                        ws = slice(T * j, T * j + T)
                        for blk in range(NB):
                            o = pst[:, down_bank(c, blk), :]
                            toks = slice(P * blk, P * blk + P)
                            M(o, u_hi[:, f, toks], w_hi[:, us, ws], start=(f == 0), stop=False)
                            M(o, u_hi[:, f, toks], w_lo[:, us, ws], start=False, stop=False)
                            last = M(o, u_lo[:, f, toks], w_hi[:, us, ws], start=False, stop=(f == FH - 1))
                    last.then_inc(dense_done, 1)

            def sb_rows(h):
                return slice(HD * (h % 2), HD * (h % 2) + HD)

            def sb_meta(grp):
                if grp == 0:
                    pe.wait_ge(sb_kmd_ready, SBH)
                else:
                    pe.wait_ge(zm_a, grp)
                for t in (2 * grp, 2 * grp + 1):
                    last = M(pst[:, 7, :], sb_kmd[:, t, :], sb_q[:, t, :], start=(t == 2 * grp), stop=(t == 2 * grp + 1))
                last.then_inc(zm_done, 1)

            SB_AT = [(4, 0), (5, 0), (6, 0), (6, 2 * P)]

            def sb_z(h):
                if h:
                    pe.wait_ge(z_a, h)
                r = sb_rows(h)
                for kb in range(NB):
                    bank, c = SB_AT[kb]
                    last = M(pst[:, bank, c:c + T - P * kb], sb_k[r, h // 2, MB + P * kb:MB + P * kb + P],
                             sb_q[r, h // 2, P * kb:T], start=(kb < 3), stop=True, skip_group_check=(kb == 3))
                last.then_inc(z_done, 1)

            def sb_arg(h):
                pe.wait_ge(z_cs, h + 1)
                for kb in range(NB):
                    bank, c = SB_AT[kb]
                    w = SBW[kb]
                    last = M(pst[:, bank, c:c + w], C("suffix"), sb_s[:, SB_COL[kb]:SB_COL[kb] + w], start=False,
                             stop=True, skip_group_check=True)
                    if kb < 3:
                        rhs = (sb_s if kb == 2 else sb_cs)[:, SB_COL[kb + 1]:SB_COL[kb + 1] + w - P]
                        last = M(pst[:, bank, c + P:c + w], C("neg_ones"), rhs, start=False, stop=True,
                                 skip_group_check=True)
                last.then_inc(z_arg, 1)
                grp, j = h // 4, h % 4
                if j == 0:
                    pe.wait_ge(zm_sp, grp + 1)
                    M(pst[:, 7, :], C("suffix_meta"), sb_sm[:], start=False, stop=True, skip_group_check=True)
                o = 3 * MB - MB * j
                last = M(pst[:, 7, :], C("carry_meta", o, o + P), sb_cs[:, 0:T], start=False, stop=True,
                         skip_group_check=True)
                if j == 3:
                    last.then_inc(zm_arg, 1)

            def sb_o(h):
                pe.wait_ge(z_am, h + 1)
                grp, t = h // 4, h // 2
                if h % 4 == 0 and grp:
                    pe.wait_ge(yl_ready, y_count(BRANCH_SB) + 2 * grp)
                if h == 0:
                    pe.wait_ge(*all_out("av", ("av", 1, NB)))
                r = sb_rows(h)
                bank = 1 + 2 * (t % 2)
                for kb in range(NB):
                    last = M(pst[r, bank, P * kb:T], sb_v[:, kb, HD * h:HD * h + HD],
                             sb_e[h % 2][:, SB_COL[kb]:SB_COL[kb] + SBW[kb]],
                             start=(kb == 0), stop=False)
                last.then_inc(sb_used, 1)

            def sb_end(grp):
                pe.wait_ge(sb_vmd_ready, 16 * SBH)
                pe.wait_ge(zm_a, grp + 1)
                for h in range(4 * grp, 4 * grp + 4):
                    last = M(pst[sb_rows(h), 1 + 2 * (h // 2 % 2), :], sb_vmd[:, h, :], sb_em[:], start=False, stop=True)
                    if h % 2:
                        last.then_inc(o_done, 1)

            def ret_scores(b):
                n, c0 = rw_blocks[b]
                toks = slice(c0, c0 + n)
                if b == 0:
                    pe.wait_ge(ret_qk_in, 48)
                    pe.wait_ge(yl_ready, y_count(BRANCH_RET))
                else:
                    pe.wait_ge(rstate, 4 * b)
                for t in range(2):
                    last = nc.tensor.transpose(pst[0:n, 4, P * t:P * t + P], rk[:, t, toks], ident)
                last.then_inc(rkt_done, 1)
                if b:
                    if b > 1:
                        pe.wait_ge(rsc_ready, 2 * (b - 1))
                    for h in range(RETH):
                        r = slice(HD * (h % 2), HD * (h % 2) + HD)
                        last = M(pst[:, 5 + h % 2, P * (h // 2):P * (h // 2) + P], rk[r, h // 2, toks],
                                 rq[r, h // 2, P * (b - 1):P * b], start=True, stop=True)
                    last.then_inc(rs_done, 1)

            def ret_out(b):
                n, c0 = rw_blocks[b]
                if b < NB:
                    pe.wait_ge(rkd_ready, b + 1)
                    if b == 0:
                        pe.wait_ge(ret_v_in, 16)
                    vv = rv[:, b - 1, :] if b else rvm[:]
                    for h in range(RETH):
                        last = M(pst[HD * (h % 2):HD * (h % 2) + HD, 4, 2 * P + P * (h // 2):3 * P + P * (h // 2)],
                                 rkd[0:n, h, :], vv[:, P * h:P * h + P], start=True, stop=True)
                    last.then_inc(rkv_done, 1)
                if b:
                    pe.wait_ge(rsc_ready, 2 * b)
                    if b == 1:
                        pe.wait_ge(rqd_ready, 2)
                    if b >= 3:
                        pe.wait_ge(ro_ready, b - 2)
                    for h in range(RETH):
                        o = pst[:, 7 if b % 2 else 1, P * h:P * h + P]
                        M(o, rv[:, b - 1, P * h:P * h + P], rsc[:, h, :], start=True, stop=False)
                        last = M(o, rsz[:, h, :], rqd[:, h // 2, P * (b - 1):P * b], start=False, stop=True)
                    last.then_inc(ro_done, 1)

            def ret_sum(h):
                pe.wait_ge(rsq_ready, h + 1)
                M(pst[:, 4 + h % 2, :], C("neg_ones"), rsq[:, h % 2, :], start=True, stop=True).then_inc(rss_done, 1)

            def sw_sum(i):
                pe.wait_ge(dsq_ready, i + 1)
                if i:
                    pe.wait_ge(drs_ready, i)
                    last = M(pst[:, 3, :], headsum, dsq[:, i % 2, 0:T], start=True, stop=True)
                else:
                    for hf in range(2):
                        last = M(pst[:, 1 + 2 * hf, 0:HL], headsum, dsq[:, 0, HL * hf:HL * hf + HL],
                                 start=True, stop=True)
                last.then_inc(dss_done, 1)

            def sw_scores(i):
                b, kv = i // 2, i % 2
                if i == 0:
                    pe.wait_ge(rrs_ready, RETH)
                    pe.wait_ge(dn_ready, 5)
                    pe.wait_ge(dk2_own, 2)
                    pe.wait_ge(dk2_in, 32)
                else:
                    pe.wait_ge(ds_read, i)
                w = 2 * P if b else P
                for j in range(4):
                    h = 4 * kv + j
                    r = slice(HD * (h % 2), HD * (h % 2) + HD)
                    o = 2 * P * (j // 2)
                    M(pst[:, 4 + j % 2, o:o + w], dq[r, h // 2, P * b:P * b + P],
                      dk2[r, kv, MB + P * (b + 1) - w:MB + P * (b + 1)], start=True, stop=True)
                if i >= 2:
                    pe.wait_ge(ysw_ready, i - 1)
                for j in range(4):
                    h = 4 * kv + j
                    r = slice(HD * (h % 2), HD * (h % 2) + HD)
                    last = M(pst[:, 6 + j % 2, MB * (j // 2):MB * (j // 2) + MB], dq[r, h // 2, P * b:P * b + P],
                             dk2[r, kv, 0:MB], start=True, stop=True)
                last.then_inc(ds_done, 1)

            def sw_turn(i):
                b = i // 2
                pe.wait_ge(dp_ready, i + 1)
                own = MB + (P if b else 0)
                if i:
                    pe.wait_ge(dpt_act, i)
                    pe.wait_ge(dpt_dve, i)
                for j in range(4):
                    p_ = dsc[:, i % 2, j, :]
                    c = slice(P * j, P * j + P)
                    nc.tensor.transpose(pst[:, 1, c], p_[:, own:own + P], ident)
                    if b:
                        nc.tensor.transpose(pst[:, 3, c], p_[:, MB:MB + P], ident)
                nc.tensor.transpose(pst[:, 7, P:2 * P], dpm[:, i % 2].rearrange("p h m -> p (h m)"), ident)\
                    .then_inc(dpt_done, 1)

            def sw_out(i):
                b, kv = i // 2, i % 2
                pe.wait_ge(dpt_act, i + 1)
                pe.wait_ge(dpt_dve, i + 1)
                if i == 0:
                    pe.wait_ge(sw_in, 48)
                    pe.wait_ge(sw_vmd_ready, 16 * 8)
                else:
                    pe.wait_ge(ysw_ready, i)
                vc = slice(HD * kv, HD * kv + HD)
                for par_ in range(2):
                    o = pst[HD * par_:HD * par_ + HD, 6, P:3 * P].rearrange("p (t q) -> p t q", t=2)

                    def pick(which):
                        return dpt[:, i % 2, which, :].rearrange("p (t s q) -> p s t q", t=2, s=2)[:, par_]
                    M(o, dv[:, b, vc], pick(0), start=True, stop=True)
                    if b:
                        M(o, dv[:, b - 1, vc], pick(1), start=False, stop=True, skip_group_check=True)
                    for t in range(2):
                        last = M(o[:, t], dvmd[:, kv, 2 * t + par_, :], dpmt[:, i % 2, :], start=False, stop=True,
                                 skip_group_check=True)
                last.then_inc(do_done, 1)

            def norm2_turn(b):
                pe.wait_ge(h2n_ready, b + 1)
                if b >= 2:
                    pe.wait_ge(h2lo_ready, KD * (b - 1))
                for k in range(KD):
                    last = nc.tensor.transpose(norm2_psum(b, k), h2n[:, b, P * k:P * k + P], ident)
                    if k % 4 == 3:
                        last.then_inc(h2t_done, 1)

            kksum(3)
            pe.wait_ge(rw_elem, 4)
            for b, (n, c0) in enumerate(rw_blocks):
                toks = slice(c0, c0 + n)
                chunks = chunks_of(b)
                m = chunks[0][2]
                for q, tile in enumerate((lambda t: KR[:, t, 0, toks], lambda t: RV[:, t, toks],
                                          lambda t: KH[:, t, toks], lambda t: BH[:, t, toks])):
                    if b >= 1:
                        pe.wait_ge(mn_ready, 1 + 4 * (b - 1))
                        pe.wait_ge(q_ready, min(2 * b - 1, NCHUNK - 1))
                    if q == 2 and b >= 2:
                        pe.wait_ge(yy_copied, 2 * (b - 1))
                    for t in range(4):
                        last = nc.tensor.transpose(pst[0:n, 4 + q, P * t:P * t + P], tile(t), ident)
                    last.then_inc(tok_done, 1)
                fill = RW_FILL[b]
                pe.wait_ge(tok_act, 2 * b + 2)
                pe.wait_ge(tok_dve, 2 * b + 2)
                for g in range(2):
                    for ab, keys in ((0, KH), (1, BH)):
                        for t in (2 * g, 2 * g + 1):
                            for par_ in range(2):
                                r = slice(HD * par_, HD * par_ + HD)
                                o = 256 * (t % 2) + 128 * ab
                                for rows, col, _ in chunks:
                                    last = M(pst[rows, 4 + 2 * g + par_, o:o + 128]
                                             .rearrange("p (a c) -> p a c", a=2)[:, :, 0:m],
                                             keys[r, t, col:col + m], KR[r, t, :, col:col + m], start=True, stop=True)
                                if ab == 1 and t % 2:
                                    last.then_inc(am_done, 1)
                    if g == 0:
                        pieces(fill["score"])
                for l in range(levels_of[b]):
                    step = level0[b] + l
                    for g in range(2):
                        pe.wait_ge(m_ready[g], step + 1)
                        if l:
                            pe.wait_ge(x_ready[g], step)
                        for h in range(4 * g, 4 * g + 4):
                            o = CH * (h % 4)
                            for rows, _, _ in chunks:
                                last = M(pst[rows, 4 + 2 * g, o:o + m], MM[rows, step % 2, h, 0:m],
                                         TT[rows, h, 0:m] if l else C("ident_chunk", 0, m)[rows],
                                         start=True, stop=True)
                        last.then_inc(c1_done[g], 1)
                    pieces(fill["c1"][l])
                    for g in range(2 if l else 0):
                        pe.wait_ge(c1_copied[g], step - b)
                        for h in range(4 * g, 4 * g + 4):
                            o = CH * (h % 4)
                            if l < levels_of[b] - 1:
                                for rows, _, _ in chunks:
                                    M(pst[rows, 4 + 2 * g, 256 + o:256 + o + m], XX[rows, h, 0:m], C1[rows, h, 0:m],
                                      start=True, stop=True)
                        for h in range(4 * g, 4 * g + 4):
                            o = CH * (h % 4)
                            for rows, _, _ in chunks:
                                last = M(pst[rows, 5 + 2 * g, o:o + m], C1[rows, h, 0:m], XX[rows, h, 0:m],
                                         start=True, stop=True)
                        last.then_inc(tu_done[g], 1)
                    pieces(fill["tu"][l])
                for g in range(2):
                    pe.wait_ge(x_ready[g], level0[b] + levels_of[b])
                    for h in range(4 * g, 4 * g + 4):
                        for rows, _, _ in chunks:
                            last = M(pst[rows, 4 + 2 * g, HD * (h % 4):HD * (h % 4) + HD], AM[rows, h, 0, 0:m],
                                     VT[rows, HD * h:HD * h + HD], start=True, stop=True)
                    last.then_inc(f_done, 1)
                pieces(fill["f"])
                for g in range(2):
                    pe.wait_ge(f_copied, 2 * b + g + 1)
                    for h in range(4 * g, 4 * g + 4):
                        for rows, _, _ in chunks:
                            last = M(pst[rows, 5 + 2 * g, P * (h % 4):P * (h % 4) + P].rearrange("p (a d) -> p a d", a=2),
                                     XX[rows, h, 0:m], FK[rows, h, :, :], start=True, stop=True)
                    last.then_inc(wz_done, 1)
                pieces(fill["wz"])
                for g in range(2):
                    pe.wait_ge(wz_ready, 2 * b + g + 1)
                    for ci, (rows, _, _) in enumerate(chunks):
                        bank = 4 + 2 * g + ci
                        for h in range(4 * g, 4 * g + 4):
                            out_rows = slice(HD * (h % 2), HD * (h % 2) + HD)
                            cc = HD * (h // 2 % 2)
                            hc = slice(HD * h, HD * h + HD)
                            if b:
                                M(pst[out_rows, bank, cc:cc + CH], FK[rows, h, 0, :], AM[rows, h, 3, :],
                                  start=True, stop=True)
                                M(pst[out_rows, bank, 128 + cc:128 + cc + HD], FK[rows, h, 0, :], BT[rows, hc],
                                  start=True, stop=True)
                            M(pst[out_rows, bank, 256 + cc:256 + cc + HD], KT[rows, hc], VT[rows, hc],
                              start=True, stop=False)
                            last = M(pst[out_rows, bank, 256 + cc:256 + cc + HD], BT[rows, hc], FK[rows, h, 1, :],
                                     start=False, stop=True)
                        last.then_inc(mn_done, 1)
                    pieces(fill["end" if g else "mn"])
                if b == 0:
                    continue
                pe.wait_ge(mn_ready, 1 + 4 * b)
                for ci, (rows, _, _) in enumerate(chunks):
                    for h in range(RWH):
                        dst = pst[HD * (h % 2):HD * (h % 2) + HD, 6 + ci, CH * (h // 2):CH * (h // 2) + CH]
                        M(dst, VT[rows, HD * h:HD * h + HD], AM[rows, h, 1, :], start=(h < 2), stop=True,
                          skip_group_check=True)
                        M(dst, FK[rows, h, 1, :], AM[rows, h, 3, :], start=False, stop=True, skip_group_check=True)
                for ci, (_, col, _) in enumerate(chunks):
                    c = 2 * b - 1 + ci
                    pe.wait_ge(q_ready, c)
                    if c < NCHUNK - 1:
                        for t in range(4):
                            last = M(pst[:, 4 + ci, HD * t:HD * t + HD], MD[:, ci, t, :], QQ[:, t, :],
                                     start=True, stop=True)
                        last.then_inc(qn_done, 1)
                    pe.wait_ge(qd_ready, 2 * c)
                    for t in range(4):
                        last = M(pst[:, 6 + ci, CH * t:CH * t + CH], QD[:, ci, t, :], KR[:, t, 1, col:col + CH],
                                 start=False, stop=True, skip_group_check=True)
                    last.then_inc(yy_done, 1)
            pe.wait_ge(yy_copied, 2 * NB)
            pe.wait_ge(sg_ready, 1)

            def post_sum(t):
                M(pst[:, 4 - 3 * (t % 2), :], headsum, KR[:, t, 0, MB:L], start=True, stop=True).then_inc(post_done, 1)

            post_sum(0)
            for t in range(4):
                if t:
                    pe.wait_ge(yf_ready, t)
                M(pst[:, 5, :], headsum, BON[:, t, MB:L], start=True, stop=True).then_inc(post_done, 1)
                M(pst[:, 6, :], g2[:, P * t:P * t + P], SG[:, MB:L], start=True, stop=True).then_inc(post_done, 1)
                pe.wait_ge(postq_ready, t + 1)
                M(pst[:, 7 - 4 * (t % 2), :], headsum, post["sq"][:], start=True, stop=True).then_inc(postv_done, 1)
                if t < 3:
                    post_sum(t + 1)
                pieces(RW_NORM_FILL[t])
            pe.wait_ge(yf_ready, 4)

            run_after_rw(pieces, jobs, dict(
                sb_meta=sb_meta, sb_z=sb_z, sb_arg=sb_arg, sb_o=sb_o, sb_end=sb_end, ret_scores=ret_scores,
                ret_out=ret_out, ret_sum=ret_sum, sw_sum=sw_sum, sw_scores=sw_scores,
                sw_turn=sw_turn, sw_out=sw_out, norm2_turn=norm2_turn))


def host_layout(inp):
    f = lambda a: np.asarray(a)
    weights = pack_weights(*(f(inp[k]) for k in ("w_in", "p_sb", "p_ret", "p_rw", "p_sw", "w_o", "w_up", "w_down")))
    lora = np.concatenate([np.concatenate([f(inp["rw_w2"])[0], f(inp["rw_a2"])[0]], 0), f(inp["rw_g2"])[0]], 1)
    cols = []
    for name, n in PARAMS:
        if name in ("qn", "kn"):
            v = f(inp[{"qn": "sw_qn_g", "kn": "sw_kn_g"}[name]])[0]
            cols.append(np.concatenate([v, v])[:, None])
        elif name == "sink":
            cols.append(np.broadcast_to(f(inp["sw_sink"])[0][None, :], (P, SWH)))
        else:
            cols.append(f(inp[name]).reshape(n, P).T)
    params = np.ascontiguousarray(np.concatenate(cols, 1))
    return {"weights": weights, "lora": np.ascontiguousarray(lora), "params": params,
            "consts": np.concatenate(list(CONSTS.values()), 1)}


def kernel(**inputs):
    import concourse.bacc as bacc
    from concourse.bass_utils import run_bass_kernel_spmd

    nc = bacc.Bacc("TRN2", target_bir_lowering=False, num_devices=1)
    arrays = {"x": np.asarray(inputs["x"]), "meta": np.asarray(inputs["meta"]), **host_layout(inputs)}
    aps = {k: nc.dram_tensor("in_" + k, a.shape, mybir.dt.from_np(a.dtype), kind="ExternalInput").ap()
           for k, a in arrays.items()}
    out = nc.dram_tensor("out_0", (1, T, D), F32, kind="ExternalOutput").ap()
    build(nc, out=out, **aps)
    r = run_bass_kernel_spmd(nc, [{"in_" + k: a for k, a in arrays.items()}], core_ids=[0])
    return r.results[0]["out_0"]
```
